# Optimizing a Trainium2 kernel written in Bass

```python
import math
import jax
import jax.numpy as jnp
from jax import lax
import numpy as np
import jax, jax.numpy as jnp

D_MODEL = 1024
BATCH = 1
SEQ = 512
DEPTH = 1

CTX_LEN = 256
GRID_W = 64
NORM_EPS = 1e-6

RW_HEAD = 64
RW_HEADS = D_MODEL // RW_HEAD
RW_DIM = RW_HEADS * RW_HEAD
RW_DECAY_LORA = 64
RW_AAA_LORA = 64
RW_GATE_LORA = 128
RW_GN_EPS = 64e-5
RW_COLS = 3 * RW_DIM + 2 * RW_DECAY_LORA + 2 * RW_AAA_LORA + RW_GATE_LORA
RW_SPLITS = (RW_DIM, 2 * RW_DIM, 3 * RW_DIM, 3 * RW_DIM + 2 * RW_DECAY_LORA, 3 * RW_DIM + 2 * RW_DECAY_LORA + 2 * RW_AAA_LORA)

SSM_DIM = 2 * D_MODEL
SSM_HEAD = 64
SSM_HEADS = SSM_DIM // SSM_HEAD
SSM_GROUPS = 4
SSM_HPG = SSM_HEADS // SSM_GROUPS
SSM_STATE = 128
SSM_CONV = 5
SSM_CHUNK = 128
SSM_BC = SSM_GROUPS * SSM_STATE
SSM_CONV_DIM = SSM_DIM + 2 * SSM_BC
SSM_COLS = SSM_DIM + SSM_CONV_DIM + 2 * SSM_HEADS

GATE_COLS = 2 * D_MODEL
N_IN = RW_COLS + SSM_COLS + GATE_COLS
IN_SPLITS = (RW_COLS, RW_COLS + SSM_COLS)

N_EXPERTS = 16
EXPERT_FF = 1024
EC_CAPACITY = 2

F32 = jnp.float32


def rms_norm(x, g):
    xf = x.astype(F32)
    y = xf * lax.rsqrt(jnp.mean(xf * xf, axis=-1, keepdims=True) + NORM_EPS)
    return (y * g.astype(F32)).astype(x.dtype)

def adaln_mod(cond, w, b):
    m = jnp.einsum('...d,de->...e', jax.nn.silu(cond), w) + b
    return jnp.split(m[..., None, :], 6, axis=-1)

def centred_shift(u, mu):
    zero = jnp.zeros_like(u[:, :1])
    prev = jnp.concatenate([zero, u[:, :-1]], axis=1)
    nxt = jnp.concatenate([u[:, 1:], zero], axis=1)
    return u + mu[0] * (prev - u) + mu[1] * (nxt - u)

def dw_conv_centred(u, w, b):
    pad = w.shape[1] // 2
    out = lax.conv_general_dilated(u, jnp.transpose(w)[:, None, :].astype(u.dtype), window_strides=(1,), padding=[(pad, pad)], dimension_numbers=('NWC', 'WIO', 'NWC'), feature_group_count=u.shape[-1])
    return out + b

def to_colmajor(t, rows):
    b, n, ch = t.shape
    return t.reshape(b, rows, GRID_W, ch).swapaxes(1, 2).reshape(b, n, ch)

def from_colmajor(t, rows):
    b, n, ch = t.shape
    return t.reshape(b, GRID_W, rows, ch).swapaxes(1, 2).reshape(b, n, ch)

def rwkv_prep(u, p):
    b_, n = u.shape[:2]
    r, k, v, xw, xa, xg = jnp.split(u, RW_SPLITS, axis=-1)
    xw = xw.reshape(b_, n, 2, RW_DECAY_LORA)
    xa = xa.reshape(b_, n, 2, RW_AAA_LORA)
    w_raw = (p['rw_w0'] + jnp.einsum('blde,def->bldf', jnp.tanh(xw), p['rw_w2'])).astype(F32)
    decay = jnp.exp(-jnp.exp(-jax.nn.softplus(-w_raw) - 0.5))
    a = jax.nn.sigmoid(p['rw_a0'] + jnp.einsum('blde,def->bldf', xa, p['rw_a2']))
    g = jnp.einsum('ble,ef->blf', jax.nn.sigmoid(xg), p['rw_g2'])
    kk = (k * p['rw_kk']).astype(F32).reshape(b_, n, RW_HEADS, RW_HEAD)
    kk = kk * lax.rsqrt(jnp.maximum(jnp.sum(kk * kk, axis=-1, keepdims=True), 1e-12))
    k_eff = k[:, :, None] * (1 + (a - 1) * p['rw_ka'])
    hd = lambda t: t.reshape(*t.shape[:-1], RW_HEADS, RW_HEAD)
    return dict(r=hd(r), w=hd(decay), k=hd(k_eff), v=hd(v), kk=kk, a=hd(a), g=g)

def rwkv_scan(q, d, s0, reverse, with_output):
    seq = (q['r'], q['w'][:, :, d], q['k'][:, :, d], q['v'], q['kk'], q['a'][:, :, d])
    seq = tuple(jnp.moveaxis(t.astype(F32), 1, 0) for t in seq)

    def step(s, inp):
        r_t, w_t, k_t, v_t, kk_t, a_t = inp
        sa = jnp.einsum('bhvk,bhk->bhv', s, -kk_t)
        s = s * w_t[:, :, None, :] + sa[..., None] * (kk_t * a_t)[:, :, None, :] + v_t[..., None] * k_t[:, :, None, :]
        return s, (jnp.einsum('bhvk,bhk->bhv', s, r_t) if with_output else None)

    s, ys = lax.scan(step, s0, seq, reverse=reverse)
    return s, (jnp.moveaxis(ys, 0, 1) if with_output else None)

def rwkv_readout(y, q, p):
    b_, n = y.shape[:2]
    mean = jnp.mean(y, axis=-1, keepdims=True)
    var = jnp.mean(jnp.square(y - mean), axis=-1, keepdims=True)
    yn = ((y - mean) * lax.rsqrt(var + RW_GN_EPS)).reshape(b_, n, RW_DIM) * p['rw_ln_w'].astype(F32) + p['rw_ln_b'].astype(F32)
    bonus = jnp.einsum('blhn,bldhn,hn->blh', q['r'].astype(F32), q['k'].astype(F32), p['rw_rk'].astype(F32))[..., None] * q['v'].astype(F32)
    return (yn + bonus.reshape(b_, n, RW_DIM)) * q['g'].astype(F32)

def rwkv_branch(uc, ul, p, ctx_out):
    qc = rwkv_prep(centred_shift(uc, p['rw_mu']), p)
    ql = rwkv_prep(centred_shift(ul, p['rw_mu']), p)
    s0 = jnp.zeros((ul.shape[0], RW_HEADS, RW_HEAD, RW_HEAD), F32)
    sc_f, yc_f = rwkv_scan(qc, 0, s0, False, ctx_out)
    sc_b, yc_b = rwkv_scan(qc, 1, s0, True, ctx_out)
    _, yl_f = rwkv_scan(ql, 0, sc_f, False, True)
    _, yl_b = rwkv_scan(ql, 1, sc_b, True, True)
    out_l = rwkv_readout(yl_f + yl_b, ql, p)
    out_c = rwkv_readout(yc_f + yc_b, qc, p) if ctx_out else None
    return out_c, out_l

def ssm_prep(u, p):
    b_, n = u.shape[:2]
    z, xbc, dt = jnp.split(u, [SSM_DIM, SSM_DIM + SSM_CONV_DIM], axis=-1)
    xbc = jax.nn.silu(dw_conv_centred(xbc, p['ssm_conv_w'], p['ssm_conv_b']))
    xs, bm, cm = jnp.split(xbc, [SSM_DIM, SSM_DIM + SSM_BC], axis=-1)
    dt = jax.nn.softplus((dt.reshape(b_, n, 2, SSM_HEADS) + p['ssm_dt_bias']).astype(F32))
    return dict(z=z, x=xs.reshape(b_, n, SSM_HEADS, SSM_HEAD), b=bm.reshape(b_, n, SSM_GROUPS, SSM_STATE), c=cm.reshape(b_, n, SSM_GROUPS, SSM_STATE), dt=dt)

def ssd_chunked(xs, dt, bm, cm, a_head, h0, with_output):
    b_, n = xs.shape[:2]
    nc = n // SSM_CHUNK

    def chunks(t):
        t = t.astype(F32).reshape(b_, nc, SSM_CHUNK, *t.shape[2:])
        return jnp.moveaxis(t, 1, 0)

    xg = chunks(xs.reshape(b_, n, SSM_GROUPS, SSM_HPG, SSM_HEAD))
    dtg = chunks(dt.reshape(b_, n, SSM_GROUPS, SSM_HPG))
    bg, cg = chunks(bm), chunks(cm)
    ag = a_head.reshape(SSM_GROUPS, SSM_HPG)
    lower = jnp.tril(jnp.ones((SSM_CHUNK, SSM_CHUNK), bool))[None, :, :, None, None]

    def step(h, inp):
        x_c, dt_c, b_c, c_c = inp
        cum = jnp.cumsum(dt_c * ag, axis=1)
        xdt = x_c * dt_c[..., None]
        h_new = h * jnp.exp(cum[:, -1])[..., None, None] + jnp.einsum('bjgn,bjge,bjgep->bgepn', b_c, jnp.exp(cum[:, -1:] - cum), xdt)
        if not with_output:
            return h_new, None
        seg = jnp.exp(jnp.where(lower, cum[:, :, None] - cum[:, None, :], -jnp.inf))
        cb = jnp.einsum('bign,bjgn->bijg', c_c, b_c)
        y_intra = jnp.einsum('bijg,bijge,bjgep->bigep', cb, seg, xdt)
        y_inter = jnp.einsum('bign,bgepn->bigep', c_c, h) * jnp.exp(cum)[..., None]
        return h_new, y_intra + y_inter

    h, ys = lax.scan(step, h0, (xg, dtg, bg, cg))
    if not with_output:
        return h, None
    return h, jnp.moveaxis(ys, 0, 1).reshape(b_, n, SSM_HEADS, SSM_HEAD)

def ssd_direction(q, d, a_log, h0, reverse, with_output):
    seq = (q['x'], q['dt'][:, :, d], q['b'], q['c'])
    if reverse:
        seq = tuple(jnp.flip(t, axis=1) for t in seq)
    h, y = ssd_chunked(*seq, -jnp.exp(a_log[d].astype(F32)), h0, with_output)
    if reverse and with_output:
        y = jnp.flip(y, axis=1)
    return h, y

def ssm_readout(y, q, p):
    b_, n = y.shape[:2]
    y = (y + p['ssm_d'].astype(F32)[:, None] * q['x'].astype(F32)).reshape(b_, n, SSM_DIM)
    return rms_norm(y * jax.nn.silu(q['z'].astype(F32)), p['ssm_norm'])

def ssm_branch(uc, ul, p, rows, ctx_out):
    qc = ssm_prep(uc, p)
    ql = ssm_prep(to_colmajor(ul, rows), p)
    h0 = jnp.zeros((ul.shape[0], SSM_GROUPS, SSM_HPG, SSM_HEAD, SSM_STATE), F32)
    hc_f, yc_f = ssd_direction(qc, 0, p['ssm_a_log'], h0, False, ctx_out)
    hc_b, yc_b = ssd_direction(qc, 1, p['ssm_a_log'], h0, True, ctx_out)
    _, yl_f = ssd_direction(ql, 0, p['ssm_a_log'], hc_f, False, True)
    _, yl_b = ssd_direction(ql, 1, p['ssm_a_log'], hc_b, True, True)
    out_l = from_colmajor(ssm_readout(yl_f + yl_b, ql, p), rows)
    out_c = ssm_readout(yc_f + yc_b, qc, p) if ctx_out else None
    return out_c, out_l

def merge(ya, yb, gates, p):
    ga, gb = jnp.split(jax.nn.sigmoid(gates.astype(F32)), 2, axis=-1)
    ya = jnp.einsum('blc,cd->bld', ya, p['proj_a'])
    yb = jnp.einsum('blc,cd->bld', yb, p['proj_b'])
    return jnp.einsum('bld,de->ble', ga * ya + gb * yb, p['w_out']).astype(gates.dtype)

def mixer(hc, hl, p, rows, ctx_out):
    pc = jnp.einsum('bld,de->ble', hc, p['w_in'])
    pl = jnp.einsum('bld,de->ble', hl, p['w_in'])
    rw_c, ss_c, gt_c = jnp.split(pc, IN_SPLITS, axis=-1)
    rw_l, ss_l, gt_l = jnp.split(pl, IN_SPLITS, axis=-1)
    ya_c, ya_l = rwkv_branch(rw_c, rw_l, p, ctx_out)
    yb_c, yb_l = ssm_branch(ss_c, ss_l, p, rows, ctx_out)
    out_l = merge(ya_l, yb_l, gt_l, p)
    out_c = merge(ya_c, yb_c, gt_c, p) if ctx_out else None
    return out_c, out_l

def ec_moe(h, router, w1, w3, w2):
    b_, n, _ = h.shape
    cap = EC_CAPACITY * n // N_EXPERTS
    aff = jax.nn.softmax(jnp.einsum('bld,de->ble', h, router).astype(F32), axis=-1)
    gate, idx = lax.top_k(jnp.swapaxes(aff, 1, 2), cap)
    bidx = jnp.arange(b_)[:, None, None]
    xe = h[bidx, idx]
    hid = jax.nn.silu(jnp.einsum('becd,edf->becf', xe, w1)) * jnp.einsum('becd,edf->becf', xe, w3)
    ye = jnp.einsum('becf,efd->becd', hid, w2) * gate[..., None].astype(h.dtype)
    return jnp.zeros_like(h).at[bidx, idx].add(ye)

def first_inputs(seed: int = 0) -> dict:
    key = jax.random.key(seed)
    ks = list(jax.random.split(key, 40))
    cnt = [0]

    def nxt():
        cnt[0] += 1
        return ks[cnt[0] - 1]

    def nrm(shape, scale):
        return scale * jax.random.normal(nxt(), shape, jnp.float32)

    def unif(shape, lo, hi):
        return jax.random.uniform(nxt(), shape, jnp.float32, lo, hi)

    L = DEPTH
    x = nrm((BATCH, SEQ, D_MODEL), 1.0)
    c = nrm((BATCH, D_MODEL), 1.0)
    ctx = nrm((BATCH, CTX_LEN, D_MODEL), 1.0)
    c_ctx = nrm((D_MODEL,), 1.0)
    ada_w = nrm((L, D_MODEL, 6 * D_MODEL), 0.5 * D_MODEL ** -0.5)
    ada_b = nrm((L, 6 * D_MODEL), 0.02)
    norm1_pre = 1.0 + nrm((L, D_MODEL), 0.02)
    norm1_post = 1.0 + nrm((L, D_MODEL), 0.02)
    norm2_pre = 1.0 + nrm((L, D_MODEL), 0.02)
    norm2_post = 1.0 + nrm((L, D_MODEL), 0.02)
    w_in = nrm((L, D_MODEL, N_IN), D_MODEL ** -0.5)
    rw_mu = unif((L, 2, RW_COLS), 0.0, 0.5)
    rw_w0 = unif((L, 2, RW_DIM), -6.0, -0.5)
    rw_w2 = nrm((L, 2, RW_DECAY_LORA, RW_DIM), 0.5 * RW_DECAY_LORA ** -0.5)
    rw_a0 = nrm((L, 2, RW_DIM), 0.1)
    rw_a2 = nrm((L, 2, RW_AAA_LORA, RW_DIM), 0.5 * RW_AAA_LORA ** -0.5)
    rw_g2 = nrm((L, RW_GATE_LORA, RW_DIM), RW_GATE_LORA ** -0.5)
    rw_kk = 0.85 + nrm((L, RW_DIM), 0.05)
    rw_ka = 1.0 + nrm((L, RW_DIM), 0.05)
    rw_rk = nrm((L, RW_HEADS, RW_HEAD), 0.1)
    rw_ln_w = 1.0 + nrm((L, RW_DIM), 0.02)
    rw_ln_b = nrm((L, RW_DIM), 0.02)
    ssm_conv_w = nrm((L, SSM_CONV_DIM, SSM_CONV), SSM_CONV ** -0.5)
    ssm_conv_b = nrm((L, SSM_CONV_DIM), 0.02)
    dt0 = jnp.exp(unif((L, 2, SSM_HEADS), math.log(1e-3), math.log(1e-1)))
    ssm_dt_bias = dt0 + jnp.log(-jnp.expm1(-dt0))
    ssm_a_log = jnp.log(unif((L, 2, SSM_HEADS), 1.0, 16.0))
    ssm_d = 1.0 + nrm((L, SSM_HEADS), 0.02)
    ssm_norm = 1.0 + nrm((L, SSM_DIM), 0.02)
    proj_a = nrm((L, RW_DIM, D_MODEL), RW_DIM ** -0.5)
    proj_b = nrm((L, SSM_DIM, D_MODEL), SSM_DIM ** -0.5)
    w_out = nrm((L, D_MODEL, D_MODEL), D_MODEL ** -0.5)
    router = nrm((L, D_MODEL, N_EXPERTS), D_MODEL ** -0.5)
    exp_w1 = nrm((L, N_EXPERTS, D_MODEL, EXPERT_FF), D_MODEL ** -0.5)
    exp_w3 = nrm((L, N_EXPERTS, D_MODEL, EXPERT_FF), D_MODEL ** -0.5)
    exp_w2 = nrm((L, N_EXPERTS, EXPERT_FF, D_MODEL), EXPERT_FF ** -0.5)
    return {'x': x, 'c': c, 'ctx': ctx, 'c_ctx': c_ctx, 'ada_w': ada_w, 'ada_b': ada_b,
            'norm1_pre': norm1_pre, 'norm1_post': norm1_post, 'norm2_pre': norm2_pre, 'norm2_post': norm2_post,
            'w_in': w_in, 'rw_mu': rw_mu, 'rw_w0': rw_w0, 'rw_w2': rw_w2, 'rw_a0': rw_a0, 'rw_a2': rw_a2,
            'rw_g2': rw_g2, 'rw_kk': rw_kk, 'rw_ka': rw_ka, 'rw_rk': rw_rk, 'rw_ln_w': rw_ln_w, 'rw_ln_b': rw_ln_b,
            'ssm_conv_w': ssm_conv_w, 'ssm_conv_b': ssm_conv_b, 'ssm_dt_bias': ssm_dt_bias, 'ssm_a_log': ssm_a_log,
            'ssm_d': ssm_d, 'ssm_norm': ssm_norm, 'proj_a': proj_a, 'proj_b': proj_b, 'w_out': w_out,
            'router': router, 'exp_w1': exp_w1, 'exp_w3': exp_w3, 'exp_w2': exp_w2}

def first_block(x, c, ctx, c_ctx, ada_w, ada_b, norm1_pre, norm1_post, norm2_pre, norm2_post,
              w_in, rw_mu, rw_w0, rw_w2, rw_a0, rw_a2, rw_g2, rw_kk, rw_ka, rw_rk, rw_ln_w, rw_ln_b,
              ssm_conv_w, ssm_conv_b, ssm_dt_bias, ssm_a_log, ssm_d, ssm_norm, proj_a, proj_b, w_out,
              router, exp_w1, exp_w3, exp_w2):
    rows = x.shape[1] // GRID_W
    for l in range(DEPTH):
        ctx_out = l < DEPTH - 1
        p = dict(w_in=w_in[l], rw_mu=rw_mu[l], rw_w0=rw_w0[l], rw_w2=rw_w2[l], rw_a0=rw_a0[l], rw_a2=rw_a2[l],
                 rw_g2=rw_g2[l], rw_kk=rw_kk[l], rw_ka=rw_ka[l], rw_rk=rw_rk[l], rw_ln_w=rw_ln_w[l], rw_ln_b=rw_ln_b[l],
                 ssm_conv_w=ssm_conv_w[l], ssm_conv_b=ssm_conv_b[l], ssm_dt_bias=ssm_dt_bias[l], ssm_a_log=ssm_a_log[l],
                 ssm_d=ssm_d[l], ssm_norm=ssm_norm[l], proj_a=proj_a[l], proj_b=proj_b[l], w_out=w_out[l])
        sh1, sc1, g1, sh2, sc2, g2 = adaln_mod(c, ada_w[l], ada_b[l])
        csh1, csc1, cg1, csh2, csc2, cg2 = adaln_mod(c_ctx, ada_w[l], ada_b[l])
        hl = rms_norm(x, norm1_pre[l]) * (1 + sc1) + sh1
        hc = rms_norm(ctx, norm1_pre[l]) * (1 + csc1) + csh1
        mc, ml = mixer(hc, hl, p, rows, ctx_out)
        x = x + g1 * rms_norm(ml, norm1_post[l])
        h2 = rms_norm(x, norm2_pre[l]) * (1 + sc2) + sh2
        x = x + g2 * rms_norm(ec_moe(h2, router[l], exp_w1[l], exp_w3[l], exp_w2[l]), norm2_post[l])
        if ctx_out:
            ctx = ctx + cg1 * rms_norm(mc, norm1_post[l])
            hc2 = rms_norm(ctx, norm2_pre[l]) * (1 + csc2) + csh2
            ctx = ctx + cg2 * rms_norm(ec_moe(hc2, router[l], exp_w1[l], exp_w3[l], exp_w2[l]), norm2_post[l])
    return x


DEPTH_2 = 2

N_MIXERS = 2
N_ATTN_LAYERS = (DEPTH_2 + 1) // 2
N_HGRN_LAYERS = DEPTH_2 // 2
EPS = 1e-6

HEAD_DIM = 64
N_HEADS = D_MODEL // HEAD_DIM
N_KV_HEADS = 4
GROUP = N_HEADS // N_KV_HEADS
WINDOW = 128
BLOCK = 128
ROPE_THETA = 10000.0
ATTN_IN_W = (N_HEADS + 2 * N_KV_HEADS) * HEAD_DIM

HG_EXPAND = 128
HG_HEADS = D_MODEL // HG_EXPAND
HG_DK = HG_EXPAND
HG_DV = D_MODEL // HG_HEADS
HG_DF = HG_HEADS * HG_DK
HG_CHUNK = 32
HG_SPLITS = [HG_DF, 2 * HG_DF, 3 * HG_DF, 3 * HG_DF + D_MODEL]
HG_IN_W = 3 * HG_DF + 2 * D_MODEL

D_FF = 2816
CONV_W = 3


def rms_norm_2(x, gain):
    xf = x.astype(jnp.float32)
    y = xf * lax.rsqrt(jnp.mean(xf * xf, axis=-1, keepdims=True) + EPS)
    return (y * gain.astype(jnp.float32)).astype(x.dtype)

def axial_angles(rows):
    row = jnp.repeat(jnp.arange(rows, dtype=jnp.float32), GRID_W)
    col = jnp.tile(jnp.arange(GRID_W, dtype=jnp.float32), rows)
    n_pairs = HEAD_DIM // 4
    inv = ROPE_THETA ** (-jnp.arange(n_pairs, dtype=jnp.float32) / n_pairs)
    return row[:, None] * inv, col[:, None] * inv

def rope_rotate(x, ang):
    x1, x2 = jnp.split(x, 2, axis=-1)
    cos = jnp.cos(ang)[None, :, None, :].astype(x.dtype)
    sin = jnp.sin(ang)[None, :, None, :].astype(x.dtype)
    return jnp.concatenate([x1 * cos - x2 * sin, x1 * sin + x2 * cos], axis=-1)

def apply_axial_rope(x, ang_r, ang_c):
    xr, xc = jnp.split(x, 2, axis=-1)
    return jnp.concatenate([rope_rotate(xr, ang_r), rope_rotate(xc, ang_c)], axis=-1)

def sink_softmax(scores, sink_g):
    s_sink = jnp.broadcast_to(sink_g[None, :, :, None, None].astype(jnp.float32), scores.shape[:-1] + (1,))
    p = jax.nn.softmax(jnp.concatenate([scores, s_sink], axis=-1), axis=-1)
    return p[..., :-1]

def attn_project(h, w_in, q_gain, k_gain):
    b, t, _ = h.shape
    q, k, v = jnp.split(h @ w_in, [N_HEADS * HEAD_DIM, (N_HEADS + N_KV_HEADS) * HEAD_DIM], axis=-1)
    q = rms_norm_2(q.reshape(b, t, N_HEADS, HEAD_DIM), q_gain)
    k = rms_norm_2(k.reshape(b, t, N_KV_HEADS, HEAD_DIM), k_gain)
    v = v.reshape(b, t, N_KV_HEADS, HEAD_DIM)
    return q, k, v

def windowed_gqa(hx, hc, w_in, w_out, q_gain, k_gain, sink, ang_r, ang_c, need_ctx_out):
    B, L, _ = hx.shape
    nb = L // BLOCK
    scale = HEAD_DIM ** -0.5
    qx, kx, vx = attn_project(hx, w_in, q_gain, k_gain)
    qc, kc, vc = attn_project(hc, w_in, q_gain, k_gain)
    qx = apply_axial_rope(qx, ang_r, ang_c)
    kx = apply_axial_rope(kx, ang_r, ang_c)
    kc_t = kc.transpose(0, 2, 1, 3)
    vc_t = vc.transpose(0, 2, 1, 3)
    pad = ((0, 0), (0, 0), (BLOCK, BLOCK), (0, 0))
    kx_p = jnp.pad(kx.transpose(0, 2, 1, 3), pad)
    vx_p = jnp.pad(vx.transpose(0, 2, 1, 3), pad)
    q_blocks = qx.reshape(B, nb, BLOCK, N_KV_HEADS, GROUP, HEAD_DIM).transpose(1, 0, 3, 4, 2, 5)
    sink_g = sink.reshape(N_KV_HEADS, GROUP)
    q_off = jnp.arange(BLOCK, dtype=jnp.int32)
    k_off = jnp.arange(3 * BLOCK, dtype=jnp.int32) - BLOCK

    def block(args):
        n, qb = args
        start = n * BLOCK
        kb = lax.dynamic_slice_in_dim(kx_p, start, 3 * BLOCK, axis=2)
        vb = lax.dynamic_slice_in_dim(vx_p, start, 3 * BLOCK, axis=2)
        qi = start + q_off
        kj = start + k_off
        valid = ((kj >= 0) & (kj < L))[None, :] & (jnp.abs(qi[:, None] - kj[None, :]) <= WINDOW)
        s_win = jnp.einsum('bkgqd,bkjd->bkgqj', qb, kb).astype(jnp.float32) * scale
        s_win = jnp.where(valid, s_win, -jnp.inf)
        s_ctx = jnp.einsum('bkgqd,bkcd->bkgqc', qb, kc_t).astype(jnp.float32) * scale
        p = sink_softmax(jnp.concatenate([s_win, s_ctx], axis=-1), sink_g).astype(vb.dtype)
        return (jnp.einsum('bkgqj,bkjd->bkgqd', p[..., :3 * BLOCK], vb)
                + jnp.einsum('bkgqc,bkcd->bkgqd', p[..., 3 * BLOCK:], vc_t))

    o = lax.map(block, (jnp.arange(nb, dtype=jnp.int32), q_blocks))
    ox = o.transpose(1, 0, 4, 2, 3, 5).reshape(B, L, N_HEADS * HEAD_DIM)
    yc = None
    if need_ctx_out:
        C = hc.shape[1]
        qcg = qc.reshape(B, C, N_KV_HEADS, GROUP, HEAD_DIM).transpose(0, 2, 3, 1, 4)
        s = jnp.einsum('bkgqd,bkcd->bkgqc', qcg, kc_t).astype(jnp.float32) * scale
        p = sink_softmax(s, sink_g).astype(vc.dtype)
        oc = jnp.einsum('bkgqc,bkcd->bkgqd', p, vc_t).transpose(0, 3, 1, 2, 4).reshape(B, C, N_HEADS * HEAD_DIM)
        yc = oc @ w_out
    return ox @ w_out, yc

def chunk_scan(q, k, g, v, s0, need_out):
    B, T, H, dk = q.shape
    dv = v.shape[-1]
    n = T // HG_CHUNK

    def to_chunks(a):
        return a.reshape(B, n, HG_CHUNK, H, a.shape[-1]).transpose(1, 0, 3, 2, 4).astype(jnp.float32)

    tri = jnp.tril(jnp.ones((HG_CHUNK, HG_CHUNK), dtype=bool))

    def step(S, inp):
        qc, kc, gc, vc = inp
        b = jnp.cumsum(gc, axis=2)
        b_last = b[:, :, -1:, :]
        k_dec = kc * jnp.exp(b_last - b)
        S_new = jnp.exp(b_last[:, :, 0, :])[..., None] * S + jnp.einsum('bhck,bhcv->bhkv', k_dec, vc)
        if not need_out:
            return S_new, None
        o_inter = jnp.einsum('bhck,bhkv->bhcv', qc * jnp.exp(b), S)
        diff = jnp.where(tri[:, :, None], b[:, :, :, None, :] - b[:, :, None, :, :], -jnp.inf)
        a = jnp.einsum('bhtk,bhsk,bhtsk->bhts', qc, kc, jnp.exp(diff))
        return S_new, o_inter + jnp.einsum('bhts,bhsv->bhtv', a, vc)

    S_fin, o = lax.scan(step, s0, (to_chunks(q), to_chunks(k), to_chunks(g), to_chunks(v)))
    if need_out:
        o = o.transpose(1, 0, 3, 2, 4).reshape(B, T, H, dv)
    return o, S_fin

def hgrn2_bidir(hx, hc, w_in, w_out, o_gain, lb, need_ctx_out):
    def project(h):
        b, t, _ = h.shape
        q, f_fw, f_bw, inp, gate = jnp.split(h @ w_in, HG_SPLITS, axis=-1)
        q = jax.nn.silu(q).reshape(b, t, HG_HEADS, HG_DK)
        inp = inp.reshape(b, t, HG_HEADS, HG_DV)

        def forget(fl):
            f = lb + (1.0 - lb) * jax.nn.sigmoid(fl.astype(jnp.float32))
            return (1.0 - f).reshape(b, t, HG_HEADS, HG_DK), jnp.log(f).reshape(b, t, HG_HEADS, HG_DK)

        return q, forget(f_fw), forget(f_bw), inp, gate

    flip = lambda a: jnp.flip(a, axis=1)
    qx, (kxf, gxf), (kxb, gxb), vx, gx = project(hx)
    qc, (kcf, gcf), (kcb, gcb), vc, gc = project(hc)
    s0 = jnp.zeros((hc.shape[0], HG_HEADS, HG_DK, HG_DV), jnp.float32)
    oc_f, sc_f = chunk_scan(qc, kcf, gcf, vc, s0, need_ctx_out)
    oc_b, sc_b = chunk_scan(flip(qc), flip(kcb), flip(gcb), flip(vc), s0, need_ctx_out)
    ox_f, _ = chunk_scan(qx, kxf, gxf, vx, sc_f, True)
    ox_b, _ = chunk_scan(flip(qx), flip(kxb), flip(gxb), flip(vx), sc_b, True)

    def readout(o, gate, h):
        o = rms_norm_2(o, o_gain).astype(h.dtype) * jax.nn.silu(gate).reshape(o.shape)
        return o.reshape(h.shape[0], h.shape[1], D_MODEL) @ w_out

    yx = readout(ox_f + flip(ox_b), gx, hx)
    yc = readout(oc_f + flip(oc_b), gc, hc) if need_ctx_out else None
    return yx, yc

def dwconv3(u, w, b):
    up = jnp.pad(u, ((0, 0), (1, 1), (0, 0)))
    return up[:, :-2] * w[0] + up[:, 1:-1] * w[1] + up[:, 2:] * w[2] + b

def conv_glu(h, w_up, conv_w, conv_b, w_down):
    gate, val = jnp.split(h @ w_up, 2, axis=-1)
    return (jax.nn.silu(dwconv3(gate, conv_w, conv_b)) * val) @ w_down

def second_inputs(seed: int = 0) -> dict:
    key = jax.random.key(seed)
    ks = jax.random.split(key, 21)
    D = D_MODEL

    def nrm(k, shape, scale):
        return jax.random.normal(k, shape, jnp.float32) * scale

    def gain(k, shape):
        return 1.0 + 0.05 * jax.random.normal(k, shape, jnp.float32)

    return {
        'x': nrm(ks[0], (BATCH, SEQ, D), 1.0),
        'c': nrm(ks[1], (BATCH, D), 1.0),
        'ctx': nrm(ks[2], (BATCH, CTX_LEN, D), 1.0),
        'c_ctx': nrm(ks[3], (D,), 1.0),
        'ada_w': nrm(ks[4], (DEPTH_2, D, 6 * D), 0.5 * D ** -0.5),
        'ada_b': nrm(ks[5], (DEPTH_2, 6 * D), 0.02),
        'norm1_g': gain(ks[6], (DEPTH_2, D)),
        'norm2_g': gain(ks[7], (DEPTH_2, D)),
        'attn_w_in': nrm(ks[8], (N_ATTN_LAYERS, D, ATTN_IN_W), D ** -0.5),
        'attn_w_out': nrm(ks[9], (N_ATTN_LAYERS, N_HEADS * HEAD_DIM, D), (N_HEADS * HEAD_DIM) ** -0.5),
        'attn_q_gain': gain(ks[10], (N_ATTN_LAYERS, HEAD_DIM)),
        'attn_k_gain': gain(ks[11], (N_ATTN_LAYERS, HEAD_DIM)),
        'attn_sink': nrm(ks[12], (N_ATTN_LAYERS, N_HEADS), 0.5),
        'hgrn_w_in': nrm(ks[13], (N_HGRN_LAYERS, D, HG_IN_W), D ** -0.5),
        'hgrn_w_out': nrm(ks[14], (N_HGRN_LAYERS, D, D), D ** -0.5),
        'hgrn_o_gain': gain(ks[15], (N_HGRN_LAYERS, HG_DV)),
        'hgrn_lb_logits': nrm(ks[16], (DEPTH_2, HG_DF), 0.5),
        'ffn_w_up': nrm(ks[17], (DEPTH_2, D, 2 * D_FF), D ** -0.5),
        'ffn_conv_w': nrm(ks[18], (DEPTH_2, CONV_W, D_FF), CONV_W ** -0.5),
        'ffn_conv_b': nrm(ks[19], (DEPTH_2, D_FF), 0.02),
        'ffn_w_down': nrm(ks[20], (DEPTH_2, D_FF, D), D_FF ** -0.5),
    }

def second_block(x, c, ctx, c_ctx, ada_w, ada_b, norm1_g, norm2_g, attn_w_in, attn_w_out, attn_q_gain,
              attn_k_gain, attn_sink, hgrn_w_in, hgrn_w_out, hgrn_o_gain, hgrn_lb_logits, ffn_w_up,
              ffn_conv_w, ffn_conv_b, ffn_w_down):
    L = x.shape[1]
    rows = L // GRID_W
    ang_r, ang_c = axial_angles(rows)
    lb_prob = jax.nn.softmax(hgrn_lb_logits.astype(jnp.float32), axis=0)
    lb_sched = jnp.cumsum(lb_prob, axis=0) - lb_prob[0]
    for layer in range(DEPTH_2):
        last = layer == DEPTH_2 - 1
        j = layer // N_MIXERS
        mod = jax.nn.silu(c) @ ada_w[layer] + ada_b[layer]
        mod_c = jax.nn.silu(c_ctx) @ ada_w[layer] + ada_b[layer]
        sh1, sc1, g1, sh2, sc2, g2 = jnp.split(mod[:, None, :], 6, axis=-1)
        csh1, csc1, cg1, csh2, csc2, cg2 = jnp.split(mod_c, 6)
        hx = rms_norm_2(x, norm1_g[layer]) * (1.0 + sc1) + sh1
        hc = rms_norm_2(ctx, norm1_g[layer]) * (1.0 + csc1) + csh1
        if layer % N_MIXERS == 0:
            yx, yc = windowed_gqa(hx, hc, attn_w_in[j], attn_w_out[j], attn_q_gain[j], attn_k_gain[j],
                                  attn_sink[j], ang_r, ang_c, not last)
        else:
            yx, yc = hgrn2_bidir(hx, hc, hgrn_w_in[j], hgrn_w_out[j], hgrn_o_gain[j], lb_sched[layer], not last)
        x = x + g1 * yx
        hx2 = rms_norm_2(x, norm2_g[layer]) * (1.0 + sc2) + sh2
        x = x + g2 * conv_glu(hx2, ffn_w_up[layer], ffn_conv_w[layer], ffn_conv_b[layer], ffn_w_down[layer])
        if not last:
            ctx = ctx + cg1 * yc
            hc2 = rms_norm_2(ctx, norm2_g[layer]) * (1.0 + csc2) + csh2
            ctx = ctx + cg2 * conv_glu(hc2, ffn_w_up[layer], ffn_conv_w[layer], ffn_conv_b[layer], ffn_w_down[layer])
    return x


def setup_inputs(seed=0):
    out = dict(first_inputs(seed))
    for name, value in second_inputs(seed + 1).items():
        if name != "x":
            out[name + "_2"] = value
    return out


def reference(
    x, c, ctx, c_ctx, ada_w, ada_b, norm1_pre, norm1_post, norm2_pre, norm2_post, w_in, rw_mu,
    rw_w0, rw_w2, rw_a0, rw_a2, rw_g2, rw_kk, rw_ka, rw_rk, rw_ln_w, rw_ln_b, ssm_conv_w,
    ssm_conv_b, ssm_dt_bias, ssm_a_log, ssm_d, ssm_norm, proj_a, proj_b, w_out, router, exp_w1,
    exp_w3, exp_w2, c_2, ctx_2, c_ctx_2, ada_w_2, ada_b_2, norm1_g_2, norm2_g_2, attn_w_in_2,
    attn_w_out_2, attn_q_gain_2, attn_k_gain_2, attn_sink_2, hgrn_w_in_2, hgrn_w_out_2,
    hgrn_o_gain_2, hgrn_lb_logits_2, ffn_w_up_2, ffn_conv_w_2, ffn_conv_b_2, ffn_w_down_2,
):
    x = first_block(
        x, c, ctx, c_ctx, ada_w, ada_b, norm1_pre, norm1_post, norm2_pre, norm2_post, w_in,
        rw_mu, rw_w0, rw_w2, rw_a0, rw_a2, rw_g2, rw_kk, rw_ka, rw_rk, rw_ln_w, rw_ln_b,
        ssm_conv_w, ssm_conv_b, ssm_dt_bias, ssm_a_log, ssm_d, ssm_norm, proj_a, proj_b, w_out,
        router, exp_w1, exp_w3, exp_w2,
    )
    return second_block(
        x, c_2, ctx_2, c_ctx_2, ada_w_2, ada_b_2, norm1_g_2, norm2_g_2, attn_w_in_2,
        attn_w_out_2, attn_q_gain_2, attn_k_gain_2, attn_sink_2, hgrn_w_in_2, hgrn_w_out_2,
        hgrn_o_gain_2, hgrn_lb_logits_2, ffn_w_up_2, ffn_conv_w_2, ffn_conv_b_2, ffn_w_down_2,
    )


_drawn_inputs = setup_inputs


def setup_inputs(seed=0):
    import zlib

    import numpy as np

    out = dict(_drawn_inputs(seed))
    spreads = {}
    factors = {'norm2_post': 8.0,
     'rw_w2': 3.039,
     'rw_a0': 3.124,
     'rw_ln_w': 6.165,
     'rw_ln_b': 5.531,
     'ssm_conv_b': 2.825,
     'ssm_d': 4.442,
     'ssm_norm': 4.393,
     'ctx_2': 3.279,
     'norm1_g_2': 4.995,
     'norm2_g_2': 2.816,
     'attn_q_gain_2': 8.0,
     'attn_k_gain_2': 8.0,
     'attn_sink_2': 8.0,
     'hgrn_o_gain_2': 8.0,
     'hgrn_lb_logits_2': 6.599,
     'ffn_conv_b_2': 8.0}
    for name, (base, spread) in spreads.items():
        noise = np.random.default_rng([zlib.crc32(name.encode()), seed]).standard_normal(out[name].shape)
        drawn = base * np.exp(spread * noise) if base else spread * noise
        out[name] = jnp.asarray(drawn.astype(out[name].dtype))
    for name, factor in factors.items():
        out[name] = (out[name] * factor).astype(out[name].dtype)
    return out
```

```python
from contextlib import ExitStack

import numpy as np
import concourse.bass as bass
from concourse import mybir

F32 = mybir.dt.float32
ALU = mybir.AluOpType
ACT = mybir.ActivationFunctionType
AX = mybir.AxisListType.X

P = 128
BANK = 512


class Stage(ExitStack):

    def __init__(self, nc):
        super().__init__()
        self.nc, self.sems = nc, []

    def sem(self, name):
        self.sems.append(self.nc.alloc_semaphore(name))
        return self.sems[-1]

    def close_stage(self):
        self.nc.clear_and_free_semaphores(self.sems)
        self.nc.all_engine_barrier()

    def __exit__(self, *exc):
        done = super().__exit__(*exc)
        if exc[0] is None:
            self.close_stage()
        return done


def dense(nc, name, w, x_v, out_v, k_tiles, tokens, groups, width):
    span = tokens if tokens <= BANK else tokens // 2
    spans = tokens // span
    cols = width // P
    half = cols // 2
    with Stage(nc) as ctx:
        sb = lambda n, shape: ctx.enter_context(nc.sbuf_tensor(f"{name}_{n}", shape, F32))
        sem = lambda n: ctx.sem(f"{name}_{n}")
        x = sb("x", [P, k_tiles, tokens])
        w_slot = [sb(f"w{s}", [P, k_tiles, width]) for s in range(2)]
        stage = [sb(f"stage{s}", [P, cols, tokens]) for s in range(2)]
        acc = [ctx.enter_context(nc.psum_tensor(f"{name}_acc{b}", [P, spans, BANK], F32)) for b in range(2)]
        x_loaded = sem("x_loaded")
        w_loaded = [sem(f"w_loaded{s}") for s in range(2)]
        acc_ready = sem("acc_ready")
        evacuated = [sem(f"evacuated{b}") for b in range(2)]
        stored = [sem(f"stored{s}") for s in range(2)]
        stage_free = [sem(f"stage_free{s}") for s in range(2)]
        pairs, odd = groups // 2, groups % 2

        def each(eng, step, first=0):
            if pairs > first:
                with eng.Fori(first, pairs) as i:
                    step(i * 2, 0, i)
                    step(i * 2 + 1, 1, i)
            if odd:
                step(groups - 1, 0, pairs)

        with nc.Block() as block:
            @block.sync
            def _(sp):
                def load(g, s):
                    sp.dma_start(w_slot[s][:], w[bass.ds(g, 1)].rearrange("a p k n -> (a p) k n")).then_inc(w_loaded[s], 16)

                def reload(g, s, i):
                    sp.wait_ge(acc_ready, (g - 1) * cols)
                    load(g, s)

                sp.dma_start(x[:], x_v[:, :, 0:tokens]).then_inc(x_loaded, 16)
                load(0, 0)
                load(1, 1)
                each(sp, reload, 1)

            @block.tensor
            def _(pe):
                pe.wait_ge(x_loaded, 16)

                def products(g, s, i):
                    pe.wait_ge(w_loaded[s], i * 16 + 16)
                    for c in range(cols):
                        b = c % 2
                        pe.wait_ge(evacuated[b], g * half + (c // 2 + 1))
                        for k in range(k_tiles):
                            for h in range(spans):
                                last = pe.matmul(acc[b][:, h, 0:span], w_slot[s][:, k, c * P:(c + 1) * P],
                                                 x[:, k, h * span:(h + 1) * span], start=(k == 0), stop=(k == k_tiles - 1))
                        last.then_inc(acc_ready, 1)
                each(pe, products)

            def copies(eng, copy, b):
                def copy_out(g, s, i):
                    eng.wait_ge(stage_free[s], i + 1)
                    for c in range(b, cols, 2):
                        eng.wait_ge(acc_ready, g * cols + (c + 1))
                        copy(stage[s][:, c, :].rearrange("p (h n) -> p h n", h=spans), acc[b][:, :, 0:span]).then_inc(evacuated[b], 1)
                eng.sem_inc(evacuated[b], 1)
                each(eng, copy_out)

            @block.scalar
            def _(act):
                copies(act, act.copy, 0)

            @block.vector
            def _(dve):
                copies(dve, dve.tensor_copy, 1)

            @block.gpsimd
            def _(pool):
                def store(g, s, i):
                    for b in range(2):
                        pool.wait_ge(evacuated[b], g * half + (half + 1))
                    pool.dma_start(out_v[bass.ds(g, 1), :, :, 0:tokens].rearrange("a p c t -> (a p) c t"), stage[s][:]).then_inc(stored[s], 16)
                    pool.wait_ge(stored[s], i * 16 + 16)
                    pool.sem_inc(stage_free[s], 1)
                for s in range(2):
                    pool.sem_inc(stage_free[s], 1)
                each(pool, store)



D = 1024
LAT, CTX = 512, 256
TOK = LAT + CTX
CH = 128
SHIFTED = LAT + 1 + CTX
PADDED = SHIFTED + 2
C_DECAY = float(np.exp(-0.5))
K_T, V_T, XW_T, XA_T, XBC_T, DT_T, R_T, XG_T, Z_T, GATE_T = 0, 8, 16, 17, 18, 42, 43, 51, 52, 68


def rwkv(nc, pt, loras, params, edges, consts, ya):
    w2, a2, g2 = loras
    with Stage(nc) as ctx:
        def sb(n, shape):
            return ctx.enter_context(nc.sbuf_tensor(f"rw_{n}", shape, F32))

        def sem(n):
            return ctx.sem(f"rw_{n}")

        raw = sb("raw", [P, 3, PADDED])
        small = sb("small", [P, 3, SHIFTED])
        lora_w = sb("lora_w", [P, 3, P])
        par = sb("par", [P, 16])
        edge = sb("edge", [P, 8])
        col = sb("col", [P, 8])
        ident = sb("ident", [P, CH])
        mask_g = sb("mask_g", [P, 2, 512])
        mask_l = sb("mask_l", [P, 4, CH])
        level_t = sb("level_t", [P, 7, 2, CH])
        blockones = sb("blockones", [P, CH])
        keep = sb("keep", [P, 6, CH + 1])
        tiny = sb("tiny", [P, 3])
        rkv = sb("rkv", [P, 3, SHIFTED])
        kk = sb("kk", [P, SHIFTED])
        sq = sb("sq", [P, SHIFTED])
        bkt = sb("bkt", [P, 6, 4, CH])
        sig = sb("sig", [P, 2, 6, CH + 1])
        aa = sb("aa", [P, 2, SHIFTED])
        run = sb("run", [P, 2, 6, CH + 1])
        up = sb("up", [P, 2, 6, CH + 1])
        down = sb("down", [P, 2, 6, CH + 1])
        keff = sb("keff", [P, 2, SHIFTED])
        rstd = sb("rstd", [P, SHIFTED])
        ar = sb("ar", [P, 2, 6, 2, CH])
        bm = sb("bm", [P, 2, 6, CH])
        km = sb("km", [P, 2, 6, CH])
        mg = sb("mg", [P, 6, 4, 512])
        xs = sb("xs", [P, 6, 4, CH])
        xt = sb("xt", [P, 6, 4, CH])
        flat_of = lambda t, pat, n: t[:].rearrange(pat)[:, 0:n].rearrange("p (a j n) -> p a j n", j=4, n=CH)
        lo = flat_of(aa, "p d n -> p (d n)", 2 * 4 * CH)
        t1 = flat_of(run, "p d c n -> p (d c n)", 2 * 4 * CH)
        ltm = flat_of(up, "p d c n -> p (d c n)", 2 * 4 * CH)
        ys = down[:].rearrange("p d c n -> p (d c n)")[:, 0:2 * LAT].rearrange("p (d n) -> p d n", d=2)
        vt = sb("vt", [P, 6, CH])
        fac = sb("fac", [P, 2, 6])
        st = sb("st", [P, 2, 2, 64])
        sf = sb("sf", [P, 2, 64])
        rhs = sb("rhs", [P, 2, 2, 64])
        sas = sb("sas", [P, 4, 64])
        gs = sb("gs", [P, LAT])
        outp = keff[:, 1, 0:LAT]
        big = ctx.enter_context(nc.psum_tensor("rw_big", [P, 8, 512], F32))
        flat = big[:].rearrange("p b n -> p (b n)")
        g_bank, t_bank, x_bank, xt_bank = (0, 1), (2, 3), (4, 5), (6, 7)

        const_in, edge_in = sem("const_in"), sem("edge_in")
        tile_in = sem("tile_in")
        raw_used, cols_ready, sq_ready = sem("raw_used"), sem("cols_ready"), sem("sq_ready")
        lora_ready, exps_done, norm_ready, rstd_done = sem("lora_ready"), sem("exps_done"), sem("norm_ready"), sem("rstd_done")
        run_ready, decays_done, ops_ready = sem("run_ready"), sem("decays_done"), sem("ops_ready")
        g_ready, g_masked, l_ready, l_masked, x0_done = sem("g_ready"), sem("g_masked"), sem("l_ready"), sem("l_masked"), sem("x0_done")
        tr_ready, tr_copied = sem("tr_ready"), sem("tr_copied")
        ltm_ready, t1_ready, t1_copied, xx_ready, x_updated = sem("ltm_ready"), sem("t1_ready"), sem("t1_copied"), sem("xx_ready"), sem("x_updated")
        p1_ready, rhs_done, sa_ready, sa_done = sem("p1_ready"), sem("rhs_done"), sem("sa_ready"), sem("sa_done")
        delta_ready, y_ready, state_done, y_copied = sem("delta_ready"), sem("y_ready"), sem("state_done"), sem("y_copied")
        red_in, red_ready, red_done, tile_done, stored, out_free = sem("red_in"), sem("red_ready"), sem("red_done"), sem("tile_done"), sem("stored"), sem("out_free")
        edge_sq, edge_exp = sem("edge_sq"), sem("edge_exp")

        def lat(ap):
            return ap[:, 0:LAT].rearrange("p (c n) -> p c n", n=CH)

        def con(ap):
            return ap[:, LAT + 1:SHIFTED].rearrange("p (c n) -> p c n", n=CH)

        ORDER = ([4, 5, 0, 1, 2, 3], [5, 4, 3, 2, 1, 0])
        LEVELS = 6
        shifted_halves = ((0, LAT), (LAT, SHIFTED))

        with nc.Block() as block:
            @block.sync
            def _(sp):
                for dst, src in ((ident, "ident"), (mask_g, "mask_g"), (mask_l, "mask_l"), (level_t, "level_t"),
                                 (blockones, "blockones"), (keep, "keep"), (edge, None)):
                    sp.dma_start(dst[:], consts[src] if src else edges).then_inc(const_in, 16)

                def streams(dst, row):
                    for a, b, t0 in ((1, LAT + 1, 0), (LAT + 2, PADDED - 1, LAT)):
                        yield dst[:, a:b], pt[row, :, t0:t0 + b - a] if not isinstance(row, bass.DynSlice) else pt[row, :, t0:t0 + b - a].rearrange("a p t -> (a p) t")

                sp.sem_inc(out_free, 1)
                sp.wait_ge(cols_ready, 1)
                for n, row in enumerate((XW_T, XA_T, XG_T)):
                    for dst, src in list(streams(raw[:, n, :], row))[:2 - n // 2]:
                        sp.dma_start(dst, src).then_inc(edge_in, 16)
                with sp.Fori(0, 8) as i:
                    sp.wait_ge(raw_used, i + 1)
                    for n, row in enumerate((R_T, K_T, V_T)):
                        for dst, src in list(streams(raw[:, n, :], bass.ds(i + row, 1)))[:1 + (n > 0)]:
                            sp.dma_start(dst, src).then_inc(tile_in, 16)
                    sp.wait_ge(tile_done, i + 1)
                    for n, w in enumerate((w2, a2, g2)):
                        sp.dma_start(lora_w[:, n, :], w[:, bass.ds(i * P, P)]).then_inc(tile_in, 16)
                    sp.dma_start(par[:], params[bass.ds(i, 1)].rearrange("a p n -> (a p) n")).then_inc(tile_in, 16)

            @block.vector
            def _(dve):
                def shift(out, u, c, m0, m1):
                    dve.tensor_scalar(out, u[:, 1:PADDED - 1], c, None, ALU.mult)
                    dve.drain()
                    dve.scalar_tensor_tensor(out, u[:, 0:PADDED - 2], m0, out, ALU.mult, ALU.add)
                    dve.drain()
                    dve.scalar_tensor_tensor(out, u[:, 2:PADDED], m1, out, ALU.mult, ALU.add)
                    dve.drain()

                dve.sem_inc(tile_done, 1)
                dve.memset(raw[:], 0.0)
                dve.memset(sig[:], 0.0)
                dve.memset(rkv[:], 0.0)
                dve.memset(tiny[:, 0:1], -1e-12)
                dve.memset(tiny[:, 2:3], 1e-12)
                dve.memset(tiny[:, 1:2], 64e-5)
                dve.drain().then_inc(cols_ready, 1)
                dve.wait_ge(const_in, 16 * 7)
                dve.wait_ge(edge_in, 16 * 5)
                e = edge
                for n in range(3):
                    dve.tensor_tensor(col[:, n:n + 1], e[:, 2 * n:2 * n + 1], e[:, 2 * n + 1:2 * n + 2], ALU.add)
                dve.drain()
                dve.tensor_scalar(col[:, 0:3], col[:, 0:3], -1.0, 1.0, ALU.mult, ALU.add)
                dve.drain()
                for n in range(3):
                    shift(small[:, n, :], raw[:, n, :], col[:, n:n + 1], e[:, 2 * n:2 * n + 1], e[:, 2 * n + 1:2 * n + 2])
                dve.drain().then_inc(edge_sq, 1)
                dve.wait_ge(edge_exp, 1)
                dve.drain().then_inc(raw_used, 1)

                with dve.Fori(0, 8) as i:
                    dve.wait_ge(tile_in, i * 144 + 144)
                    mu = par[:, 0:6].rearrange("p (n m) -> p n m", m=2)
                    dve.tensor_tensor(col[:, 0:3], mu[:, :, 0], mu[:, :, 1], ALU.add)
                    dve.tensor_scalar(col[:, 7:8], par[:, 11:12], -1.0, 1.0, ALU.mult, ALU.add)
                    dve.drain()
                    dve.tensor_scalar(col[:, 0:3], col[:, 0:3], -1.0, 1.0, ALU.mult, ALU.add)
                    dve.drain().then_inc(cols_ready, 1)
                    for n in range(3):
                        shift(rkv[:, n, :], raw[:, n, :], col[:, n:n + 1], par[:, 2 * n:2 * n + 1], par[:, 2 * n + 1:2 * n + 2])
                    dve.drain().then_inc(raw_used, 1)
                    dve.tensor_scalar(kk[:], rkv[:, 1, :], par[:, 10:11], None, ALU.mult)
                    dve.drain()
                    dve.tensor_tensor(sq[:], kk[:], kk[:], ALU.mult)
                    dve.drain().then_inc(sq_ready, 1)
                    dve.wait_ge(exps_done, i + 1)
                    dve.wait_ge(out_free, i + 1)
                    for d in range(2):
                        dve.tensor_tensor_scan(run[:, d].rearrange("p c n -> p (c n)"), keep[:].rearrange("p c n -> p (c n)"),
                                               sig[:, d].rearrange("p c n -> p (c n)"), 0.0, ALU.mult, ALU.add)
                        dve.tensor_scalar(keff[:, d, :], aa[:, d, :], par[:, 11:12], col[:, 7:8], ALU.mult, ALU.add)
                    dve.drain()
                    for d in range(2):
                        dve.tensor_tensor(sig[:, d], run[:, d], run[:, d, :, 64:65].to_broadcast([P, 6, CH + 1]), ALU.subtract)
                        dve.tensor_tensor(keff[:, d, :], keff[:, d, :], rkv[:, 1, :], ALU.mult)
                    dve.drain().then_inc(run_ready, 1)
                    dve.wait_ge(rstd_done, i + 1)
                    dve.tensor_tensor(kk[:], kk[:], rstd[:], ALU.mult)
                    dve.drain()
                    dve.wait_ge(decays_done, i + 1)
                    dve.memset(sig[:], 0.0)
                    for d in range(2):
                        r_e = (up[:, 0, :, 1:], down[:, 1, :, 0:CH])[d]
                        a_e = (up[:, 0, :, 0:CH], down[:, 1, :, 1:])[d]
                        k_e = (down[:, 0, :, 1:], up[:, 1, :, 0:CH])[d]
                        for part, c0, c1 in ((lat, 0, 4), (con, 4, 6)):
                            dve.tensor_tensor(ar[:, d, c0:c1, 0, :], part(kk[:]), a_e[:, c0:c1], ALU.mult)
                            dve.tensor_tensor(ar[:, d, c0:c1, 1, :], part(rkv[:, 0, :]), r_e[:, c0:c1], ALU.mult)
                            dve.tensor_tensor(km[:, d, c0:c1, :], part(keff[:, d, :]), k_e[:, c0:c1], ALU.mult)
                            dve.tensor_tensor(bm[:, d, c0:c1, :], part(kk[:]), part(aa[:, d, :]), ALU.mult)
                    dve.drain()
                    for d in range(2):
                        k_e = (down[:, 0, :, 1:], up[:, 1, :, 0:CH])[d]
                        dve.tensor_tensor(bm[:, d], bm[:, d], k_e, ALU.mult)
                        for n in range(5):
                            c, c2 = ORDER[d][n], ORDER[d][n + 1]
                            if d == 0:
                                dve.tensor_tensor(fac[:, d, n:n + 1], up[:, 0, c, CH:], down[:, 0, c2, 0:1], ALU.mult)
                            else:
                                dve.tensor_tensor(fac[:, d, n:n + 1], down[:, 1, c, 0:1], up[:, 1, c2, CH:], ALU.mult)
                    dve.tensor_tensor(keff[:, 0, :], keff[:, 0, :], keff[:, 1, :], ALU.add)
                    dve.memset(st[:, 0], 0.0)
                    dve.drain().then_inc(ops_ready, 1)
                    for c in range(6):
                        for j in range(4):
                            n = c * 4 + j
                            dve.wait_ge(g_ready, i * 24 + (n + 1))
                            if c < 4:
                                dve.tensor_tensor(mg[:, c, j, :], big[:, g_bank[n % 2], :], mask_g[:, j // 2, :], ALU.mult).then_inc(g_masked, 1)
                            else:
                                v = lambda ap: ap.rearrange("p (a b n) -> p a b n", a=2, b=2)[:, :, 0, :]
                                dve.tensor_tensor(v(mg[:, c, j, :]), v(big[:, g_bank[n % 2], :]), v(mask_g[:, j // 2, :]), ALU.mult).then_inc(g_masked, 1)
                        dve.wait_ge(l_ready, i * 6 + (c + 1))
                        if c >= 2:
                            dve.wait_ge(x0_done, i * 6 + (c - 1))
                        heads_first = lambda ap: ap.rearrange("p (d h) n -> p h d n", d=2)
                        dve.tensor_tensor(heads_first(lo[:, c % 2]), big[:, t_bank[0]:t_bank[1] + 1, 0:256].rearrange("p h (d n) -> p h d n", d=2),
                                          heads_first(mask_l[:]), ALU.mult).then_inc(l_masked, 1)
                    for pair in range(3):
                        for lv in range(1, LEVELS + 1):
                            for q in range(2):
                                c = 2 * pair + q
                                n = (pair * LEVELS + lv - 1) * 2 + q
                                dve.wait_ge(xx_ready, i * 36 + (n + 1))
                                if lv < LEVELS:
                                    dve.tensor_tensor(xs[:, c], xs[:, c], big[:, x_bank[q], :].rearrange("p (j n) -> p j n", j=4), ALU.subtract)
                                dve.tensor_tensor(xt[:, c], xt[:, c], big[:, xt_bank[q], :].rearrange("p (j n) -> p j n", j=4), ALU.subtract)
                                dve.drain().then_inc(x_updated, 1)
                    for n in range(6):
                        if n < 5:
                            for d in range(2):
                                dve.tensor_scalar(sf[:, d, :], st[:, n % 2, d, :], fac[:, d, n:n + 1], None, ALU.mult)
                            dve.drain()
                            dve.wait_ge(delta_ready, i * 5 + (n + 1))
                            for d in range(2):
                                dve.scalar_tensor_tensor(st[:, (n + 1) % 2, d, :], big[:, xt_bank[0], d * 64:d * 64 + 64], fac[:, d, n:n + 1],
                                                         sf[:, d, :], ALU.mult, ALU.add)
                            dve.drain().then_inc(state_done, 1)
                        if n >= 2:
                            dve.wait_ge(y_ready, i * 4 + (n - 1))
                            for d in range(2):
                                c = ORDER[d][n]
                                for h in range(2):
                                    rows = slice(64 * h, 64 * h + 64)
                                    dve.tensor_copy(ys[rows, d, c * CH:(c + 1) * CH], big[rows, (g_bank, t_bank)[h][d], 0:CH])
                            dve.drain().then_inc(y_copied, 1)
                    dve.tensor_tensor(ys[:, 0, :], ys[:, 0, :], ys[:, 1, :], ALU.add)
                    dve.tensor_tensor(sq[:, 0:LAT], rkv[:, 0, 0:LAT], keff[:, 0, 0:LAT], ALU.mult)
                    dve.drain()
                    dve.tensor_scalar(sq[:, 0:LAT], sq[:, 0:LAT], par[:, 12:13], None, ALU.mult)
                    dve.drain().then_inc(red_in, 1)
                    dve.wait_ge(red_ready, i * 3 + 1)
                    dve.scalar_tensor_tensor(ys[:, 0, :], big[:, 0, :], -1.0 / 64, ys[:, 0, :], ALU.mult, ALU.add)
                    dve.drain()
                    dve.tensor_tensor(ys[:, 1, :], ys[:, 0, :], ys[:, 0, :], ALU.mult)
                    dve.drain().then_inc(red_in, 1)
                    dve.wait_ge(red_ready, i * 3 + 2)
                    dve.tensor_tensor(sq[:, 0:LAT], big[:, 1, :], rkv[:, 2, 0:LAT], ALU.mult)
                    dve.wait_ge(red_done, i + 1)
                    dve.tensor_tensor(ys[:, 0, :], ys[:, 0, :], rstd[:, 0:LAT], ALU.mult)
                    dve.drain()
                    dve.tensor_scalar(ys[:, 0, :], ys[:, 0, :], par[:, 13:14], par[:, 14:15], ALU.mult, ALU.add)
                    dve.drain()
                    dve.tensor_tensor(ys[:, 0, :], ys[:, 0, :], sq[:, 0:LAT], ALU.add)
                    dve.drain()
                    dve.tensor_tensor(outp, ys[:, 0, :], gs[:], ALU.mult)
                    dve.drain().then_inc(tile_done, 1)

            @block.scalar
            def _(act):
                act.wait_ge(edge_sq, 1)
                act.activation(small[:, 0, :], small[:, 0, :], ACT.Tanh)
                act.activation(small[:, 2, :], small[:, 2, :], ACT.Sigmoid)
                act.drain().then_inc(edge_exp, 1)
                with act.Fori(0, 8) as i:
                    act.wait_ge(cols_ready, i + 2)
                    act.wait_ge(lora_ready, i + 1)
                    for d in range(2):
                        w_psum = flat[:, 2048 * d:2048 * d + SHIFTED]
                        act.activation(sig[:, d, 0:4, 1:], lat(w_psum), ACT.Sigmoid, bias=par[:, 6 + d:7 + d])
                        act.activation(sig[:, d, 4:6, 1:], con(w_psum), ACT.Sigmoid, bias=par[:, 6 + d:7 + d])
                        act.activation(aa[:, d, :], flat[:, 2048 * d + 1024:2048 * d + 1024 + SHIFTED], ACT.Sigmoid, bias=par[:, 8 + d:9 + d])
                    act.drain().then_inc(exps_done, 1)
                    act.wait_ge(norm_ready, i + 1)
                    act.copy(gs[:], big[:, 2, :])
                    act.activation(rstd[:], flat[:, 0:SHIFTED], ACT.Relu, bias=tiny[:, 0:1])
                    act.drain()
                    act.activation(rstd[:], rstd[:], ACT.Ln, bias=tiny[:, 2:3])
                    act.drain()
                    act.activation(rstd[:], rstd[:], ACT.Exp, scale=-0.5)
                    act.drain().then_inc(rstd_done, 1)
                    act.wait_ge(run_ready, i + 1)
                    act.activation(up[:], sig[:], ACT.Exp, scale=-C_DECAY)
                    act.activation(down[:], sig[:], ACT.Exp, scale=C_DECAY)
                    act.drain().then_inc(decays_done, 1)
                    for n in range(8):
                        act.wait_ge(tr_ready, i * 8 + (n + 1))
                        if n < 6:
                            act.copy(bkt[:, n].rearrange("p j n -> p (j n)"), big[:, x_bank[n % 2], :]).then_inc(tr_copied, 1)
                        elif n == 6:
                            act.copy(vt[:, 0:4].rearrange("p j n -> p (j n)"), big[:, x_bank[0], :]).then_inc(tr_copied, 1)
                        else:
                            act.copy(vt[:, 4:6].rearrange("p j n -> p (j n)"), big[:, x_bank[1], 0:256]).then_inc(tr_copied, 1)
                    for pair in range(3):
                        for lv in range(1, LEVELS + 1):
                            for q in range(2):
                                n = (pair * LEVELS + lv - 1) * 2 + q
                                act.wait_ge(t1_ready, i * 36 + (n + 1))
                                act.copy(t1[:, q].rearrange("p j n -> p (j n)"), big[:, t_bank[q], :]).then_inc(t1_copied, 1)
                    for n in range(6):
                        act.wait_ge(p1_ready, i * 6 + (n + 1))
                        act.mul(rhs[:].rearrange("p h d n -> p h (d n)"), big[:, x_bank[0]:x_bank[1] + 1, 0:128], -1.0).then_inc(rhs_done, 1)
                        act.wait_ge(sa_ready, i * 6 + (n + 1))
                        act.copy(sas[:].rearrange("p j n -> p (j n)"), big[:, xt_bank[1], 0:256]).then_inc(sa_done, 1)
                    act.wait_ge(red_ready, i * 3 + 3)
                    act.activation(rstd[:, 0:LAT], big[:, 2, :], ACT.Ln, scale=1.0 / 64, bias=tiny[:, 1:2])
                    act.drain()
                    act.activation(rstd[:, 0:LAT], rstd[:, 0:LAT], ACT.Exp, scale=-0.5)
                    act.drain().then_inc(red_done, 1)

            def pairs_of(ap):
                return ap.rearrange("p (d h) n -> p d h n", d=2)

            def level(lv):
                return level_t[:, lv].unsqueeze(2).to_broadcast([P, 2, 2, CH])

            @block.gpsimd
            def _(pool):
                with pool.Fori(0, 8) as i:
                    for c in range(6):
                        pool.wait_ge(l_masked, i * 6 + (c + 1))
                        pool.wait_ge(g_masked, i * 24 + (4 * c + 4))
                        for d in range(2):
                            pool.tensor_tensor(xs[:, c, 2 * d:2 * d + 2], lo[:, c % 2, 2 * d:2 * d + 2],
                                               level_t[:, 0, 1 - d].unsqueeze(1).to_broadcast([P, 2, CH]), ALU.mult)
                        pool.tensor_tensor(pairs_of(xt[:, c]), pairs_of(mg[:, c, :, 0:CH]), level(0), ALU.mult)
                        pool.drain()
                        pool.tensor_tensor(xs[:, c], ident[:].unsqueeze(1).to_broadcast([P, 4, CH]), xs[:, c], ALU.subtract)
                        pool.tensor_tensor(xt[:, c], ident[:].unsqueeze(1).to_broadcast([P, 4, CH]), xt[:, c], ALU.subtract)
                        pool.drain().then_inc(x0_done, 1)
                    for pair in range(3):
                        for lv in range(1, LEVELS + 1):
                            for q in range(2):
                                n = (pair * LEVELS + lv - 1) * 2 + q
                                if n >= 2:
                                    pool.wait_ge(t1_ready, i * 36 + (n - 1))
                                pool.tensor_tensor(pairs_of(ltm[:, q]), pairs_of(mg[:, 2 * pair + q, :, 0:CH]), level(lv), ALU.mult).then_inc(ltm_ready, 1)
                    pool.wait_ge(tile_done, i + 2)
                    pool.dma_start(ya[bass.ds(i, 1)].rearrange("a p t -> (a p) t"), outp).then_inc(stored, 16)
                    pool.wait_ge(stored, i * 16 + 16)
                    pool.sem_inc(out_free, 1)

            @block.tensor
            def _(pe):
                pe.wait_ge(const_in, 16 * 7)
                with pe.Fori(0, 8) as i:
                    pe.wait_ge(raw_used, i + 1)
                    pe.wait_ge(tile_in, i * 144 + 144)
                    pe.wait_ge(tile_done, i + 1)
                    for d in range(2):
                        for m in range(2):
                            for a, b in shifted_halves:
                                last = pe.matmul(flat[:, 1024 * (2 * d + m) + a:1024 * (2 * d + m) + b], lora_w[64 * d:64 * d + 64, m, :],
                                                 small[64 * d:64 * d + 64, m, a:b], start=True, stop=True)
                    last.then_inc(lora_ready, 1)
                    pe.wait_ge(sq_ready, i + 1)
                    pe.wait_ge(exps_done, i + 1)
                    for a, b in shifted_halves:
                        pe.matmul(flat[:, a:b], blockones[:], sq[:, a:b], start=True, stop=True)
                    pe.matmul(big[:, 2, :], lora_w[:, 2, :], small[:, 2, 0:LAT], start=True, stop=True).then_inc(norm_ready, 1)
                    pe.wait_ge(ops_ready, i + 1)
                    for c in range(6):
                        for j in range(4):
                            n, d, h = c * 4 + j, j // 2, 64 * (j % 2)
                            if n >= 2:
                                pe.wait_ge(g_masked, i * 24 + (n - 1))
                            bank = big[:, g_bank[n % 2], :]
                            w = 256 if c < 4 else 128
                            rows = ar[h:h + 64, d, c].rearrange("p a n -> p (a n)")[:, 0:w]
                            pe.matmul(bank[:, 0:w], bm[h:h + 64, d, c], rows, start=True, stop=True)
                            pe.matmul(bank[:, 256:256 + w], km[h:h + 64, d, c], rows, start=True, stop=True).then_inc(g_ready, 1)
                        if c:
                            pe.wait_ge(l_masked, i * 6 + c)
                        for j in range(4):
                            d, h = j // 2, 64 * (j % 2)
                            last = pe.matmul(big[:, t_bank[j % 2], d * CH:(d + 1) * CH], ar[h:h + 64, d, c, 0], bm[h:h + 64, d, c], start=True, stop=True)
                        last.then_inc(l_ready, 1)
                    for n in range(8):
                        if n >= 2:
                            pe.wait_ge(tr_copied, i * 8 + (n - 1))
                        bank = big[:, x_bank[n % 2], :]
                        if n < 6:
                            srcs = [bm[:, 0, n], bm[:, 1, n], km[:, 0, n], km[:, 1, n]]
                        else:
                            part = lat(rkv[:, 2, :]) if n == 6 else con(rkv[:, 2, :])
                            srcs = [part[:, q] for q in range(4 if n == 6 else 2)]
                        for m, s in enumerate(srcs):
                            last = pe.transpose(bank[:, m * CH:(m + 1) * CH], s, ident[:])
                        last.then_inc(tr_ready, 1)
                    pe.wait_ge(tr_copied, i * 8 + 8)
                    pe.wait_ge(l_masked, i * 6 + 6)
                    for pair in range(3):
                        for lv in range(1, LEVELS + 1):
                            for q in range(2):
                                c = 2 * pair + q
                                n = (pair * LEVELS + lv - 1) * 2 + q
                                pe.wait_ge(ltm_ready, i * 36 + (n + 1))
                                pe.wait_ge(x0_done, i * 6 + (c + 1))
                                if n >= 2:
                                    pe.wait_ge(x_updated, i * 36 + (n - 1))
                                for j in range(4):
                                    last = pe.matmul(big[:, t_bank[q], j * CH:(j + 1) * CH], ltm[:, q, j], xs[:, c, j], start=True, stop=True)
                                last.then_inc(t1_ready, 1)
                            for q in range(2):
                                c = 2 * pair + q
                                n = (pair * LEVELS + lv - 1) * 2 + q
                                pe.wait_ge(t1_copied, i * 36 + (n + 1))
                                for j in range(4):
                                    if lv < LEVELS:
                                        pe.matmul(big[:, x_bank[q], j * CH:(j + 1) * CH], xt[:, c, j], t1[:, q, j], start=True, stop=True)
                                    last = pe.matmul(big[:, xt_bank[q], j * CH:(j + 1) * CH], t1[:, q, j], xt[:, c, j], start=True, stop=True)
                                last.then_inc(xx_ready, 1)
                    pe.wait_ge(x_updated, i * 36 + 36)
                    for n in range(6):
                        if n:
                            pe.wait_ge(state_done, i * 5 + n)
                        for j in range(4):
                            d, h = j // 2, 64 * (j % 2)
                            c = ORDER[d][n]
                            out = big[:, x_bank[j % 2], d * 64:d * 64 + 64]
                            pe.matmul(out, ar[h:h + 64, d, c, 0], st[h:h + 64, n % 2, d], start=True, stop=False)
                            last = pe.matmul(out, mg[:, c, j, 256:384], vt[:, c, h:h + 64], start=False, stop=True)
                        last.then_inc(p1_ready, 1)
                        pe.wait_ge(rhs_done, i * 6 + (n + 1))
                        for j in range(4):
                            last = pe.matmul(big[:, xt_bank[1], j * 64:j * 64 + 64], xt[:, ORDER[j // 2][n], j], rhs[:, j % 2, j // 2], start=True, stop=True)
                        last.then_inc(sa_ready, 1)
                        pe.wait_ge(sa_done, i * 6 + (n + 1))
                        if n < 5:
                            for j in range(4):
                                d, h = j // 2, 64 * (j % 2)
                                c = ORDER[d][n]
                                out = big[h:h + 64, xt_bank[0], d * 64:d * 64 + 64]
                                pe.matmul(out, bkt[:, c, d, h:h + 64], sas[:, j], start=True, stop=False)
                                last = pe.matmul(out, bkt[:, c, 2 + d, h:h + 64], vt[:, c, h:h + 64], start=False, stop=True)
                            last.then_inc(delta_ready, 1)
                        if n >= 2:
                            if n > 2:
                                pe.wait_ge(y_copied, i * 4 + (n - 2))
                            for j in range(4):
                                d, h = j // 2, 64 * (j % 2)
                                c = ORDER[d][n]
                                out = big[h:h + 64, (g_bank, t_bank)[j % 2][d], 0:CH]
                                pe.matmul(out, sas[:, j], mg[:, c, j, 128:256], start=True, stop=False)
                                pe.matmul(out, st[h:h + 64, n % 2, d], ar[h:h + 64, d, c, 1], start=False, stop=False)
                                last = pe.matmul(out, vt[:, c, h:h + 64], mg[:, c, j, 384:512], start=False, stop=True)
                            last.then_inc(y_ready, 1)
                    pe.wait_ge(red_in, i * 2 + 1)
                    pe.matmul(big[:, 0, :], blockones[:], ys[:, 0, :], start=True, stop=True).then_inc(red_ready, 1)
                    pe.matmul(big[:, 1, :], blockones[:], sq[:, 0:LAT], start=True, stop=True).then_inc(red_ready, 1)
                    pe.wait_ge(red_in, i * 2 + 2)
                    pe.matmul(big[:, 2, :], blockones[:], ys[:, 1, :], start=True, stop=True).then_inc(red_ready, 1)



ROWS, GRID = 8, 64
CONV = 5
CV_W = LAT + 2 + CTX + 4
CV_OUT = CV_W - 4
GH = 8


def ssm(nc, pt, dt_bias, a_log, d_skip, params, consts, u_out):
    with Stage(nc) as ctx:
        def sb(n, shape):
            return ctx.enter_context(nc.sbuf_tensor(f"ss_{n}", shape, F32))

        def sem(n):
            return ctx.sem(f"ss_{n}")

        ident = sb("ident", [P, CH])
        tri = sb("tri", [P, 2, CH])
        ones = sb("ones", [P, CH])
        one = sb("one", [P, 1])
        bias = sb("bias", [64, 1])
        alog = sb("alog", [P, 64])
        skip = sb("skip", [P, 32])
        dtf = sb("dtf", [64, 3, TOK])
        kinds = sb("kinds", [P, 6, 6, 2, 32])
        mine = sb("mine", [P, 6, 6, 2, GH])
        nat = sb("nat", [P, 6, LAT])
        raw = sb("raw", [P, 6, CV_W])
        par = sb("par", [P, 6, 8])
        xbc = sb("xbc", [P, 6, CV_OUT])
        ex = sb("ex", [P, 6, CV_OUT])
        z = sb("z", [P, 4, LAT])
        ez = sb("ez", [P, 4, LAT])
        xtok = sb("xtok", [P, 6, 512])
        btok = sb("btok", [P, 6, CH])
        cbm = sb("cbm", [P, 2, 4, CH])
        xw = sb("xw", [P, 2, 512])
        xdt = sb("xdt", [P, 2, 512])
        seg = sb("seg", [P, 2, 4, CH])
        h = sb("h", [P, 2, 512])
        hf = sb("hf", [P, 512])
        tmp = sb("tmp", [P, 512])
        ys = sb("ys", [P, 4, 512])
        yf = sb("yf", [P, 4, LAT])
        big = ctx.enter_context(nc.psum_tensor("ss_big", [P, 8, 512], F32))
        row_bank, intra_bank, inter_bank, state_bank, tr_bank = (0, 1), 2, 3, 4, (5, 6)
        DT, DTA, CUM, ECUM, ETOT, WJ = range(6)
        ORDER = ([4, 5, 0, 1, 2, 3], [5, 4, 3, 2, 1, 0])
        steps = [(d, n) for d in range(2) for n in range(6)]

        names = ("const_in dt_in dt_ready dtt_ready dtt_copied dta_ready cum_ready cums_done kinds_done group_in raw_used "
                 "permuted conv_done exp_done xbc_done tr_ready tr_copied cb_ready cb_done row_ready seg_done seg_exp g_done "
                 "xw_done xdt_done inter_ready intra_ready y_done state_ready h_done z_exp group_done stored pads mine_done h_zero "
                 "ty_ready ty_copied out_free").split()
        S = {n: sem(n) for n in names}

        def lat_c(ap):
            return ap[..., 0:LAT].rearrange("p (c n) -> p c n", n=CH)

        def token_tile(ap, c):
            a = c * CH if c < 4 else LAT + 2 + (c - 4) * CH
            return ap[:, a:a + CH]

        with nc.Block() as block:
            @block.sync
            def _(sp):
                for dst, src in ((ident[:], consts["ident"]), (tri[:], consts["tri"]), (ones[:], consts["ones"]), (bias[:], dt_bias),
                                 (alog[:], a_log), (skip[:], d_skip)):
                    sp.dma_start(dst, src).then_inc(S["const_in"], 16)
                sp.dma_start(dtf[:, 0, :], pt[DT_T, 0:64, :]).then_inc(S["dt_in"], 16)
                sp.sem_inc(S["out_free"], 1)
                sp.wait_ge(S["pads"], 1)
                with sp.Fori(0, 4) as g:
                    sp.wait_ge(S["permuted"], g + 1)
                    sp.wait_ge(S["raw_used"], g + 1)
                    xs_rows = [(0, 4, bass.ds(g * 4 + XBC_T, 4)), (4, 1, bass.ds(g + (XBC_T + 16), 1)), (5, 1, bass.ds(g + (XBC_T + 20), 1))]
                    for a, n, rows in xs_rows:
                        sp.dma_start(nat[:, a:a + n, :], pt[rows, :, 0:LAT].rearrange("a p t -> p a t")).then_inc(S["group_in"], 16)
                        sp.dma_start(raw[:, a:a + n, LAT + 4:LAT + 4 + CTX], pt[rows, :, LAT:TOK].rearrange("a p t -> p a t")).then_inc(S["group_in"], 16)
                    sp.wait_ge(S["group_done"], g + 1)
                    sp.dma_start(par[:], params[bass.ds(g, 1)].rearrange("a p t n -> (a p) t n")).then_inc(S["group_in"], 16)
                    sp.dma_start(z[:], pt[bass.ds(g * 4 + Z_T, 4), :, 0:LAT].rearrange("a p t -> p a t")).then_inc(S["group_in"], 16)

            @block.vector
            def _(dve):
                for n in ("raw_used", "group_done", "h_done"):
                    dve.sem_inc(S[n], 1)
                dve.memset(raw[:], 0.0)
                dve.memset(one[:], 1.0)
                dve.drain().then_inc(S["pads"], 1)
                dve.wait_ge(S["const_in"], 96)
                dve.wait_ge(S["dt_in"], 16)
                dve.tensor_scalar(dtf[:, 1, 0:LAT].rearrange("p (c r) -> p c r", r=ROWS), dtf[:, 0, 0:LAT].rearrange("p (r c) -> p c r", c=GRID), bias[:, 0:1], None, ALU.add)
                dve.tensor_scalar(dtf[:, 1, LAT:TOK], dtf[:, 0, LAT:TOK], bias[:, 0:1], None, ALU.add)
                dve.drain().then_inc(S["dt_ready"], 1)
                dve.wait_ge(S["dt_ready"], 2)
                dve.scalar_tensor_tensor(dtf[:, 0, :], dtf[:, 1, :], 0.0, dtf[:, 2, :], ALU.max, ALU.add)
                dve.drain().then_inc(S["dtt_ready"], 1)
                dve.wait_ge(S["dtt_copied"], 1)
                for c in range(6):
                    dve.scalar_tensor_tensor(kinds[:, DTA, c].rearrange("p d h -> p (d h)"), alog[:], -1.0, kinds[:, DT, c].rearrange("p d h -> p (d h)"), ALU.mult, ALU.mult)
                dve.drain().then_inc(S["dta_ready"], 1)
                dve.wait_ge(S["cum_ready"], 1)
                for c in range(6):
                    cum_ps, tot_ps = big[:, 0, c * 64:c * 64 + 64], big[:, 1, c * 64:c * 64 + 64]
                    fl = lambda k: kinds[:, k, c].rearrange("p d h -> p (d h)")
                    dve.tensor_copy(fl(CUM), cum_ps)
                    dve.drain()
                    dve.tensor_tensor(fl(WJ), tot_ps, fl(CUM), ALU.subtract)
                dve.drain().then_inc(S["cums_done"], 1)
                dve.wait_ge(S["kinds_done"], 1)
                for c in range(6):
                    fl = lambda k: kinds[:, k, c].rearrange("p d h -> p (d h)")
                    dve.tensor_tensor(fl(WJ), fl(WJ), fl(DT), ALU.mult)
                dve.drain()
                with dve.Fori(0, 4) as g:
                    dve.wait_ge(S["permuted"], g + 2)
                    dve.tensor_copy(mine[:].rearrange("p k c d h -> p (k c d) h"),
                                    kinds[:].rearrange("p k c d h -> p (k c d) h")[:, :, bass.ds(g * GH, GH)])
                    dve.drain().then_inc(S["mine_done"], 1)
                    for t in range(6):
                        dve.tensor_scalar(xbc[:, t, :], raw[:, t, 0:CV_OUT], par[:, t, 0:1], None, ALU.mult)
                    for k in range(1, CONV):
                        dve.drain()
                        for t in range(6):
                            dve.scalar_tensor_tensor(xbc[:, t, :], raw[:, t, k:k + CV_OUT], par[:, t, k:k + 1], xbc[:, t, :], ALU.mult, ALU.add)
                    dve.drain().then_inc(S["raw_used"], 1)
                    dve.tensor_tensor(xbc[:], xbc[:], par[:, :, 5:6].to_broadcast([P, 6, CV_OUT]), ALU.add)
                    dve.drain().then_inc(S["conv_done"], 1)
                    dve.wait_ge(S["exp_done"], g + 1)
                    dve.tensor_tensor(xbc[:], xbc[:], ex[:], ALU.mult)
                    dve.memset(h[:, 0, :], 0.0)
                    dve.drain().then_inc(S["xbc_done"], 1)
                    dve.wait_ge(S["cb_ready"], g + 1)
                    for d in range(2):
                        dve.tensor_tensor(cbm[:, d], big[:, inter_bank, :].rearrange("p (c n) -> p c n", n=CH),
                                          tri[:, d].unsqueeze(1).to_broadcast([P, 4, CH]), ALU.mult)
                    dve.drain().then_inc(S["cb_done"], 1)
                    dve.wait_ge(S["tr_copied"], g * 8 + 8)
                    for c in range(4):
                        heads = lambda ap: ap.rearrange("p (h n) -> p h n", n=64)
                        dve.tensor_tensor(heads(ys[:, c]), heads(xtok[:, c]),
                                          skip[:, bass.ds(g * GH, GH)].unsqueeze(2).to_broadcast([P, GH, 64]), ALU.mult)
                    dve.drain()
                    m = 0
                    ns = 0
                    for d, n in steps:
                        c = ORDER[d][n]
                        if n < 5:
                            dve.tensor_tensor(heads(hf[:]), heads(h[:, n % 2]), mine[:, ETOT, c, d].unsqueeze(2).to_broadcast([P, GH, 64]), ALU.mult)
                            dve.drain()
                            dve.wait_ge(S["state_ready"], g * 10 + (ns + 1))
                            dve.tensor_tensor(h[:, (n + 1) % 2], hf[:], big[:, state_bank, :], ALU.add)
                            ns += 1
                            dve.drain().then_inc(S["h_done"], 1)
                        if n >= 2:
                            for half in range(2):
                                b = 2 * m + half
                                dve.wait_ge(S["row_ready"], g * 16 + (b + 1))
                                if b >= 2:
                                    dve.wait_ge(S["intra_ready"], g * 16 + (b - 1))
                                for e in range(4):
                                    dve.tensor_scalar(seg[:, b % 2, e], big[:, row_bank[b % 2], e * CH:(e + 1) * CH],
                                                      mine[:, CUM, c, d, 4 * half + e:4 * half + e + 1], 0.0, ALU.subtract, ALU.min)
                                dve.drain().then_inc(S["seg_done"], 1)
                            dve.wait_ge(S["inter_ready"], g * 8 + (m + 1))
                            dve.tensor_tensor(heads(tmp[:]), heads(big[:, inter_bank, :]), mine[:, ECUM, c, d].unsqueeze(2).to_broadcast([P, GH, 64]), ALU.mult)
                            dve.drain()
                            dve.tensor_tensor(ys[:, c], ys[:, c], tmp[:], ALU.add)
                            dve.drain()
                            dve.wait_ge(S["intra_ready"], g * 16 + (2 * m + 2))
                            dve.tensor_tensor(ys[:, c], ys[:, c], big[:, intra_bank, :], ALU.add)
                            dve.drain().then_inc(S["y_done"], 1)
                            m += 1
                        if d == 0 and n == 5:
                            dve.memset(h[:, 0, :], 0.0)
                            dve.drain().then_inc(S["h_done"], 1)
                    dve.wait_ge(S["z_exp"], g + 1)
                    dve.tensor_tensor(z[:], z[:], ez[:], ALU.mult)
                    dve.drain()
                    dve.wait_ge(S["ty_copied"], g * 4 + 4)
                    for t in range(4):
                        dve.tensor_tensor(ez[:, t].rearrange("p (r c) -> p r c", c=GRID), yf[:, t].rearrange("p (c r) -> p r c", r=ROWS),
                                          z[:, t].rearrange("p (r c) -> p r c", c=GRID), ALU.mult)
                    dve.drain().then_inc(S["group_done"], 1)

            @block.scalar
            def _(act):
                act.sem_inc(S["permuted"], 1)
                act.wait_ge(S["dt_ready"], 1)
                act.activation(dtf[:, 2, :], dtf[:, 1, :], ACT.Abs)
                act.drain()
                act.activation(dtf[:, 2, :], dtf[:, 2, :], ACT.Exp, scale=-1.0)
                act.drain()
                act.activation(dtf[:, 2, :], dtf[:, 2, :], ACT.Ln, bias=one[0:64, :])
                act.activation(alog[:], alog[:], ACT.Exp)
                act.drain().then_inc(S["dt_ready"], 1)
                act.wait_ge(S["dtt_ready"], 2)
                act.copy(kinds[:, DT].rearrange("p c d h -> p (c d h)"), big[:, 0, 0:384])
                act.drain().then_inc(S["dtt_copied"], 1)
                act.wait_ge(S["cum_ready"], 1)
                act.wait_ge(S["cums_done"], 1)
                act.activation(kinds[:, ETOT].rearrange("p c d h -> p (c d h)"), big[:, 1, 0:384], ACT.Exp)
                act.activation(kinds[:, ECUM], kinds[:, CUM], ACT.Exp)
                act.activation(kinds[:, WJ], kinds[:, WJ], ACT.Exp)
                act.drain().then_inc(S["kinds_done"], 1)
                with act.Fori(0, 4) as g:
                    act.wait_ge(S["group_in"], g * 128 + 128)
                    act.wait_ge(S["raw_used"], g + 1)
                    for t in range(6):
                        act.copy(raw[:, t, 2:LAT + 2].rearrange("p (c r) -> p c r", r=ROWS), nat[:, t].rearrange("p (r c) -> p c r", c=GRID))
                    act.drain().then_inc(S["permuted"], 1)
                    act.wait_ge(S["conv_done"], g + 1)
                    act.activation(ex[:], xbc[:], ACT.Sigmoid)
                    act.drain().then_inc(S["exp_done"], 1)
                    act.wait_ge(S["out_free"], g + 1)
                    act.activation(ez[:], z[:], ACT.Sigmoid)
                    act.drain().then_inc(S["z_exp"], 1)
                    for n in range(8):
                        act.wait_ge(S["tr_ready"], g * 8 + (n + 1))
                        bank = big[:, tr_bank[n % 2], :]
                        if n < 6:
                            act.copy(xtok[:, n], bank).then_inc(S["tr_copied"], 1)
                        elif n == 6:
                            act.copy(btok[:, 0:4].rearrange("p c n -> p (c n)"), bank).then_inc(S["tr_copied"], 1)
                        else:
                            act.copy(btok[:, 4:6].rearrange("p c n -> p (c n)"), bank[:, 0:256]).then_inc(S["tr_copied"], 1)
                    for b in range(16):
                        act.wait_ge(S["seg_done"], g * 16 + (b + 1))
                        act.activation(seg[:, b % 2], seg[:, b % 2], ACT.Exp).then_inc(S["seg_exp"], 1)
                    for t in range(4):
                        act.wait_ge(S["ty_ready"], g * 4 + (t + 1))
                        act.copy(yf[:, t], big[:, tr_bank[t % 2], :]).then_inc(S["ty_copied"], 1)

            @block.gpsimd
            def _(pool):
                heads = lambda ap: ap.rearrange("p (h n) -> p h n", n=64)
                with pool.Fori(0, 4) as g:
                    pool.wait_ge(S["tr_copied"], g * 8 + 8)
                    pool.wait_ge(S["mine_done"], g + 1)
                    pool.wait_ge(S["cb_done"], g + 1)
                    m = ns = 0
                    for d, n in steps:
                        c = ORDER[d][n]
                        if n < 5:
                            if ns >= 2:
                                pool.wait_ge(S["state_ready"], g * 10 + (ns - 1))
                            pool.tensor_tensor(heads(xw[:, ns % 2]), heads(xtok[:, c]), mine[:, WJ, c, d].unsqueeze(2).to_broadcast([P, GH, 64]), ALU.mult).then_inc(S["xw_done"], 1)
                            ns += 1
                        if n >= 2:
                            if m >= 2:
                                pool.wait_ge(S["intra_ready"], g * 16 + 2 * (m - 1))
                            pool.tensor_tensor(heads(xdt[:, m % 2]), heads(xtok[:, c]), mine[:, DT, c, d].unsqueeze(2).to_broadcast([P, GH, 64]), ALU.mult).then_inc(S["xdt_done"], 1)
                            for half in range(2):
                                b = 2 * m + half
                                pool.wait_ge(S["seg_exp"], g * 16 + (b + 1))
                                pool.tensor_tensor(seg[:, b % 2], seg[:, b % 2], cbm[:, d, c].unsqueeze(1).to_broadcast([P, 4, CH]), ALU.mult).then_inc(S["g_done"], 1)
                            m += 1
                    pool.wait_ge(S["group_done"], g + 2)
                    pool.dma_start(u_out[bass.ds(g * 4, 4)].rearrange("a p t -> p a t"), ez[:]).then_inc(S["stored"], 16)
                    pool.wait_ge(S["stored"], g * 16 + 16)
                    pool.sem_inc(S["out_free"], 1)

            @block.tensor
            def _(pe):
                pe.wait_ge(S["const_in"], 96)
                pe.wait_ge(S["dtt_ready"], 1)
                for c in range(6):
                    last = pe.transpose(big[:, 0, c * 64:c * 64 + 64], dtf[:, 0, c * CH:(c + 1) * CH], ident[0:64, 0:64])
                last.then_inc(S["dtt_ready"], 1)
                pe.wait_ge(S["dta_ready"], 1)
                for c in range(6):
                    for d in range(2):
                        rhs = kinds[:, DTA, c, d]
                        pe.matmul(big[:, 0, c * 64 + d * 32:c * 64 + d * 32 + 32], tri[:, d], rhs, start=True, stop=True)
                        last = pe.matmul(big[:, 1, c * 64 + d * 32:c * 64 + d * 32 + 32], ones[:], rhs, start=True, stop=True)
                last.then_inc(S["cum_ready"], 1)
                pe.wait_ge(S["kinds_done"], 1)
                with pe.Fori(0, 4) as g:
                    pe.wait_ge(S["xbc_done"], g + 1)
                    pe.wait_ge(S["mine_done"], g + 1)
                    for c in range(4):
                        last = pe.matmul(big[:, inter_bank, c * CH:(c + 1) * CH], token_tile(xbc[:, 4], c), token_tile(xbc[:, 5], c), start=True, stop=True)
                    last.then_inc(S["cb_ready"], 1)
                    for n in range(8):
                        if n >= 2:
                            pe.wait_ge(S["tr_copied"], g * 8 + (n - 1))
                        bank = big[:, tr_bank[n % 2], :]
                        srcs = [token_tile(xbc[:, t], n) for t in range(4)] if n < 6 else [token_tile(xbc[:, 4], c) for c in (range(4) if n == 6 else (4, 5))]
                        for k, s in enumerate(srcs):
                            last = pe.transpose(bank[:, k * CH:(k + 1) * CH], s, ident[:])
                        last.then_inc(S["tr_ready"], 1)
                    pe.wait_ge(S["cb_done"], g + 1)
                    pe.wait_ge(S["tr_copied"], g * 8 + 8)

                    def cum_rows(b):
                        d, c = b // 8, ORDER[b // 8][2 + b // 2 % 4]
                        if b >= 2:
                            pe.wait_ge(S["seg_done"], g * 16 + (b - 1))
                        for e in range(4):
                            k = 4 * (b % 2) + e
                            last = pe.matmul(big[:, row_bank[b % 2], e * CH:(e + 1) * CH], mine[:, DTA, c, d, k:k + 1].to_broadcast([P, CH]), tri[:, d], start=True, stop=True)
                        last.then_inc(S["row_ready"], 1)

                    cum_rows(0)
                    m = ns = 0
                    for d, n in steps:
                        c = ORDER[d][n]
                        if n < 5:
                            pe.wait_ge(S["xw_done"], g * 10 + (ns + 1))
                            pe.wait_ge(S["h_done"], g * 11 + (ns + d + 1))
                            pe.matmul(big[:, state_bank, :], btok[:, c], xw[:, ns % 2], start=True, stop=True).then_inc(S["state_ready"], 1)
                            ns += 1
                        if n >= 2:
                            if m:
                                pe.wait_ge(S["y_done"], g * 8 + m)
                            pe.wait_ge(S["h_done"], g * 11 + (n + 6 * d + 1))
                            pe.matmul(big[:, inter_bank, :], token_tile(xbc[:, 5], c), h[:, n % 2], start=True, stop=True).then_inc(S["inter_ready"], 1)
                            pe.wait_ge(S["xdt_done"], g * 8 + (m + 1))
                            for half in range(2):
                                b = 2 * m + half
                                if b < 15:
                                    cum_rows(b + 1)
                                pe.wait_ge(S["g_done"], g * 16 + (b + 1))
                                for e in range(4):
                                    k = 4 * half + e
                                    last = pe.matmul(big[:, intra_bank, k * 64:k * 64 + 64], seg[:, b % 2, e], xdt[:, m % 2, k * 64:k * 64 + 64], start=True, stop=True)
                                last.then_inc(S["intra_ready"], 1)
                            m += 1
                    pe.wait_ge(S["y_done"], g * 8 + 8)
                    for t in range(4):
                        if t >= 2:
                            pe.wait_ge(S["ty_copied"], g * 4 + (t - 1))
                        for c in range(4):
                            last = pe.transpose(big[:, tr_bank[t % 2], c * CH:(c + 1) * CH], ys[:, c, t * CH:(t + 1) * CH], ident[:])
                        last.then_inc(S["ty_ready"], 1)
                    pe.wait_ge(S["ty_copied"], g * 4 + 4)



KD = D // P


def norm_step(nc, name, x_in, x_out, h_out, consts, tokens, gate_mod=None, h_mod=None, shift=None, scale=None,
              gain=None, delta=None, delta_tokens=0, gate=None, post=None):
    def streams(n):
        return [(0, 0, LAT)] + ([(1, LAT, n)] if n > LAT else [])

    rounds = ([(0, delta_tokens)] if post is not None else []) + ([(1, tokens)] if h_out is not None else [])
    with Stage(nc) as ctx:
        def sb(n, shape):
            return ctx.enter_context(nc.sbuf_tensor(f"{name}_{n}", shape, F32))

        def sem(n):
            return ctx.sem(f"{name}_{n}")

        x = sb("x", [P, KD, tokens])
        dl = sb("delta", [P, KD, delta_tokens]) if delta is not None else None
        h = sb("h", [P, KD, tokens])
        sq = sb("sq", [P, 2, tokens])
        rstd = sb("rstd", [P, tokens])
        mod = sb("mod", [P, 2, 48, 2])
        bias = sb("bias", [P, 2, 48])
        gains = sb("gains", [P, 2, KD])
        fac = sb("fac", [P, 2, 2, KD])
        eps = sb("eps", [P, 1])
        ones = sb("ones", [P, CH])
        acc = ctx.enter_context(nc.psum_tensor(f"{name}_acc", [P, 1024], F32))
        loaded, eps_set, mods_done, squares, square_used, rstd_done = (sem(n) for n in ("loaded", "eps_set", "mods_done", "squares", "square_used", "rstd_done"))
        x_ready, scaled, h_ready, stored = sem("x_ready"), sem("scaled"), sem("h_ready"), sem("stored")
        loads = [(ones[:], consts["ones"])]
        for n, m in enumerate((gate_mod, h_mod)):
            if m is not None:
                loads += [(mod[:, n].rearrange("p k s -> p (k s)"), m[0]), (bias[:, n], m[1])]
        if h_out is not None:
            loads.append((gains[:, 1, :], gain))
        if post is not None:
            loads.append((gains[:, 0, :], post))
        if delta is not None:
            loads.append((dl[:], delta[:, 0:delta_tokens].rearrange("(k p) t -> p k t", p=P)))
        for src, a, b in x_in:
            loads.append((x[:, :, a:b], src.rearrange("(k p) t -> p k t", p=P)))

        with nc.Block() as block:
            @block.sync
            def _(sp):
                for dst, src in loads:
                    sp.dma_start(dst, src).then_inc(loaded, 16)
                n = 0
                if x_out is not None:
                    sp.wait_ge(x_ready, 1)
                    sp.dma_start(x_out[:, 0:tokens].rearrange("(k p) t -> p k t", p=P), x[:]).then_inc(stored, 16)
                    n += 16
                if h_out is not None:
                    sp.wait_ge(h_ready, 1)
                    sp.dma_start(h_out[:, 0:tokens].rearrange("(k p) t -> p k t", p=P), h[:]).then_inc(stored, 16)
                    n += 16
                sp.wait_ge(stored, n)

            @block.vector
            def _(dve):
                dve.memset(eps[:], 1e-6)
                dve.drain().then_inc(eps_set, 1)
                dve.wait_ge(loaded, 16 * len(loads))
                for n, m in enumerate((gate_mod, h_mod)):
                    if m is not None:
                        dve.tensor_tensor(mod[:, n], mod[:, n], bias[:, n].unsqueeze(2).to_broadcast([P, 48, 2]), ALU.add)
                dve.drain()
                for s, a, b in streams(delta_tokens):
                    if post is not None:
                        dve.tensor_tensor(fac[:, 0, s], mod[:, 0, gate:gate + KD, s], gains[:, 0], ALU.mult)
                    elif delta is not None:
                        dve.tensor_copy(fac[:, 0, s], mod[:, 0, gate:gate + KD, s])
                if h_out is not None:
                    for s, a, b in streams(tokens):
                        dve.scalar_tensor_tensor(fac[:, 1, s], mod[:, 1, scale:scale + KD, s], 1.0, gains[:, 1], ALU.add, ALU.mult)
                dve.drain().then_inc(mods_done, 1)
                if post is not None:
                    dve.wait_ge(rstd_done, 1)
                    dve.tensor_tensor(dl[:], dl[:], rstd[:, 0:delta_tokens].unsqueeze(1).to_broadcast([P, KD, delta_tokens]), ALU.mult)
                    dve.drain()
                if delta is not None:
                    for k in range(KD):
                        for s, a, b in streams(delta_tokens):
                            dve.scalar_tensor_tensor(x[:, k, a:b], dl[:, k, a:b], fac[:, 0, s, k:k + 1], x[:, k, a:b], ALU.mult, ALU.add)
                dve.drain().then_inc(x_ready, 1)
                if h_out is not None:
                    dve.wait_ge(rstd_done, len(rounds))
                    dve.tensor_tensor(h[:], x[:], rstd[:].unsqueeze(1).to_broadcast([P, KD, tokens]), ALU.mult)
                    dve.drain().then_inc(scaled, 1)

            @block.scalar
            def _(act):
                act.wait_ge(loaded, 16 * len(loads))
                act.wait_ge(eps_set, 1)
                for r, (what, toks) in enumerate(rounds):
                    src = (dl, x)[what]
                    if what == 1:
                        act.wait_ge(x_ready, 1)
                    for k in range(KD):
                        if r * KD + k >= 2:
                            act.wait_ge(square_used, r * KD + k - 1)
                        act.activation(sq[:, k % 2, 0:toks], src[:, k], ACT.Square).then_inc(squares, 1)
                    act.wait_ge(square_used, (r + 1) * KD)
                    act.activation(rstd[:, 0:toks], acc[:, 0:toks], ACT.Ln, scale=1.0 / D, bias=eps[:])
                    act.drain()
                    act.activation(rstd[:, 0:toks], rstd[:, 0:toks], ACT.Exp, scale=-0.5)
                    act.drain().then_inc(rstd_done, 1)
                if h_out is not None:
                    act.wait_ge(scaled, 1)
                    for k in range(KD):
                        for s, a, b in streams(tokens):
                            act.activation(h[:, k, a:b], h[:, k, a:b], ACT.Identity, scale=fac[:, 1, s, k:k + 1], bias=mod[:, 1, shift + k, s:s + 1])
                    act.drain().then_inc(h_ready, 1)

            @block.tensor
            def _(pe):
                pe.wait_ge(loaded, 16 * len(loads))
                for r, (what, toks) in enumerate(rounds):
                    if r:
                        pe.wait_ge(rstd_done, r)
                    for k in range(KD):
                        pe.wait_ge(squares, r * KD + k + 1)
                        for s, a, b in streams(toks):
                            last = pe.matmul(acc[:, a:b], ones[:], sq[:, k % 2, a:b], start=(k == 0), stop=(k == KD - 1))
                        last.then_inc(square_used, 1)


def silu_columns(nc, name, c_in, c_out):
    with Stage(nc) as ctx:
        n = c_in.shape[1]
        c = ctx.enter_context(nc.sbuf_tensor(f"{name}_c", [P, n], F32))
        s = ctx.enter_context(nc.sbuf_tensor(f"{name}_s", [P, n], F32))
        moved, done = (ctx.sem(f"{name}_{k}") for k in ("moved", "done"))
        with nc.Block() as block:
            @block.sync
            def _(sp):
                sp.dma_start(c[:], c_in).then_inc(moved, 16)
                sp.wait_ge(done, 2)
                sp.dma_start(c_out, c[:]).then_inc(moved, 16)
                sp.wait_ge(moved, 32)

            @block.scalar
            def _(act):
                act.wait_ge(moved, 16)
                act.activation(s[:], c[:], ACT.Sigmoid).then_inc(done, 1)

            @block.vector
            def _(dve):
                dve.wait_ge(done, 1)
                dve.tensor_tensor(c[:], c[:], s[:], ALU.mult).then_inc(done, 1)


def branch_norm(nc, u_in, gain, consts, out):
    with Stage(nc) as ctx:
        def sb(n, shape):
            return ctx.enter_context(nc.sbuf_tensor(f"bn_{n}", shape, F32))

        KT = 16
        u, sq, rstd = sb("u", [P, KT, LAT]), sb("sq", [P, 2, LAT]), sb("rstd", [P, LAT])
        g, eps, ones = sb("g", [P, KT]), sb("eps", [P, 1]), sb("ones", [P, CH])
        acc = ctx.enter_context(nc.psum_tensor("bn_acc", [P, LAT], F32))
        loaded, squares, square_used, rstd_done, eps_set, done, stored = (ctx.sem(f"bn_{n}") for n in (
            "loaded", "squares", "square_used", "rstd_done", "eps_set", "done", "stored"))
        with nc.Block() as block:
            @block.sync
            def _(sp):
                sp.dma_start(g[:], gain).then_inc(loaded, 16)
                sp.dma_start(ones[:], consts["ones"]).then_inc(loaded, 16)
                sp.dma_start(u[:], u_in.rearrange("k p t -> p k t")).then_inc(loaded, 16)
                sp.wait_ge(done, 1)
                sp.dma_start(out.rearrange("k p t -> p k t"), u[:]).then_inc(stored, 16)
                sp.wait_ge(stored, 16)

            @block.scalar
            def _(act):
                act.wait_ge(loaded, 48)
                for k in range(KT):
                    if k >= 2:
                        act.wait_ge(square_used, k - 1)
                    act.activation(sq[:, k % 2], u[:, k], ACT.Square).then_inc(squares, 1)
                act.wait_ge(square_used, KT)
                act.wait_ge(eps_set, 1)
                act.activation(rstd[:], acc[:], ACT.Ln, scale=1.0 / (KT * P), bias=eps[:])
                act.drain()
                act.activation(rstd[:], rstd[:], ACT.Exp, scale=-0.5)
                act.drain().then_inc(rstd_done, 1)

            @block.tensor
            def _(pe):
                pe.wait_ge(loaded, 48)
                for k in range(KT):
                    pe.wait_ge(squares, k + 1)
                    pe.matmul(acc[:], ones[:], sq[:, k % 2], start=(k == 0), stop=(k == KT - 1)).then_inc(square_used, 1)

            @block.vector
            def _(dve):
                dve.memset(eps[:], 1e-6)
                dve.drain().then_inc(eps_set, 1)
                dve.wait_ge(rstd_done, 1)
                for k in range(KT):
                    dve.scalar_tensor_tensor(u[:, k], u[:, k], g[:, k:k + 1], rstd[:], ALU.mult, ALU.mult)
                dve.drain().then_inc(done, 1)


def gated_sum(nc, gates, a_in, b_in, out):
    with Stage(nc) as ctx:
        g = ctx.enter_context(nc.sbuf_tensor("gs_g", [P, 2, 2, LAT], F32))
        v = ctx.enter_context(nc.sbuf_tensor("gs_v", [P, 2, 2, LAT], F32))
        loaded = [ctx.sem(f"gs_loaded{s}") for s in range(2)]
        stored = [ctx.sem(f"gs_stored{s}") for s in range(2)]
        gated, done = (ctx.sem(f"gs_{n}") for n in ("gated", "done"))
        with nc.Block() as block:
            @block.sync
            def _(sp):
                for k in range(KD):
                    s = k % 2
                    sp.wait_ge(stored[s], 16 * (k // 2))
                    sp.dma_start(g[:, s, 0], gates[k, :, 0:LAT]).then_inc(loaded[s], 16)
                    sp.dma_start(g[:, s, 1], gates[KD + k, :, 0:LAT]).then_inc(loaded[s], 16)
                    sp.dma_start(v[:, s, 0], a_in[k * P:(k + 1) * P, :]).then_inc(loaded[s], 16)
                    sp.dma_start(v[:, s, 1], b_in[k * P:(k + 1) * P, :]).then_inc(loaded[s], 16)

            @block.scalar
            def _(act):
                for k in range(KD):
                    act.wait_ge(loaded[k % 2], 64 * (k // 2 + 1))
                    act.activation(g[:, k % 2], g[:, k % 2], ACT.Sigmoid).then_inc(gated, 1)

            @block.vector
            def _(dve):
                for k in range(KD):
                    s = k % 2
                    dve.wait_ge(gated, k + 1)
                    dve.tensor_tensor(v[:, s], v[:, s], g[:, s], ALU.mult)
                    dve.drain()
                    dve.tensor_tensor(v[:, s, 0], v[:, s, 0], v[:, s, 1], ALU.add)
                    dve.drain().then_inc(done, 1)

            @block.gpsimd
            def _(pool):
                for k in range(KD):
                    pool.wait_ge(done, k + 1)
                    pool.dma_start(out[k * P:(k + 1) * P, :], v[:, k % 2, 0]).then_inc(stored[k % 2], 16)
                for s in range(2):
                    pool.wait_ge(stored[s], 16 * KD // 2)


N_EXP, CAP = 16, 64


def route(nc, h_in, router, consts, xe_out, sel_out):
    with Stage(nc) as ctx:
        def sb(n, shape):
            return ctx.enter_context(nc.sbuf_tensor(f"ro_{n}", shape, F32))

        ht, htok = sb("ht", [P, KD, LAT]), sb("htok", [P, 4, D])
        wr, ident = sb("wr", [P, KD, N_EXP]), sb("ident", [P, CH])
        slots = sb("slots", [P, CAP])
        aff, mx, work = sb("aff", [P, 4, N_EXP]), sb("mx", [P, 4]), sb("work", [N_EXP, 3, LAT])
        top = sb("top", [N_EXP, 8, 8])
        ones = sb("ones", [N_EXP, LAT])
        slot_t, val = sb("slot_t", [P, 4, N_EXP]), sb("val", [P, 4, N_EXP])
        onehot = sb("onehot", [P, 4, N_EXP * CAP])
        weighted = sb("weighted", [P, 4, N_EXP * CAP])
        xe, sel = sb("xe", [P, KD, N_EXP * CAP]), sb("sel", [P, KD, LAT])
        big = ctx.enter_context(nc.psum_tensor("ro_big", [P, 8, 512], F32))
        S = {n: ctx.sem(f"ro_{n}") for n in (
            "loaded logits maxed exped aff_done rows_ready slots_done cols_ready hot_done weighted_done ht_ready ht_copied xe_ready xe_copied sel_ready sel_copied stored").split()}
        with nc.Block() as block:
            @block.sync
            def _(sp):
                sp.dma_start(wr[:], router.rearrange("(k p) e -> p k e", p=P)).then_inc(S["loaded"], 16)
                sp.dma_start(ident[:], consts["ident"]).then_inc(S["loaded"], 16)
                sp.dma_start(slots[:], consts["slots"]).then_inc(S["loaded"], 16)
                sp.dma_start(ht[:], h_in[:, 0:LAT].rearrange("(k p) t -> p k t", p=P)).then_inc(S["loaded"], 16)
                sp.wait_ge(S["xe_copied"], 16)
                sp.dma_start(xe_out.rearrange("k p n -> p k n"), xe[:]).then_inc(S["stored"], 16)
                sp.wait_ge(S["sel_copied"], 8)
                sp.dma_start(sel_out.rearrange("k p n -> p k n"), sel[:]).then_inc(S["stored"], 16)
                sp.wait_ge(S["stored"], 32)

            @block.tensor
            def _(pe):
                pe.wait_ge(S["loaded"], 64)
                for t in range(4):
                    for k in range(KD):
                        last = pe.matmul(big[:, 0, t * 16:t * 16 + 16], ht[:, k, t * P:(t + 1) * P], wr[:, k], start=(k == 0), stop=(k == KD - 1))
                last.then_inc(S["logits"], 1)
                for n in range(8):
                    t, half = n // 2, n % 2
                    if n >= 2:
                        pe.wait_ge(S["ht_copied"], n - 1)
                    for q in range(4):
                        last = pe.transpose(big[:, 2 + n % 2, q * P:(q + 1) * P], ht[:, 4 * half + q, t * P:(t + 1) * P], ident[:])
                    last.then_inc(S["ht_ready"], 1)
                pe.wait_ge(S["aff_done"], 1)
                for t in range(4):
                    last = pe.transpose(big[0:N_EXP, 1, t * P:(t + 1) * P], aff[:, t], ident[:])
                last.then_inc(S["rows_ready"], 1)
                pe.wait_ge(S["slots_done"], 1)
                for t in range(4):
                    last = pe.transpose(big[:, 0, t * 16:t * 16 + 16], work[:, 2, t * P:(t + 1) * P], ident[0:N_EXP, 0:N_EXP])
                last.then_inc(S["cols_ready"], 1)
                pe.wait_ge(S["ht_copied"], 8)
                pe.wait_ge(S["hot_done"], 1)
                for n in range(16):
                    k, half = n // 2, n % 2
                    if n >= 2:
                        pe.wait_ge(S["xe_copied"], n - 1)
                    for t in range(4):
                        last = pe.matmul(big[:, 4 + n % 2, :], htok[:, t, k * P:(k + 1) * P], onehot[:, t, half * 512:half * 512 + 512], start=(t == 0), stop=(t == 3))
                    last.then_inc(S["xe_ready"], 1)
                pe.wait_ge(S["weighted_done"], 1)
                for n in range(8):
                    if n >= 2:
                        pe.wait_ge(S["sel_copied"], n - 1)
                    for t in range(4):
                        last = pe.transpose(big[:, 6 + n % 2, t * P:(t + 1) * P], weighted[:, t, n * P:(n + 1) * P], ident[:])
                    last.then_inc(S["sel_ready"], 1)

            @block.vector
            def _(dve):
                dve.memset(ones[:], 1.0)
                dve.wait_ge(S["logits"], 1)
                logits = big[:, 0, 0:64].rearrange("p (t e) -> p t e", e=N_EXP)
                dve.tensor_reduce(mx[:], logits, AX, ALU.max)
                dve.drain()
                dve.tensor_tensor(aff[:], logits, mx[:].unsqueeze(2).to_broadcast([P, 4, N_EXP]), ALU.subtract)
                dve.drain().then_inc(S["maxed"], 1)
                dve.wait_ge(S["exped"], 1)
                dve.tensor_reduce(mx[:], aff[:], AX, ALU.add)
                dve.drain()
                dve.reciprocal(mx[:], mx[:])
                dve.drain()
                dve.tensor_tensor(aff[:], aff[:], mx[:].unsqueeze(2).to_broadcast([P, 4, N_EXP]), ALU.mult)
                dve.drain().then_inc(S["aff_done"], 1)
                dve.wait_ge(S["rows_ready"], 1)
                dve.tensor_copy(work[:, 0], big[0:N_EXP, 1, :])
                for r in range(8):
                    dve.drain()
                    dve.max(out=top[:, r], in_=work[:, 0])
                    dve.drain()
                    dve.match_replace(out=work[:, 0], in_to_replace=top[:, r], in_values=work[:, 0], imm_value=-1.0)
                dve.drain()
                dve.tensor_scalar(work[:, 1], work[:, 0], 0.0, None, ALU.is_lt)
                dve.drain()
                dve.tensor_tensor_scan(work[:, 2], ones[:], work[:, 1], 0.0, ALU.mult, ALU.add)
                dve.drain()
                dve.tensor_tensor(work[:, 2], work[:, 2], work[:, 1], ALU.mult)
                dve.drain().then_inc(S["slots_done"], 1)
                dve.wait_ge(S["cols_ready"], 1)
                dve.tensor_copy(slot_t[:], big[:, 0, 0:64].rearrange("p (t e) -> p t e", e=N_EXP))
                dve.drain()
                for t in range(4):
                    dve.tensor_tensor(onehot[:, t].rearrange("p (e c) -> p e c", c=CAP), slot_t[:, t].unsqueeze(2).to_broadcast([P, N_EXP, CAP]),
                                      slots[:].unsqueeze(1).to_broadcast([P, N_EXP, CAP]), ALU.is_equal)
                dve.drain().then_inc(S["hot_done"], 1)
                for t in range(4):
                    dve.tensor_tensor(weighted[:, t].rearrange("p (e c) -> p e c", c=CAP), onehot[:, t].rearrange("p (e c) -> p e c", c=CAP),
                                      aff[:, t].unsqueeze(2).to_broadcast([P, N_EXP, CAP]), ALU.mult)
                dve.drain().then_inc(S["weighted_done"], 1)
                for n in range(8):
                    dve.wait_ge(S["sel_ready"], n + 1)
                    dve.tensor_copy(sel[:, n], big[:, 6 + n % 2, :]).then_inc(S["sel_copied"], 1)

            @block.scalar
            def _(act):
                act.wait_ge(S["maxed"], 1)
                act.activation(aff[:], aff[:], ACT.Exp).then_inc(S["exped"], 1)
                for n in range(8):
                    act.wait_ge(S["ht_ready"], n + 1)
                    act.copy(htok[:, n // 2, (n % 2) * 512:(n % 2) * 512 + 512], big[:, 2 + n % 2, :]).then_inc(S["ht_copied"], 1)
                for n in range(16):
                    act.wait_ge(S["xe_ready"], n + 1)
                    act.copy(xe[:, n // 2, (n % 2) * 512:(n % 2) * 512 + 512], big[:, 4 + n % 2, :]).then_inc(S["xe_copied"], 1)


def experts(nc, xe_in, sel_in, w1, w3, w2, out):
    with Stage(nc) as ctx:
        def sb(n, shape):
            return ctx.enter_context(nc.sbuf_tensor(f"ex_{n}", shape, F32))

        def sem(n):
            return ctx.sem(f"ex_{n}")

        SL = 2
        xe = sb("xe", [P, KD, N_EXP * CAP])
        sel = sb("sel", [P, KD, LAT])
        w13 = [sb(f"w13_{s}", [P, 2, KD, 512]) for s in range(SL)]
        w2s = [sb(f"w2_{s}", [P, KD, 512]) for s in range(2)]
        sg = sb("sg", [P, 2, 4 * CAP])
        hid = sb("hid", [P, KD, CAP])
        ye = sb("ye", [P, KD, D])
        res = sb("res", [P, 2, LAT])
        big = ctx.enter_context(nc.psum_tensor("ex_big", [P, 8, 512], F32))
        in_ = sem("in_")
        w13_in = [sem(f"w13_in{s}") for s in range(2)]
        w2_in = [sem(f"w2_in{s}") for s in range(2)]
        up_ready, act_done, hid_done, down_ready, ye_done = sem("up_ready"), sem("act_done"), sem("hid_done"), sem("down_ready"), sem("ye_done")
        out_ready, out_done, stored = sem("out_ready"), sem("out_done"), [sem("stored0"), sem("stored1")]
        with nc.Block() as block:
            @block.sync
            def _(sp):
                def load13(e, half):
                    for m, w in enumerate((w1, w3)):
                        sp.dma_start(w13[half][:, m], w[bass.ds(e, 1), half].rearrange("a p k n -> (a p) k n")).then_inc(w13_in[half], 16)

                def load2(e, half):
                    sp.dma_start(w2s[half][:], w2[bass.ds(e, 1), half].rearrange("a p k n -> (a p) k n")).then_inc(w2_in[half], 16)

                sp.dma_start(xe[:], xe_in.rearrange("k p n -> p k n")).then_inc(in_, 16)
                sp.dma_start(sel[:], sel_in.rearrange("k p n -> p k n")).then_inc(in_, 16)
                for half in range(2):
                    load13(0, half)
                for half in range(2):
                    load2(0, half)
                with sp.Fori(1, N_EXP) as e:
                    for half in range(2):
                        sp.wait_ge(up_ready, e * 2 + (half - 1))
                        load13(e, half)
                    for half in range(2):
                        sp.wait_ge(down_ready, e * 2 + half)
                        load2(e, half)

            @block.tensor
            def _(pe):
                pe.sem_inc(down_ready, 1)
                pe.wait_ge(in_, 32)

                def expert(e2, par):
                    e = e2 * 2 + par
                    for half in range(2):
                        pe.wait_ge(w13_in[half], e * 32 + 32)
                        pe.wait_ge(hid_done, e * 2 + (half + 1))
                        for m in range(2):
                            for f in range(4):
                                for k in range(KD):
                                    last = pe.matmul(big[:, 2 * half + m, f * CAP:(f + 1) * CAP], w13[half][:, m, k, f * P:(f + 1) * P],
                                                     xe[:, k, bass.ds(e * CAP, CAP)], start=(k == 0), stop=(k == KD - 1))
                        last.then_inc(up_ready, 1)
                    for half in range(2):
                        pe.wait_ge(w2_in[half], e * 16 + 16)
                        pe.wait_ge(hid_done, e * 2 + 4)
                        pe.wait_ge(ye_done, e * 2 + (half + 1))
                        for k in range(KD):
                            last = pe.matmul(big[64 * par:64 * par + 64, 4 + half, :], hid[:, k], w2s[half][:, k], start=(k == 0), stop=(k == KD - 1))
                        last.then_inc(down_ready, 1)
                with pe.Fori(0, N_EXP // 2) as e2:
                    expert(e2, 0)
                    expert(e2, 1)
                pe.wait_ge(ye_done, 2 * N_EXP + 2)
                for d in range(KD):
                    if d >= 2:
                        pe.wait_ge(out_done, d - 1)
                    for k in range(KD):
                        last = pe.matmul(big[:, 6 + d % 2, :], ye[:, k, d * P:(d + 1) * P], sel[:, k], start=(k == 0), stop=(k == KD - 1))
                    last.then_inc(out_ready, 1)

            @block.scalar
            def _(act):
                with act.Fori(0, N_EXP // 2) as e2:
                    for par in range(2):
                        for half in range(2):
                            act.wait_ge(up_ready, e2 * 4 + (2 * par + half + 1))
                            act.wait_ge(hid_done, e2 * 4 + (2 * par + half + 1))
                            act.activation(sg[:, half], big[:, 2 * half, 0:4 * CAP], ACT.Sigmoid).then_inc(act_done, 1)
                        for half in range(2):
                            act.wait_ge(down_ready, e2 * 4 + (2 * par + half + 2))
                            rows = slice(64 * par, 64 * par + 64)
                            act.copy(ye[rows, bass.ds(e2, 1), half * 512:half * 512 + 512].rearrange("p a n -> p (a n)"), big[rows, 4 + half, :]).then_inc(ye_done, 1)

            @block.vector
            def _(dve):
                dve.sem_inc(hid_done, 2)
                dve.sem_inc(ye_done, 2)
                with dve.Fori(0, N_EXP) as e:
                    for half in range(2):
                        dve.wait_ge(act_done, e * 2 + (half + 1))
                        if half == 0:
                            dve.wait_ge(down_ready, e * 2 + 1)
                        dve.tensor_tensor(sg[:, half], sg[:, half], big[:, 2 * half, 0:4 * CAP], ALU.mult)
                        dve.drain()
                        dve.tensor_tensor(hid[:, 4 * half:4 * half + 4].rearrange("p k n -> p (k n)"), sg[:, half], big[:, 2 * half + 1, 0:4 * CAP], ALU.mult)
                        dve.drain().then_inc(hid_done, 1)
                for d in range(KD):
                    if d >= 2:
                        dve.wait_ge(stored[d % 2], 16 * (d // 2))
                    dve.wait_ge(out_ready, d + 1)
                    dve.tensor_copy(res[:, d % 2], big[:, 6 + d % 2, :]).then_inc(out_done, 1)

            @block.gpsimd
            def _(pool):
                for d in range(KD):
                    pool.wait_ge(out_done, d + 1)
                    pool.dma_start(out[d * P:(d + 1) * P, :], res[:, d % 2]).then_inc(stored[d % 2], 16)
                for s in range(2):
                    pool.wait_ge(stored[s], 16 * KD // 2)



HQ, HD = 16, 64
ATT_SCALE = HD ** -0.5


def attention(nc, qkv, sinks, gains, consts, o_out):
    with Stage(nc) as ctx:
        def sb(n, shape):
            return ctx.enter_context(nc.sbuf_tensor(f"at_{n}", shape, F32))

        ident, blockones, turn = sb("ident", [P, CH]), sb("blockones", [P, CH]), sb("turn", [P, CH])
        cos, sin, mask = sb("cos", [P, LAT]), sb("sin", [P, LAT]), sb("mask", [P, 3 * CH])
        sink, sink4, gain, eps = sb("sink", [P, HQ]), sb("sink4", [P, 4]), sb("gain", [P, 2]), sb("eps", [P, 1])
        x = sb("x", [P, 3, TOK])
        v = sb("v", [HD, TOK])
        sq, rstd = sb("sq", [P, 3, TOK]), sb("rstd", [P, 3, TOK])
        vt = sb("vt", [P, 6, HD])
        s = sb("s", [P, 2, 384])
        p = sb("p", [P, 2, 640])
        pt_s = sb("pt", [P, 2, 640])
        st = sb("st", [P, 2, 8])
        o = sb("o", [P, 2, TOK])
        big = ctx.enter_context(nc.psum_tensor("at_big", [P, 8, 512], F32))
        flat = big[:].rearrange("p b n -> p (b n)")
        S = {n: ctx.sem(f"at_{n}") for n in (
            "const_in head_in squares sums_ready rstd_done normed turned roped vt_ready vt_copied sinks_done scores maxed exped den_done scaled "
            "pt_ready pt_copied pv_ready o_copied stored out_free").split()}
        units = [(h, b) for h in range(4) for b in range(6)]
        NU = len(units)

        def window(b):
            lo, hi = max(0, b - 1), min(3, b + 1)
            return (lo, hi) if b < 4 else (0, -1)

        def width(b):
            lo, hi = window(b)
            return (hi - lo + 1) * CH

        with nc.Block() as block:
            @block.sync
            def _(sp):
                for dst, src in ((ident, "ident"), (blockones, "blockones"), (turn, "turn"), (cos, "cos"), (sin, "sin"), (mask, "window")):
                    sp.dma_start(dst[:], consts[src]).then_inc(S["const_in"], 16)
                sp.dma_start(sink[:], sinks).then_inc(S["const_in"], 16)
                sp.dma_start(gain[:], gains).then_inc(S["const_in"], 16)
                sp.sem_inc(S["out_free"], 1)
                with sp.Fori(0, 4) as g:
                    sp.wait_ge(S["pv_ready"], g * NU + 1)
                    sp.dma_start(x[:, 0:2], qkv[bass.ds(g * 256, 256), :].rearrange("(a p) t -> p a t", p=P)).then_inc(S["head_in"], 16)
                    for half in range(2):
                        sp.dma_start(x[64 * half:64 * half + 64, 2], qkv[bass.ds(g * 64 + 1024, 64), :]).then_inc(S["head_in"], 16)
                    sp.dma_start(v[:], qkv[bass.ds(g * 64 + 1280, 64), :]).then_inc(S["head_in"], 16)

            @block.vector
            def _(dve):
                dve.memset(eps[:], 1e-6)
                dve.wait_ge(S["const_in"], 128)
                with dve.Fori(0, 4) as g:
                    dve.wait_ge(S["head_in"], g * 64 + 64)
                    dve.tensor_copy(sink4[:], sink[:, bass.ds(g * 4, 4)])
                    dve.tensor_tensor(sq[:], x[:], x[:], ALU.mult)
                    dve.drain().then_inc(S["squares"], 1)
                    dve.wait_ge(S["rstd_done"], g + 1)
                    for k in range(3):
                        dve.scalar_tensor_tensor(x[:, k], x[:, k], gain[:, k // 2:k // 2 + 1], rstd[:, k], ALU.mult, ALU.mult)
                    dve.drain().then_inc(S["normed"], 1)
                    dve.wait_ge(S["turned"], g + 1)
                    turned = big[:].rearrange("p (k b) n -> p k b n", b=2)[:, 0:3, 0, :]
                    tab = lambda a: a[:].unsqueeze(1).to_broadcast([P, 3, LAT])
                    dve.tensor_tensor(sq[:, :, 0:LAT], turned, tab(sin), ALU.mult)
                    dve.tensor_tensor(x[:, :, 0:LAT], x[:, :, 0:LAT], tab(cos), ALU.mult)
                    dve.drain()
                    dve.tensor_tensor(x[:, :, 0:LAT], x[:, :, 0:LAT], sq[:, :, 0:LAT], ALU.add)
                    dve.drain().then_inc(S["roped"], 1)

                    def maxima(u):
                        h, b = units[u]
                        w, lo = width(b), window(b)[0]
                        st_u = st[:, u % 2]
                        dve.wait_ge(S["scores"], g * NU + (u + 1))
                        if u >= 2:
                            dve.wait_ge(S["den_done"], g * NU + (u - 1))
                        bank = 2 * (u % 2)
                        if w:
                            off = (lo - (b - 1)) * CH
                            dve.tensor_tensor(s[:, u % 2, 0:w], big[:, bank, 0:w], mask[:, off:off + w], ALU.add)
                            dve.drain()
                            dve.tensor_reduce(st_u[:, 0:1], s[:, u % 2, 0:w], AX, ALU.max)
                        dve.tensor_reduce(st_u[:, 1:2], big[:, bank + 1, 0:256], AX, ALU.max)
                        dve.drain()
                        if w:
                            dve.tensor_tensor(st_u[:, 1:2], st_u[:, 0:1], st_u[:, 1:2], ALU.max)
                            dve.drain()
                        dve.scalar_tensor_tensor(st_u[:, 1:2], st_u[:, 1:2], ATT_SCALE, sink4[:, h:h + 1], ALU.mult, ALU.max)
                        dve.drain()
                        dve.tensor_scalar(st_u[:, 2:3], st_u[:, 1:2], -1.0, None, ALU.mult)
                        dve.drain().then_inc(S["maxed"], 1)

                    def denominators(u):
                        st_u = st[:, u % 2]
                        dve.wait_ge(S["exped"], g * NU + (u + 1))
                        lo_col = 3 if width(units[u][1]) else 4
                        dve.tensor_reduce(st_u[:, 6:7], st_u[:, lo_col:6], AX, ALU.add)
                        dve.drain()
                        dve.reciprocal(st_u[:, 7:8], st_u[:, 6:7])
                        dve.drain().then_inc(S["den_done"], 1)

                    def transposed(u):
                        w = width(units[u][1]) + 256
                        dve.wait_ge(S["pt_ready"], g * NU + (u + 1))
                        dve.tensor_copy(pt_s[:, u % 2, 0:w], flat[:, 2048:2048 + w]).then_inc(S["pt_copied"], 1)

                    maxima(0)
                    for u in range(NU):
                        if u + 1 < NU:
                            maxima(u + 1)
                        denominators(u)
                        if u:
                            transposed(u - 1)
                    transposed(NU - 1)

            @block.scalar
            def _(act):
                act.sem_inc(S["o_copied"], 1)
                act.wait_ge(S["const_in"], 128)
                with act.Fori(0, 4) as g:
                    act.wait_ge(S["sums_ready"], g + 1)
                    act.activation(rstd[:], flat[:, 0:3072].rearrange("p (k n) -> p k n", k=3)[:, :, 0:TOK], ACT.Ln, scale=1.0 / HD, bias=eps[:])
                    act.drain()
                    act.activation(rstd[:], rstd[:], ACT.Exp, scale=-0.5)
                    act.drain().then_inc(S["rstd_done"], 1)
                    act.wait_ge(S["vt_ready"], g + 1)
                    act.copy(vt[:].rearrange("p c n -> p (c n)"), big[:, 6, 0:384]).then_inc(S["vt_copied"], 1)

                    def outputs(u):
                        h, b = units[u]
                        rows = slice(64 * (h % 2), 64 * (h % 2) + 64)
                        act.wait_ge(S["pv_ready"], g * NU + (u + 2))
                        if u == 0:
                            act.wait_ge(S["out_free"], g + 1)
                        act.copy(o[rows, h // 2, b * CH:(b + 1) * CH], big[rows, 6 + u % 2, 0:CH]).then_inc(S["o_copied"], 1)

                    for u in range(NU):
                        h, b = units[u]
                        w = width(b)
                        st_u, bank = st[:, u % 2], 2 * (u % 2)
                        act.wait_ge(S["maxed"], g * NU + (u + 1))
                        if u >= 2:
                            act.wait_ge(S["pt_ready"], g * NU + (u - 1))
                        if w:
                            act.activation(p[:, u % 2, 0:w], s[:, u % 2, 0:w], ACT.Exp, scale=ATT_SCALE, bias=st_u[:, 2:3], accum_out=st_u[:, 3:4])
                        act.activation(p[:, u % 2, w:w + 256], big[:, bank + 1, 0:256], ACT.Exp, scale=ATT_SCALE, bias=st_u[:, 2:3], accum_out=st_u[:, 4:5])
                        act.activation(st_u[:, 5:6], sink4[:, h:h + 1], ACT.Exp, bias=st_u[:, 2:3])
                        act.drain().then_inc(S["exped"], 1)
                        if u >= 2:
                            outputs(u - 2)
                    outputs(NU - 2)
                    outputs(NU - 1)

            @block.gpsimd
            def _(pool):
                with pool.Fori(0, 4) as g:
                    for u in range(NU):
                        w = width(units[u][1]) + 256
                        pool.wait_ge(S["den_done"], g * NU + (u + 1))
                        pool.tensor_tensor(p[:, u % 2, 0:w], p[:, u % 2, 0:w], st[:, u % 2, 7:8].to_broadcast([P, w]), ALU.mult).then_inc(S["scaled"], 1)
                    pool.wait_ge(S["o_copied"], g * NU + (NU + 1))
                    pool.dma_start(o_out[bass.ds(g * 256, 256), :].rearrange("(a p) t -> p a t", p=P), o[:]).then_inc(S["stored"], 16)
                    pool.wait_ge(S["stored"], g * 16 + 16)
                    pool.sem_inc(S["out_free"], 1)

            @block.tensor
            def _(pe):
                pe.sem_inc(S["pv_ready"], 1)
                pe.wait_ge(S["const_in"], 128)
                with pe.Fori(0, 4) as g:
                    pe.wait_ge(S["squares"], g + 1)
                    pe.wait_ge(S["o_copied"], g * NU + 1)
                    for k in range(3):
                        for a, b in ((0, LAT), (LAT, TOK)):
                            last = pe.matmul(flat[:, 1024 * k + a:1024 * k + b], blockones[:], sq[:, k, a:b], start=True, stop=True)
                    last.then_inc(S["sums_ready"], 1)
                    for c in range(6):
                        last = pe.transpose(big[:, 6, c * HD:(c + 1) * HD], v[:, c * CH:(c + 1) * CH], ident[0:HD, 0:HD])
                    last.then_inc(S["vt_ready"], 1)
                    pe.wait_ge(S["normed"], g + 1)
                    for k in range(3):
                        last = pe.matmul(big[:, 2 * k, :], turn[:], x[:, k, 0:LAT], start=True, stop=True)
                    last.then_inc(S["turned"], 1)
                    pe.wait_ge(S["roped"], g + 1)
                    pe.wait_ge(S["vt_copied"], g + 1)

                    def scores(u):
                        h, b = units[u]
                        half = slice(64 * (h % 2), 64 * (h % 2) + 64)
                        bank = 2 * (u % 2)
                        if u >= 2:
                            pe.wait_ge(S["exped"], g * NU + (u - 1))
                        q = x[half, h // 2, b * CH:(b + 1) * CH]
                        w, lo = width(b), window(b)[0]
                        if w:
                            pe.matmul(big[:, bank, 0:w], q, x[half, 2, lo * CH:lo * CH + w], start=True, stop=True)
                        pe.matmul(big[:, bank + 1, 0:256], q, x[half, 2, LAT:TOK], start=True, stop=True).then_inc(S["scores"], 1)

                    def transposes(u):
                        pe.wait_ge(S["scaled"], g * NU + (u + 1))
                        if u:
                            pe.wait_ge(S["pt_copied"], g * NU + u)
                        for k in range(width(units[u][1]) // CH + 2):
                            last = pe.transpose(flat[:, 2048 + k * CH:2048 + (k + 1) * CH], p[:, u % 2, k * CH:(k + 1) * CH], ident[:])
                        last.then_inc(S["pt_ready"], 1)

                    def values(u):
                        h, b = units[u]
                        lo, hi = window(b)
                        tiles = list(range(lo, hi + 1)) + [4, 5]
                        pe.wait_ge(S["pt_copied"], g * NU + (u + 1))
                        if u >= 2:
                            pe.wait_ge(S["o_copied"], g * NU + u)
                        out = big[64 * (h % 2):64 * (h % 2) + 64, 6 + u % 2, 0:CH]
                        for k, t in enumerate(tiles):
                            last = pe.matmul(out, vt[:, t], pt_s[:, u % 2, k * CH:(k + 1) * CH], start=(k == 0), stop=(k == len(tiles) - 1))
                        last.then_inc(S["pv_ready"], 1)

                    scores(0)
                    for u in range(NU):
                        if u + 1 < NU:
                            scores(u + 1)
                        transposes(u)
                        if u:
                            values(u - 1)
                    values(NU - 1)


def dense_glu(nc, name, w, conv, x_t, out_t, tokens, groups):
    k_tiles = KD
    span = 512 if tokens % 512 == 0 else tokens // 2
    spans = tokens // span
    padded = tokens + 2 + (tokens > LAT)
    out_w = padded - 2
    with Stage(nc) as ctx:
        def sb(n, shape):
            return ctx.enter_context(nc.sbuf_tensor(f"{name}_{n}", shape, F32))

        def sem(n):
            return ctx.sem(f"{name}_{n}")

        x = sb("x", [P, k_tiles, tokens])
        w_slot = [sb(f"w{s}", [P, k_tiles, 512]) for s in range(2)]
        cpar, cp = sb("cpar", [P, groups * 2, 4]), sb("cp", [P, 2, 4])
        gate, conved, sg = sb("gate", [P, 2, padded]), sb("conved", [P, 2, out_w]), sb("sg", [P, 2, out_w])
        stage = [sb(f"stage{s}", [P, 2, tokens]) for s in range(2)]
        acc = [ctx.enter_context(nc.psum_tensor(f"{name}_acc{b}", [P, spans, BANK], F32)) for b in range(2)]
        acc_v = [ctx.enter_context(nc.psum_tensor(f"{name}_accv{b}", [P, spans, BANK], F32)) for b in range(2)]
        x_loaded, pads = sem("x_loaded"), sem("pads")
        w_loaded = [sem(f"w_loaded{s}") for s in range(2)]
        gate_ready, value_ready, gate_done, conv_done, sig_done, value_done = (sem(n) for n in (
            "gate_ready", "value_ready", "gate_done", "conv_done", "sig_done", "value_done"))
        stored = [sem(f"stored{s}") for s in range(2)]
        stage_free = [sem(f"stage_free{s}") for s in range(2)]
        out_v = out_t.rearrange("(g c p) t -> g p c t", p=P, c=2)
        pairs, odd = groups // 2, groups % 2
        pieces = [(0, LAT, 0)] + ([(LAT, TOK, 1)] if tokens > LAT else [])

        def each(eng, step, first=0):
            with eng.Fori(first, pairs) as i:
                step(i * 2, 0, i)
                step(i * 2 + 1, 1, i)
            if odd:
                step(groups - 1, 0, pairs)

        with nc.Block() as block:
            @block.sync
            def _(sp):
                def load(g, s):
                    sp.dma_start(w_slot[s][:], w[bass.ds(g, 1)].rearrange("a p k n -> (a p) k n")).then_inc(w_loaded[s], 16)

                def reload(g, s, i):
                    sp.wait_ge(value_ready, g * 2 - 2)
                    load(g, s)

                sp.dma_start(x[:], x_t[:, 0:tokens].rearrange("(k p) t -> p k t", p=P)).then_inc(x_loaded, 16)
                sp.dma_start(cpar[:], conv).then_inc(x_loaded, 16)
                load(0, 0)
                load(1, 1)
                each(sp, reload, 1)

            @block.tensor
            def _(pe):
                pe.wait_ge(x_loaded, 32)

                def products(g, s, i):
                    pe.wait_ge(w_loaded[s], i * 16 + 16)
                    for c in range(2):
                        for bank, col, freed, ready in ((acc[c], 2 * c, gate_done, gate_ready), (acc_v[c], 2 * c + 1, value_done, value_ready)):
                            pe.wait_ge(freed, g * 2 + (c + 1))
                            for k in range(k_tiles):
                                for h in range(spans):
                                    last = pe.matmul(bank[:, h, 0:span], w_slot[s][:, k, col * P:(col + 1) * P],
                                                     x[:, k, h * span:(h + 1) * span], start=(k == 0), stop=(k == k_tiles - 1))
                            last.then_inc(ready, 1)
                each(pe, products)

            def copy_spans(act, c):
                for h in range(spans):
                    for a, b, o in pieces:
                        lo, hi = max(a, h * span), min(b, (h + 1) * span)
                        if lo < hi:
                            act.copy(gate[:, c, 1 + o + lo:1 + o + hi], acc[c][:, h, lo - h * span:hi - h * span])

            @block.scalar
            def _(act):
                act.wait_ge(pads, 1)
                act.sem_inc(gate_done, 2)

                def gates(g, s, i):
                    for c in range(2):
                        act.wait_ge(gate_ready, g * 2 + (c + 1))
                        act.wait_ge(conv_done, g * 2 + (c + 1))
                        copy_spans(act, c)
                        act.drain().then_inc(gate_done, 1)
                        act.wait_ge(conv_done, g * 2 + (c + 3))
                        act.activation(sg[:, c], conved[:, c], ACT.Sigmoid).then_inc(sig_done, 1)
                each(act, gates)

            @block.vector
            def _(dve):
                dve.memset(gate[:], 0.0)
                dve.drain().then_inc(pads, 1)
                dve.sem_inc(conv_done, 2)
                dve.sem_inc(value_done, 2)
                dve.wait_ge(x_loaded, 32)

                def values(g, s, i):
                    dve.tensor_copy(cp[:], cpar[:, bass.ds(g * 2, 2), :])
                    dve.drain()
                    for c in range(2):
                        dve.wait_ge(gate_done, g * 2 + (c + 3))
                        dve.tensor_scalar(conved[:, c], gate[:, c, 0:out_w], cp[:, c, 0:1], cp[:, c, 3:4], ALU.mult, ALU.add)
                        dve.drain()
                        dve.scalar_tensor_tensor(conved[:, c], gate[:, c, 1:1 + out_w], cp[:, c, 1:2], conved[:, c], ALU.mult, ALU.add)
                        dve.drain()
                        dve.scalar_tensor_tensor(conved[:, c], gate[:, c, 2:2 + out_w], cp[:, c, 2:3], conved[:, c], ALU.mult, ALU.add)
                        dve.drain().then_inc(conv_done, 1)
                        dve.wait_ge(sig_done, g * 2 + (c + 1))
                        dve.tensor_tensor(conved[:, c], conved[:, c], sg[:, c], ALU.mult)
                        dve.drain()
                        dve.wait_ge(value_ready, g * 2 + (c + 1))
                        if c == 0:
                            dve.wait_ge(stage_free[s], i + 1)
                        for h in range(spans):
                            for a, b, o in pieces:
                                lo, hi = max(a, h * span), min(b, (h + 1) * span)
                                if lo < hi:
                                    dve.tensor_tensor(stage[s][:, c, lo:hi], conved[:, c, lo + o:hi + o], acc_v[c][:, h, lo - h * span:hi - h * span], ALU.mult)
                        dve.drain().then_inc(value_done, 1)
                each(dve, values)

            @block.gpsimd
            def _(pool):
                def store(g, s, i):
                    pool.wait_ge(value_done, g * 2 + 4)
                    pool.dma_start(out_v[bass.ds(g, 1), :, :, 0:tokens].rearrange("a p c t -> (a p) c t"), stage[s][:]).then_inc(stored[s], 16)
                    pool.wait_ge(stored[s], i * 16 + 16)
                    pool.sem_inc(stage_free[s], 1)
                for s in range(2):
                    pool.sem_inc(stage_free[s], 1)
                each(pool, store)



HG = 8
F_T, I_T, Q_T, G_T = 0, 16, 24, 32
HALVES = (64, 32, 16, 8, 4, 2, 1)


def hgrn(nc, hp, lb_logits, gain, consts, out):
    with Stage(nc) as ctx:
        def sb(n, shape):
            return ctx.enter_context(nc.sbuf_tensor(f"hg_{n}", shape, F32))

        ident, ones, keep = sb("ident", [P, CH]), sb("ones", [P, CH]), sb("keep", [P, 6, CH + 1])
        masks = sb("masks", [P, 2, 8, CH])
        logits, lb, gains, eps, colh = sb("logits", [P, 2, HG]), sb("lb", [P, 2, HG]), sb("gains", [P, 1]), sb("eps", [P, 1]), sb("colh", [P, 2])
        q, f, v, gate = sb("q", [P, LAT]), sb("f", [P, 2, TOK]), sb("v", [P, TOK]), sb("gate", [P, LAT])
        sq, sgate = sb("sq", [P, LAT]), sb("sgate", [P, LAT])
        k = sb("k", [P, 2, TOK])
        g = sb("g", [P, 2, 6, CH + 1])
        run = sb("run", [P, 2, 6, CH + 1])
        rest = sb("rest", [P, 2, 6, CH + 1])
        ea, eb = sb("ea", [P, 2, 6, CH + 1]), sb("eb", [P, 2, 6, CH + 1])
        kd, qd = sb("kd", [P, 2, 6, CH]), sb("qd", [P, 2, 4, CH])
        lev = sb("lev", [P, 2, 7, LAT])
        vt, kt = sb("vt", [P, 6, CH]), sb("kt", [P, 2, 6, CH])
        state = sb("state", [P, 2, 6, CH])
        prod = sb("prod", [P, 16, CH])
        a = sb("a", [P, 4, CH])
        o, rstd = sb("o", [P, LAT]), sb("rstd", [P, LAT])
        big = ctx.enter_context(nc.psum_tensor("hg_big", [P, 8, 512], F32))
        S = {n: ctx.sem(f"hg_{n}") for n in (
            "const_in pads lb_done head_in sig_done f_done logs_done run_ready decays_done lev_right lev_left lev_exp lev_q lev_k kd_done "
            "tr_ready tr_copied pair_ready pair_done a_done st_ready st_done o_ready o_copied sum_ready rstd_done head_done stored").split()}
        ORDER = ([4, 5, 0, 1, 2, 3], [5, 4, 3, 2, 1, 0])

        def halves(ap, h, side):
            return ap.rearrange("p (b s n) -> p b s n", s=2, n=h)[:, :, side, :]

        with nc.Block() as block:
            @block.sync
            def _(sp):
                for dst, src in ((ident, consts["ident"]), (ones, consts["ones"]), (keep, consts["keep"]), (masks, consts["pairs"]), (logits, lb_logits), (gains, gain)):
                    sp.dma_start(dst[:], src).then_inc(S["const_in"], 16)
                tile = lambda row, n: hp[bass.ds(row, 1), :, 0:n].rearrange("a p t -> (a p) t")
                with sp.Fori(0, HG) as i:
                    sp.wait_ge(S["head_done"], i + 1)
                    for d in range(2):
                        sp.dma_start(f[:, d], tile(i + (F_T + 8 * d), TOK)).then_inc(S["head_in"], 16)
                    sp.dma_start(v[:], tile(i + I_T, TOK)).then_inc(S["head_in"], 16)
                    sp.dma_start(q[:], tile(i + Q_T, LAT)).then_inc(S["head_in"], 16)
                    sp.dma_start(gate[:], tile(i + G_T, LAT)).then_inc(S["head_in"], 16)
                    sp.wait_ge(S["head_done"], i + 2)
                    sp.dma_start(out[bass.ds(i, 1)].rearrange("a p t -> (a p) t"), o[:]).then_inc(S["stored"], 16)
                sp.wait_ge(S["stored"], 16 * HG)

            @block.scalar
            def _(act):
                act.wait_ge(S["pads"], 1)
                act.activation(lb[:, 0], lb[:, 1], ACT.Sigmoid)
                act.drain().then_inc(S["lb_done"], 1)
                with act.Fori(0, HG) as i:
                    act.wait_ge(S["head_in"], i * 80 + 80)
                    act.activation(f[:], f[:], ACT.Sigmoid)
                    act.activation(sq[:], q[:], ACT.Sigmoid)
                    act.activation(sgate[:], gate[:], ACT.Sigmoid)
                    act.drain().then_inc(S["sig_done"], 1)
                    act.wait_ge(S["f_done"], i + 1)
                    for d in range(2):
                        act.activation(g[:, d, 0:4, 1:], f[:, d, 0:LAT].rearrange("p (c n) -> p c n", n=CH), ACT.Ln)
                        act.activation(g[:, d, 4:6, 1:], f[:, d, LAT:TOK].rearrange("p (c n) -> p c n", n=CH), ACT.Ln)
                    act.drain().then_inc(S["logs_done"], 1)
                    act.wait_ge(S["run_ready"], i + 1)
                    act.activation(ea[:], run[:], ACT.Exp)
                    act.activation(eb[:], rest[:], ACT.Exp)
                    act.drain().then_inc(S["decays_done"], 1)
                    for n in range(14):
                        act.wait_ge(S["lev_right"], i * 14 + (n + 1))
                        act.wait_ge(S["lev_left"], i * 14 + (n + 1))
                        act.activation(lev[:, n // 7, n % 7], lev[:, n // 7, n % 7], ACT.Exp)
                        act.drain().then_inc(S["lev_exp"], 1)
                    for n in range(5):
                        act.wait_ge(S["tr_ready"], i * 5 + (n + 1))
                        bank = big[:, n % 2, :]
                        if n < 4:
                            dst = kt[:, n // 2, 3 * (n % 2):3 * (n % 2) + 3]
                            act.copy(dst.rearrange("p c n -> p (c n)"), bank[:, 0:384]).then_inc(S["tr_copied"], 1)
                        else:
                            act.copy(vt[:].rearrange("p (b c) n -> p b (c n)", b=2), big[:, 4:6, 0:384]).then_inc(S["tr_copied"], 1)
                    act.wait_ge(S["o_ready"], i + 1)
                    act.copy(o[:], big[:, 6, :])
                    act.drain()
                    act.activation(rstd[:], o[:], ACT.Square)
                    act.drain().then_inc(S["o_copied"], 1)
                    act.wait_ge(S["sum_ready"], i + 1)
                    act.activation(rstd[:], big[:, 7, :], ACT.Ln, scale=1.0 / P, bias=eps[:])
                    act.drain()
                    act.activation(rstd[:], rstd[:], ACT.Exp, scale=-0.5)
                    act.drain().then_inc(S["rstd_done"], 1)

            @block.vector
            def _(dve):
                dve.sem_inc(S["head_done"], 1)
                dve.memset(g[:], 0.0)
                dve.memset(eps[:], 1e-6)
                dve.memset(state[:], 0.0)
                dve.wait_ge(S["const_in"], 96)
                dve.tensor_tensor(lb[:, 1], logits[:, 1], logits[:, 0], ALU.subtract)
                dve.drain().then_inc(S["pads"], 1)
                dve.wait_ge(S["lb_done"], 1)
                dve.tensor_scalar(lb[:, 1], lb[:, 0], -1.0, 1.0, ALU.mult, ALU.add)
                dve.drain()
                with dve.Fori(0, HG) as i:
                    dve.tensor_copy(colh[:].unsqueeze(2), lb[:, :, bass.ds(i, 1)])
                    dve.drain()
                    dve.wait_ge(S["sig_done"], i + 1)
                    dve.tensor_scalar(f[:], f[:], colh[:, 1:2], colh[:, 0:1], ALU.mult, ALU.add)
                    dve.tensor_tensor(q[:], q[:], sq[:], ALU.mult)
                    dve.tensor_tensor(gate[:], gate[:], sgate[:], ALU.mult)
                    dve.drain().then_inc(S["f_done"], 1)
                    dve.tensor_scalar(k[:], f[:], -1.0, 1.0, ALU.mult, ALU.add)
                    dve.wait_ge(S["logs_done"], i + 1)
                    for d in range(2):
                        dve.tensor_tensor_scan(run[:, d].rearrange("p c n -> p (c n)"), keep[:].rearrange("p c n -> p (c n)"),
                                               g[:, d].rearrange("p c n -> p (c n)"), 0.0, ALU.mult, ALU.add)
                    dve.drain()
                    for d in range(2):
                        dve.tensor_tensor(rest[:, d], run[:, d, :, CH:].to_broadcast([P, 6, CH + 1]), run[:, d], ALU.subtract)
                    dve.drain().then_inc(S["run_ready"], 1)
                    for n in range(14):
                        d, h = n // 7, HALVES[n % 7]
                        for c in range(4):
                            mid = run[:, d, c, h:h + CH - h:2 * h].unsqueeze(2).to_broadcast([P, CH // (2 * h), h])
                            b = run[:, d, c, 1 - d:1 - d + CH]
                            right = halves(lev[:, d, n % 7, c * CH:(c + 1) * CH], h, 1)
                            dve.tensor_tensor(right, halves(b, h, 1), mid, ALU.subtract)
                        dve.drain().then_inc(S["lev_right"], 1)
                    for n in range(14):
                        d, h = n // 7, HALVES[n % 7]
                        src = q[:] if d == 0 else k[:, 1, 0:LAT]
                        right = halves(lev[:, d, n % 7], h, 1)
                        dve.wait_ge(S["lev_exp"], i * 14 + (n + 1))
                        dve.tensor_tensor(right, right, halves(src, h, 1), ALU.mult)
                        dve.drain().then_inc(S["lev_q"], 1)
                    dve.wait_ge(S["decays_done"], i + 1)
                    for d in range(2):
                        k_e = (eb[:, 0, :, 1:], ea[:, 1, :, 0:CH])[d]
                        q_e = (ea[:, 0, 0:4, 1:], eb[:, 1, 0:4, 0:CH])[d]
                        dve.tensor_tensor(kd[:, d], k[:, d].rearrange("p (c n) -> p c n", n=CH), k_e, ALU.mult)
                        dve.tensor_tensor(qd[:, d], q[:].rearrange("p (c n) -> p c n", n=CH), q_e, ALU.mult)
                    dve.drain().then_inc(S["kd_done"], 1)
                    for n in range(5):
                        dve.wait_ge(S["st_ready"], i * 5 + (n + 1))
                        for d in range(2):
                            c = ORDER[d][n]
                            dve.scalar_tensor_tensor(state[:, d, n + 1], state[:, d, n], ea[:, d, c, CH:], big[:, 2 + n % 2, d * CH:(d + 1) * CH], ALU.mult, ALU.add)
                        dve.drain().then_inc(S["st_done"], 1)
                    for c in range(4):
                        dve.wait_ge(S["pair_ready"], i * 4 + (c + 1))
                        dve.tensor_tensor(prod[:], big[:, 0:4, :].rearrange("p b (l n) -> p (b l) n", n=CH), masks[:].rearrange("p d l n -> p (d l) n"), ALU.mult)
                        dve.drain().then_inc(S["pair_done"], 1)
                        dve.tensor_reduce(a[:, c], prod[:].rearrange("p l n -> p n l"), AX, ALU.add)
                        dve.drain().then_inc(S["a_done"], 1)
                    dve.wait_ge(S["rstd_done"], i + 1)
                    dve.scalar_tensor_tensor(o[:], o[:], gains[:, 0:1], rstd[:], ALU.mult, ALU.mult)
                    dve.drain()
                    dve.tensor_tensor(o[:], o[:], gate[:], ALU.mult)
                    dve.drain().then_inc(S["head_done"], 1)

            @block.gpsimd
            def _(pool):
                with pool.Fori(0, HG) as i:
                    pool.wait_ge(S["run_ready"], i + 1)
                    for n in range(14):
                        d, h = n // 7, HALVES[n % 7]
                        for c in range(4):
                            mid = run[:, d, c, h:h + CH - h:2 * h].unsqueeze(2).to_broadcast([P, CH // (2 * h), h])
                            b = run[:, d, c, 1 - d:1 - d + CH]
                            left = halves(lev[:, d, n % 7, c * CH:(c + 1) * CH], h, 0)
                            pool.tensor_tensor(left, mid, halves(b, h, 0), ALU.subtract)
                        pool.drain().then_inc(S["lev_left"], 1)
                    for n in range(14):
                        d, h = n // 7, HALVES[n % 7]
                        src = k[:, 0, 0:LAT] if d == 0 else q[:]
                        left = halves(lev[:, d, n % 7], h, 0)
                        pool.wait_ge(S["lev_exp"], i * 14 + (n + 1))
                        pool.tensor_tensor(left, left, halves(src, h, 0), ALU.mult)
                        pool.drain().then_inc(S["lev_k"], 1)

            @block.tensor
            def _(pe):
                pe.wait_ge(S["const_in"], 96)
                with pe.Fori(0, HG) as i:
                    pe.wait_ge(S["head_done"], i + 1)
                    pe.wait_ge(S["kd_done"], i + 1)
                    for n in range(5):
                        if n >= 2:
                            pe.wait_ge(S["tr_copied"], i * 5 + (n - 1))
                        for c in range(3):
                            if n < 4:
                                last = pe.transpose(big[:, n % 2, c * CH:(c + 1) * CH], kd[:, n // 2, 3 * (n % 2) + c], ident[:])
                            else:
                                for b in range(2):
                                    last = pe.transpose(big[:, 4 + b, c * CH:(c + 1) * CH], v[:, (3 * b + c) * CH:(3 * b + c + 1) * CH], ident[:])
                        last.then_inc(S["tr_ready"], 1)
                    pe.wait_ge(S["tr_copied"], i * 5 + 5)
                    for n in range(5):
                        if n >= 2:
                            pe.wait_ge(S["st_done"], i * 5 + (n - 1))
                        for d in range(2):
                            c = ORDER[d][n]
                            last = pe.matmul(big[:, 2 + n % 2, d * CH:(d + 1) * CH], kt[:, d, c], vt[:, c], start=True, stop=True)
                        last.then_inc(S["st_ready"], 1)
                    pe.wait_ge(S["st_done"], i * 5 + 5)
                    pe.wait_ge(S["lev_q"], i * 14 + 14)
                    pe.wait_ge(S["lev_k"], i * 14 + 14)

                    def outputs(c):
                        pe.wait_ge(S["a_done"], i * 4 + (c + 1))
                        dst = big[:, 6, c * CH:(c + 1) * CH]
                        for d in range(2):
                            pe.matmul(dst, state[:, d, ORDER[d].index(c)], qd[:, d, c], start=(d == 0), stop=False)
                        last = pe.matmul(dst, vt[:, c], a[:, c], start=False, stop=True)
                        if c == 3:
                            last.then_inc(S["o_ready"], 1)

                    for c in range(4):
                        if c:
                            pe.wait_ge(S["pair_done"], i * 4 + c)
                        for d in range(2):
                            for l in range(8):
                                bank = big[:, 2 * d + l // 4, (l % 4) * CH:(l % 4 + 1) * CH]
                                if l < 7:
                                    x = lev[:, d, l, c * CH:(c + 1) * CH]
                                    last = pe.matmul(bank, x, x, start=True, stop=True)
                                else:
                                    last = pe.matmul(bank, k[:, d, c * CH:(c + 1) * CH], q[:, c * CH:(c + 1) * CH], start=True, stop=True)
                        last.then_inc(S["pair_ready"], 1)
                        if c:
                            outputs(c - 1)
                    outputs(3)
                    pe.wait_ge(S["o_copied"], i + 1)
                    pe.matmul(big[:, 7, :], ones[:], rstd[:], start=True, stop=True).then_inc(S["sum_ready"], 1)



def shape_constants():
    f=np.float32
    eye=np.eye(P,dtype=f)
    a,b=np.indices((P,P))
    strict=(a<b).astype(f); incl=(a<=b).astype(f)
    fwd=np.concatenate([strict,incl,strict,incl],1)
    bwd=np.concatenate([strict.T,incl.T,strict.T,incl.T],1)
    def level(k):
        blk,half=2<<k,1<<k
        return ((a//blk==b//blk)&(a%blk<half)&(b%blk>=half)).astype(f)
    lt=np.stack([np.stack([level(k),level(k).T],1) for k in range(7)],1)
    keep=np.ones((P,6,CH+1),f); keep[:,:,0]=0
    c={}
    c["ident"]=eye
    c["mask_g"]=np.stack([fwd,bwd],1)
    c["mask_l"]=np.stack([strict.T]*2+[strict]*2,1)
    c["level_t"]=lt
    c["blockones"]=(a//64==b//64).astype(f)
    c["keep"]=keep
    c["tri"]=np.stack([incl,incl.T],1)
    c["ones"]=np.ones((P,P),f)
    turn=np.zeros((P,P),f)
    for i in range(P):
        if i%32<16: turn[i+16,i]=-1
        else: turn[i-16,i]=1
    c["turn"]=turn
    dy=[level(k) for k in range(6,-1,-1)]
    c["pairs"]=np.stack([np.stack(dy+[eye],1),np.stack([m.T for m in dy]+[eye],1)],1)
    inv=(np.float32(10000.0)**(-np.arange(16,dtype=f)/np.float32(16))).astype(f)
    t=np.arange(512)
    pos=np.where((np.arange(P)[:,None]%64)<32,(t//64)[None],(t%64)[None]).astype(f)
    ang=pos*inv[np.arange(P)%16][:,None]
    c["cos"],c["sin"]=np.cos(ang),np.sin(ang)
    q,k=np.indices((P,3*CH)); k=k-CH
    c["window"]=np.where(np.abs(q-k)<=CH,0.0,-1e30)
    c["slots"]=np.broadcast_to(np.arange(1,65,dtype=f),(P,64))
    return {k:np.ascontiguousarray(v,f) for k,v in c.items()}



SHIFT1, SCALE1, GATE1, SHIFT2, SCALE2, GATE2 = (KD * n for n in range(6))
FF = 2816


def program(nc, a, out):
    def scratch(name, shape):
        return nc.dram_tensor(name, shape, F32).ap()

    def rows(t, tokens):
        return t[:, 0:tokens].rearrange("(k p) t -> p k t", p=P)

    def tiles(t, tokens, cols=4):
        return t[:, 0:tokens].rearrange("(g c p) t -> g p c t", p=P, c=cols)

    cond = scratch("cond", [P, 32])
    mod1, mod2 = scratch("mod1", [P, 96]), scratch("mod2", [P, 192])
    h = scratch("h", [D, TOK])
    pt = scratch("pt", [84, P, TOK])
    ya, yb_raw, yb = scratch("ya", [KD, P, LAT]), scratch("yb_raw", [16, P, LAT]), scratch("yb", [16, P, LAT])
    pa, pb, merged, ml = (scratch(n, [D, LAT]) for n in ("pa", "pb", "merged", "ml"))
    x1, moe = scratch("x1", [D, LAT]), scratch("moe", [D, LAT])
    xe, sel = scratch("xe", [KD, P, N_EXP * CAP]), scratch("sel", [KD, P, LAT])
    x2, x3, x4, x5 = (scratch(n, [D, TOK]) for n in ("x2", "x3", "x4", "x5"))
    qkv, att, y = scratch("qkv", [1536, TOK]), scratch("att", [D, TOK]), scratch("y", [D, TOK])
    hp, hg = scratch("hp", [40, P, TOK]), scratch("hg", [KD, P, LAT])
    ff = scratch("ff", [FF, TOK])

    silu_columns(nc, "sc", a["cond"], cond)
    by_stream = lambda m: m.rearrange("p (g c s) -> g p c s", c=4, s=2)
    dense(nc, "ada1", a["ada_w"], cond[:, 0:16].rearrange("p (k s) -> p k s", s=2), by_stream(mod1), KD, 2, 12, 512)
    dense(nc, "ada2", a["ada_w_2"], cond[:, 16:32].rearrange("p (k s) -> p k s", s=2), by_stream(mod2), KD, 2, 24, 512)
    m1 = (mod1, a["ada_b"])
    m2 = [(mod2[:, 96 * n:96 * n + 96], a["ada_b_2"][:, 48 * n:48 * n + 48]) for n in range(2)]

    norm_step(nc, "n1", [(a["x"], 0, LAT), (a["ctx"], LAT, TOK)], None, h, a, TOK, h_mod=m1, shift=SHIFT1, scale=SCALE1, gain=a["norm1_pre"])
    pt_v = pt.rearrange("(g c) p t -> g p c t", c=4)
    dense(nc, "in_both", a["w_in_both"], rows(h, TOK), pt_v[0:11], KD, TOK, 11, 512)
    dense(nc, "in_lat", a["w_in_lat"], rows(h, LAT), pt_v[11:21, :, :, 0:LAT], KD, LAT, 10, 512)
    rwkv(nc, pt, (a["rw_w2"], a["rw_a2"], a["rw_g2"]), a["rw_params"], a["rw_edges"], a, ya)
    ssm(nc, pt, a["dt_bias"], a["a_log"], a["d_skip"], a["ssm_params"], a, yb_raw)
    branch_norm(nc, yb_raw, a["ssm_norm"], a, yb)
    dense(nc, "proj_a", a["proj_a"], ya.rearrange("k p t -> p k t"), tiles(pa, LAT), KD, LAT, 2, 512)
    dense(nc, "proj_b", a["proj_b"], yb.rearrange("k p t -> p k t"), tiles(pb, LAT), 16, LAT, 2, 512)
    gated_sum(nc, pt[GATE_T:GATE_T + 16], pa, pb, merged)
    dense(nc, "w_out", a["w_out"], rows(merged, LAT), tiles(ml, LAT), KD, LAT, 2, 512)
    norm_step(nc, "n2", [(a["x"], 0, LAT)], x1, h, a, LAT, gate_mod=m1, h_mod=m1, shift=SHIFT2, scale=SCALE2, gain=a["norm2_pre"],
              delta=ml, delta_tokens=LAT, gate=GATE1, post=a["norm1_post"])
    route(nc, h, a["router"], a, xe, sel)
    experts(nc, xe, sel, a["exp_w1"], a["exp_w3"], a["exp_w2"], moe)
    norm_step(nc, "n3", [(x1, 0, LAT), (a["ctx_2"], LAT, TOK)], x2, h, a, TOK, gate_mod=m1, h_mod=m2[0], shift=SHIFT1, scale=SCALE1,
              gain=a["norm1_g_2"][:, 0:KD], delta=moe, delta_tokens=LAT, gate=GATE2, post=a["norm2_post"])

    dense(nc, "att_in", a["attn_w_in"], rows(h, TOK), tiles(qkv, TOK), KD, TOK, 3, 512)
    attention(nc, qkv, a["attn_sink"], a["attn_gains"], a, att)
    dense(nc, "att_out", a["attn_w_out"], rows(att, TOK), tiles(y, TOK), KD, TOK, 2, 512)
    norm_step(nc, "n4", [(x2, 0, TOK)], x3, h, a, TOK, gate_mod=m2[0], h_mod=m2[0], shift=SHIFT2, scale=SCALE2,
              gain=a["norm2_g_2"][:, 0:KD], delta=y, delta_tokens=TOK, gate=GATE1)
    dense_glu(nc, "up0", a["ffn_w_up_0"], a["ffn_conv_0"], h, ff, TOK, 11)
    dense(nc, "down0", a["ffn_w_down_0"], rows(ff, TOK), tiles(y, TOK, 2), 22, TOK, 4, 256)
    norm_step(nc, "n5", [(x3, 0, TOK)], x4, h, a, TOK, gate_mod=m2[0], h_mod=m2[1], shift=SHIFT1, scale=SCALE1,
              gain=a["norm1_g_2"][:, KD:2 * KD], delta=y, delta_tokens=TOK, gate=GATE2)
    hp_v = hp.rearrange("(g c) p t -> g p c t", c=4)
    dense(nc, "hg_both", a["hgrn_w_both"], rows(h, TOK), hp_v[0:6], KD, TOK, 6, 512)
    dense(nc, "hg_lat", a["hgrn_w_lat"], rows(h, LAT), hp_v[6:10, :, :, 0:LAT], KD, LAT, 4, 512)
    hgrn(nc, hp, a["lb_logits"], a["hgrn_gain"], a, hg)
    dense(nc, "hg_out", a["hgrn_w_out"], hg.rearrange("k p t -> p k t"), tiles(y, LAT), KD, LAT, 2, 512)
    norm_step(nc, "n6", [(x4[:, 0:LAT], 0, LAT)], x5, h, a, LAT, gate_mod=m2[1], h_mod=m2[1], shift=SHIFT2, scale=SCALE2,
              gain=a["norm2_g_2"][:, KD:2 * KD], delta=y, delta_tokens=LAT, gate=GATE1)
    dense_glu(nc, "up1", a["ffn_w_up_1"], a["ffn_conv_1"], h, ff, LAT, 11)
    dense(nc, "down1", a["ffn_w_down_1"], rows(ff, LAT), tiles(y, LAT, 2), 22, LAT, 4, 256)
    norm_step(nc, "n7", [(x5[:, 0:LAT], 0, LAT)], out, None, a, LAT, gate_mod=m2[1], delta=y, delta_tokens=LAT, gate=GATE2)



def layouts(i):
    def cols(v):
        return v.reshape(-1, P).T

    def tiled(w, width=512):
        k, n = w.shape
        return w.reshape(k // P, P, n // width, width).transpose(2, 1, 0, 3)

    def expert_tiled(w):
        e, k, n = w.shape
        return w.reshape(e, k // P, P, n // 512, 512).transpose(0, 3, 2, 1, 4)

    def both(u, v):
        return np.stack([cols(u.reshape(-1)), cols(v.reshape(-1))], axis=2).reshape(P, 2 * KD)

    def spread(v):
        return np.broadcast_to(v.reshape(1, -1), (P, v.size))

    a = dict(shape_constants())
    a["x"], a["ctx"], a["ctx_2"] = i["x"][0].T, i["ctx"][0].T, i["ctx_2"][0].T
    a["cond"] = np.concatenate([both(i["c"], i["c_ctx"]), both(i["c_2"], i["c_ctx_2"])], axis=1)
    a["ada_w"], a["ada_b"] = tiled(i["ada_w"][0]), cols(i["ada_b"][0])
    a["ada_w_2"] = np.concatenate([tiled(i["ada_w_2"][0]), tiled(i["ada_w_2"][1])], axis=0)
    a["ada_b_2"] = cols(i["ada_b_2"])
    for n in ("norm1_pre", "norm1_post", "norm2_pre", "norm2_post", "ssm_norm"):
        a[n] = cols(i[n][0])
    a["norm1_g_2"], a["norm2_g_2"] = cols(i["norm1_g_2"]), cols(i["norm2_g_2"])

    w = i["w_in"][0]
    rw = 3 * D
    s0 = rw + 3 * P
    part = lambda first, n: w[:, first:first + n]
    pad = np.zeros((D, 64), w.dtype)
    a["w_in_both"] = tiled(np.concatenate([part(D, 2 * D), part(rw, 2 * P), part(s0 + 2 * D, 3 * D), part(s0 + 5 * D, 64), pad, part(0, P)], axis=1))
    a["w_in_lat"] = tiled(np.concatenate([part(P, D - P), part(rw + 2 * P, P), part(s0, 2 * D), part(s0 + 5 * D + 64, 2 * D)], axis=1))

    mu = i["rw_mu"][0]
    per_tile = [mu[0, 0:D], mu[1, 0:D], mu[0, D:2 * D], mu[1, D:2 * D], mu[0, 2 * D:rw], mu[1, 2 * D:rw],
                i["rw_w0"][0, 0], i["rw_w0"][0, 1], i["rw_a0"][0, 0], i["rw_a0"][0, 1],
                i["rw_kk"][0], i["rw_ka"][0], i["rw_rk"][0].reshape(-1), i["rw_ln_w"][0], i["rw_ln_b"][0], i["rw_ln_b"][0]]
    a["rw_params"] = np.stack(per_tile, axis=1).reshape(KD, P, 16)
    edges = mu[:, rw:rw + 3 * P].reshape(2, 3, P).transpose(2, 1, 0).reshape(P, 6)
    a["rw_edges"] = np.concatenate([edges, edges[:, 0:2]], axis=1)
    a["rw_w2"], a["rw_a2"], a["rw_g2"] = i["rw_w2"][0].reshape(P, D), i["rw_a2"][0].reshape(P, D), i["rw_g2"][0]

    a["dt_bias"] = i["ssm_dt_bias"][0].reshape(64, 1)
    a["a_log"], a["d_skip"] = spread(i["ssm_a_log"][0]), spread(i["ssm_d"][0])
    taps = np.concatenate([i["ssm_conv_w"][0], i["ssm_conv_b"][0][:, None], i["ssm_conv_w"][0][:, 0:2]], axis=1).reshape(24, P, 8)
    a["ssm_params"] = np.stack([np.concatenate([taps[4 * g:4 * g + 4], taps[16 + g:17 + g], taps[20 + g:21 + g]], axis=0).transpose(1, 0, 2) for g in range(4)])
    a["proj_a"], a["proj_b"], a["w_out"] = tiled(i["proj_a"][0]), tiled(i["proj_b"][0]), tiled(i["w_out"][0])
    a["router"] = i["router"][0]
    for n in ("exp_w1", "exp_w3", "exp_w2"):
        a[n] = expert_tiled(i[n][0])

    a["attn_w_in"], a["attn_w_out"] = tiled(i["attn_w_in_2"][0]), tiled(i["attn_w_out_2"][0])
    a["attn_sink"] = spread(i["attn_sink_2"][0])
    a["attn_gains"] = np.stack([np.concatenate([i[n][0]] * 2) for n in ("attn_q_gain_2", "attn_k_gain_2")], axis=1)
    w = i["hgrn_w_in_2"][0]
    a["hgrn_w_both"] = tiled(w[:, D:4 * D])
    a["hgrn_w_lat"] = tiled(np.concatenate([w[:, 0:D], w[:, 4 * D:5 * D]], axis=1))
    a["hgrn_w_out"] = tiled(i["hgrn_w_out_2"][0])
    a["hgrn_gain"] = i["hgrn_o_gain_2"][0].reshape(P, 1)
    a["lb_logits"] = i["hgrn_lb_logits_2"].reshape(2, HG, P).transpose(2, 0, 1)
    for n in range(2):
        up = i["ffn_w_up_2"][n].reshape(D, 2, FF // 256, 2, P)
        a[f"ffn_w_up_{n}"] = up.transpose(2, 0, 3, 1, 4).reshape(FF // 256, KD, P, 512).transpose(0, 2, 1, 3)
        a[f"ffn_conv_{n}"] = np.concatenate([i["ffn_conv_w_2"][n], i["ffn_conv_b_2"][n][None]], axis=0).reshape(4, FF // P, P).transpose(2, 1, 0)
        a[f"ffn_w_down_{n}"] = tiled(i["ffn_w_down_2"][n], 256)
    return {k: np.ascontiguousarray(v) for k, v in a.items()}


def kernel(**inputs):
    import concourse.bacc as bacc
    from concourse.bass_utils import run_bass_kernel_spmd

    arrays = layouts({k: np.asarray(v) for k, v in inputs.items()})
    nc = bacc.Bacc("TRN2", target_bir_lowering=False, num_devices=1)
    aps = {n: nc.dram_tensor(f"in_{n}", v.shape, mybir.dt.from_np(v.dtype), kind="ExternalInput").ap() for n, v in arrays.items()}
    out = nc.dram_tensor("out_x", (D, LAT), F32, kind="ExternalOutput").ap()
    program(nc, aps, out)
    r = run_bass_kernel_spmd(nc, [{f"in_{n}": v for n, v in arrays.items()}], core_ids=[0])
    return r.results[0]["out_x"].T.reshape(1, LAT, D)
```

```python
from contextlib import ExitStack

import numpy as np
import concourse.bass as bass
from concourse import mybir

F32 = mybir.dt.float32
F32R = mybir.dt.float32r
ALU = mybir.AluOpType
ACT = mybir.ActivationFunctionType
AX = mybir.AxisListType.X

P = 128
BANK = 512


class Stage(ExitStack):

    def __init__(self, nc):
        super().__init__()
        self.nc, self.sems = nc, []

    def sem(self, name):
        self.sems.append(self.nc.alloc_semaphore(name))
        return self.sems[-1]

    def close_stage(self):
        self.nc.clear_and_free_semaphores(self.sems)
        self.nc.all_engine_barrier()

    def __exit__(self, *exc):
        done = super().__exit__(*exc)
        if exc[0] is None:
            self.close_stage()
        return done


def dense(nc, name, w, x_v, out_v, k_tiles, tokens, groups, width):
    span = tokens if tokens <= BANK else tokens // 2
    spans = tokens // span
    cols = width // P
    half = cols // 2
    with Stage(nc) as ctx:
        sb = lambda n, shape: ctx.enter_context(nc.sbuf_tensor(f"{name}_{n}", shape, F32))
        sem = lambda n: ctx.sem(f"{name}_{n}")
        x = sb("x", [P, k_tiles, tokens])
        w_slot = [sb(f"w{s}", [P, k_tiles, width]) for s in range(2)]
        stage = [sb(f"stage{s}", [P, cols, tokens]) for s in range(2)]
        acc = [ctx.enter_context(nc.psum_tensor(f"{name}_acc{b}", [P, spans, BANK], F32)) for b in range(2)]
        x_loaded = sem("x_loaded")
        w_loaded = [sem(f"w_loaded{s}") for s in range(2)]
        acc_ready = sem("acc_ready")
        evacuated = [sem(f"evacuated{b}") for b in range(2)]
        stored = [sem(f"stored{s}") for s in range(2)]
        stage_free = [sem(f"stage_free{s}") for s in range(2)]
        pairs, odd = groups // 2, groups % 2

        def each(eng, step, first=0):
            if pairs > first:
                with eng.Fori(first, pairs) as i:
                    step(i * 2, 0, i)
                    step(i * 2 + 1, 1, i)
            if odd:
                step(groups - 1, 0, pairs)

        with nc.Block() as block:
            @block.sync
            def _(sp):
                def load(g, s):
                    sp.dma_start(w_slot[s][:], w[bass.ds(g, 1)].rearrange("a p k n -> (a p) k n")).then_inc(w_loaded[s], 16)

                def reload(g, s, i):
                    sp.wait_ge(acc_ready, (g - 1) * cols)
                    load(g, s)

                sp.dma_start(x[:], x_v[:, :, 0:tokens]).then_inc(x_loaded, 16)
                load(0, 0)
                load(1, 1)
                each(sp, reload, 1)

            @block.tensor
            def _(pe):
                pe.wait_ge(x_loaded, 16)

                def products(g, s, i):
                    pe.wait_ge(w_loaded[s], i * 16 + 16)
                    for c in range(cols):
                        b = c % 2
                        pe.wait_ge(evacuated[b], g * half + (c // 2 + 1))
                        for k in range(k_tiles):
                            for h in range(spans):
                                last = pe.matmul(acc[b][:, h, 0:span], w_slot[s][:, k, c * P:(c + 1) * P],
                                                 x[:, k, h * span:(h + 1) * span], start=(k == 0), stop=(k == k_tiles - 1))
                        last.then_inc(acc_ready, 1)
                each(pe, products)

            def copies(eng, copy, b):
                def copy_out(g, s, i):
                    eng.wait_ge(stage_free[s], i + 1)
                    for c in range(b, cols, 2):
                        eng.wait_ge(acc_ready, g * cols + (c + 1))
                        copy(stage[s][:, c, :].rearrange("p (h n) -> p h n", h=spans), acc[b][:, :, 0:span]).then_inc(evacuated[b], 1)
                eng.sem_inc(evacuated[b], 1)
                each(eng, copy_out)

            @block.scalar
            def _(act):
                copies(act, act.copy, 0)

            @block.vector
            def _(dve):
                copies(dve, dve.tensor_copy, 1)

            @block.gpsimd
            def _(pool):
                def store(g, s, i):
                    for b in range(2):
                        pool.wait_ge(evacuated[b], g * half + (half + 1))
                    pool.dma_start(out_v[bass.ds(g, 1), :, :, 0:tokens].rearrange("a p c t -> (a p) c t"), stage[s][:]).then_inc(stored[s], 16)
                    pool.wait_ge(stored[s], i * 16 + 16)
                    pool.sem_inc(stage_free[s], 1)
                for s in range(2):
                    pool.sem_inc(stage_free[s], 1)
                each(pool, store)


def each_group(eng, groups, step):
    rounds = (groups - 1) // 2
    if rounds:
        with eng.Fori(0, rounds) as i:
            step(i * 2, 0, i, True)
            step(i * 2 + 1, 1, i, True)
    for g in range(2 * rounds, groups):
        step(g, g % 2, g // 2, g + 1 < groups)


class SplitOperands:

    CHUNKS = 4

    def __init__(self, ctx, name, w, x_v, k_tiles, tokens, groups, width):
        nc = ctx.nc
        sb = lambda n, shape, dt: ctx.enter_context(nc.sbuf_tensor(f"{name}_{n}", shape, dt))
        self.w, self.x_v, self.k_tiles, self.tokens, self.groups = w, x_v, k_tiles, tokens, groups
        self.x_hi, self.x_lo = (sb(n, [P, k_tiles, tokens], F32R) for n in ("x_hi", "x_lo"))
        self.w_raw = [sb(f"w_raw{s}", [P, k_tiles, width], F32) for s in range(2)]
        self.w_hi = [sb(f"w_hi{s}", [P, k_tiles, width], F32R) for s in range(2)]
        self.w_lo = [sb(f"w_lo{s}", [P, k_tiles, width], F32R) for s in range(2)]
        self.x_loaded = [ctx.sem(f"{name}_x_loaded{c}") for c in range(self.CHUNKS)]
        self.w_loaded = [ctx.sem(f"{name}_w_loaded{s}") for s in range(2)]
        self.x_hi_done, self.x_ready, self.w_hi_done, self.w_ready = (ctx.sem(f"{name}_{n}") for n in ("x_hi_done", "x_ready", "w_hi_done", "w_ready"))

    def chunk(self, c):
        n = self.k_tiles // self.CHUNKS
        return slice(c * n, (c + 1) * n)

    def load_w(self, sp, g, s):
        sp.dma_start(self.w_raw[s][:], self.w[bass.ds(g, 1)].rearrange("a p k n -> (a p) k n")).then_inc(self.w_loaded[s], 16)

    def load(self, sp):
        self.load_w(sp, 0, 0)
        for c in range(self.CHUNKS):
            k = self.chunk(c)
            sp.dma_start(self.x_lo[:, k].bitcast(F32), self.x_v[:, k, 0:self.tokens]).then_inc(self.x_loaded[c], 16)
        self.load_w(sp, 1, 1)

    def reload(self, sp):
        def step(g, s):
            sp.wait_ge(self.w_ready, g - 1)
            self.load_w(sp, g, s)
        rest = self.groups - 2
        if rest >= 2:
            with sp.Fori(1, 1 + rest // 2) as i:
                step(i * 2, 0)
                step(i * 2 + 1, 1)
        if rest % 2:
            step(self.groups - 1, 0)

    def x_hi_parts(self, act):
        for c in range(self.CHUNKS):
            k = self.chunk(c)
            act.wait_ge(self.x_loaded[c], 16)
            act.copy(self.x_hi[:, k], self.x_lo[:, k].bitcast(F32)).then_inc(self.x_hi_done, 1)

    def x_lo_parts(self, dve):
        for c in range(self.CHUNKS):
            k = self.chunk(c)
            dve.wait_ge(self.x_hi_done, c + 1)
            dve.tensor_tensor(self.x_lo[:, k], self.x_lo[:, k].bitcast(F32), self.x_hi[:, k].bitcast(F32), ALU.subtract).then_inc(self.x_ready, 1)

    def w_hi_part(self, act, s, i):
        act.wait_ge(self.w_loaded[s], i * 16 + 16)
        act.copy(self.w_hi[s][:], self.w_raw[s][:]).then_inc(self.w_hi_done, 1)

    def w_lo_part(self, dve, g, s):
        dve.wait_ge(self.w_hi_done, g + 1)
        dve.tensor_tensor(self.w_lo[s][:], self.w_raw[s][:], self.w_hi[s][:].bitcast(F32), ALU.subtract).then_inc(self.w_ready, 1)

    def products(self, pe, bank, s, col, span, spans):
        cols = slice(col * P, (col + 1) * P)
        for k in range(self.k_tiles):
            hi, lo = self.w_hi[s][:, k, cols], self.w_lo[s][:, k, cols]
            for part, xs in ((hi, self.x_hi), (hi, self.x_lo), (lo, self.x_hi)):
                for h in range(spans):
                    last = pe.matmul(bank[:, h, 0:span], part, xs[:, k, h * span:(h + 1) * span],
                                     start=(k == 0 and xs is self.x_hi and part is hi), stop=(k == self.k_tiles - 1 and part is lo))
        return last


def dense_split(nc, name, w, x_v, out_v, k_tiles, tokens, groups, width):
    span = tokens if tokens <= BANK else tokens // 2
    spans = tokens // span
    cols = width // P
    half = cols // 2
    with Stage(nc) as ctx:
        ops = SplitOperands(ctx, name, w, x_v, k_tiles, tokens, groups, width)
        stage = [ctx.enter_context(nc.sbuf_tensor(f"{name}_stage{s}", [P, cols, tokens], F32)) for s in range(2)]
        acc = [ctx.enter_context(nc.psum_tensor(f"{name}_acc{b}", [P, spans, BANK], F32)) for b in range(2)]
        acc_ready = ctx.sem(f"{name}_acc_ready")
        evacuated = [ctx.sem(f"{name}_evacuated{b}") for b in range(2)]
        stored = [ctx.sem(f"{name}_stored{s}") for s in range(2)]
        stage_free = [ctx.sem(f"{name}_stage_free{s}") for s in range(2)]

        with nc.Block() as block:
            @block.sync
            def _(sp):
                ops.load(sp)
                ops.reload(sp)

            @block.tensor
            def _(pe):
                pe.sem_inc(acc_ready, cols)
                pe.wait_ge(ops.x_ready, ops.CHUNKS)

                def products(g, s, i, more):
                    pe.wait_ge(ops.w_ready, g + 1)
                    for c in range(cols):
                        pe.wait_ge(evacuated[c % 2], g * half + (c // 2 + 1))
                        ops.products(pe, acc[c % 2], s, c, span, spans).then_inc(acc_ready, 1)
                each_group(pe, groups, products)

            def copy_out(eng, copy, b, g, s, i):
                eng.wait_ge(stage_free[s], i + 1)
                for c in range(b, cols, 2):
                    eng.wait_ge(acc_ready, g * cols + (cols + c + 1))
                    copy(stage[s][:, c, :].rearrange("p (h n) -> p h n", h=spans), acc[b][:, :, 0:span]).then_inc(evacuated[b], 1)

            @block.scalar
            def _(act):
                act.sem_inc(evacuated[0], 1)
                ops.w_hi_part(act, 0, 0)
                ops.x_hi_parts(act)

                def step(g, s, i, more):
                    if more:
                        act.wait_ge(acc_ready, g * cols + cols)
                        ops.w_hi_part(act, 1 - s, i + s)
                    copy_out(act, act.copy, 0, g, s, i)
                each_group(act, groups, step)

            @block.vector
            def _(dve):
                dve.sem_inc(evacuated[1], 1)
                ops.w_lo_part(dve, 0, 0)
                ops.x_lo_parts(dve)

                def step(g, s, i, more):
                    if more:
                        ops.w_lo_part(dve, g + 1, 1 - s)
                    copy_out(dve, dve.tensor_copy, 1, g, s, i)
                each_group(dve, groups, step)

            @block.gpsimd
            def _(pool):
                def store(g, s, i, more):
                    for b in range(2):
                        pool.wait_ge(evacuated[b], g * half + (half + 1))
                    pool.dma_start(out_v[bass.ds(g, 1), :, :, 0:tokens].rearrange("a p c t -> (a p) c t"), stage[s][:]).then_inc(stored[s], 16)
                    pool.wait_ge(stored[s], i * 16 + 16)
                    pool.sem_inc(stage_free[s], 1)
                for s in range(2):
                    pool.sem_inc(stage_free[s], 1)
                each_group(pool, groups, store)



D = 1024
LAT, CTX = 512, 256
TOK = LAT + CTX
CH = 128
SHIFTED = LAT + 1 + CTX
PADDED = SHIFTED + 2
C_DECAY = float(np.exp(-0.5))
K_T, V_T, XW_T, XA_T, XBC_T, DT_T, R_T, XG_T, Z_T, GATE_T = 0, 8, 16, 17, 18, 42, 43, 51, 52, 68


def rwkv(nc, pt, loras, params, edges, consts, ya):
    w2, a2, g2 = loras
    with Stage(nc) as ctx:
        def sb(n, shape):
            return ctx.enter_context(nc.sbuf_tensor(f"rw_{n}", shape, F32))

        def sem(n):
            return ctx.sem(f"rw_{n}")

        raw = sb("raw", [P, 3, PADDED])
        small = sb("small", [P, 3, SHIFTED])
        lora_w = sb("lora_w", [P, 3, P])
        par = sb("par", [P, 16])
        edge = sb("edge", [P, 8])
        col = sb("col", [P, 8])
        ident = sb("ident", [P, CH])
        mask_g = sb("mask_g", [P, 2, 512])
        mask_l = sb("mask_l", [P, 4, CH])
        level_t = sb("level_t", [P, 7, 2, CH])
        blockones = sb("blockones", [P, CH])
        keep = sb("keep", [P, 6, CH + 1])
        tiny = sb("tiny", [P, 3])
        rkv = sb("rkv", [P, 3, SHIFTED])
        kk = sb("kk", [P, SHIFTED])
        sq = sb("sq", [P, SHIFTED])
        bkt = sb("bkt", [P, 6, 4, CH])
        sig = sb("sig", [P, 2, 6, CH + 1])
        aa = sb("aa", [P, 2, SHIFTED])
        run = sb("run", [P, 2, 6, CH + 1])
        up = sb("up", [P, 2, 6, CH + 1])
        down = sb("down", [P, 2, 6, CH + 1])
        keff = sb("keff", [P, 2, SHIFTED])
        rstd = sb("rstd", [P, SHIFTED])
        ar_lat = [sb(f"ar_lat{h}", [P, 2, 4, 2, CH]) for h in range(2)]
        ar_con = [sb(f"ar_con{h}", [P, 2, 2, CH]) for h in range(2)]
        bm = sb("bm", [P, 2, 6, CH])
        km = sb("km", [P, 2, 6, CH])
        mg_lat, mg_con = sb("mg_lat", [P, 4, 4, 512]), sb("mg_con", [P, 2, 4, 2, CH])
        xs = sb("xs", [P, 6, 4, CH])
        xt = sb("xt", [P, 6, 4, CH])
        flat_of = lambda t, pat, n: t[:].rearrange(pat)[:, 0:n].rearrange("p (a j n) -> p a j n", j=4, n=CH)
        lo = flat_of(aa, "p d n -> p (d n)", 2 * 4 * CH)
        t1 = flat_of(run, "p d c n -> p (d c n)", 2 * 4 * CH)
        ltm = flat_of(up, "p d c n -> p (d c n)", 2 * 4 * CH)
        ys = down[:].rearrange("p d c n -> p (d c n)")[:, 0:2 * LAT].rearrange("p (d n) -> p d n", d=2)
        vt = sb("vt", [P, 6, CH])
        fac = sb("fac", [P, 2, 6])
        st = sb("st", [P, 2, 2, 64])
        sf = sb("sf", [P, 2, 64])
        rhs = sb("rhs", [P, 2, 2, 64])
        sas = sb("sas", [P, 4, 64])
        gs = sb("gs", [P, LAT])
        outp = keff[:, 1, 0:LAT]
        big = ctx.enter_context(nc.psum_tensor("rw_big", [P, 8, 512], F32))
        flat = big[:].rearrange("p b n -> p (b n)")
        g_bank, t_bank, x_bank, xt_bank = (0, 1), (2, 3), (4, 5), (6, 7)

        const_in, edge_in = sem("const_in"), sem("edge_in")
        tile_in = sem("tile_in")
        raw_used, cols_ready, sq_ready = sem("raw_used"), sem("cols_ready"), sem("sq_ready")
        lora_ready, exps_done, norm_ready, rstd_done = sem("lora_ready"), sem("exps_done"), sem("norm_ready"), sem("rstd_done")
        run_ready, decays_done, ops_ready = sem("run_ready"), sem("decays_done"), sem("ops_ready")
        g_ready, g_masked, l_ready, l_masked, x0_done = sem("g_ready"), sem("g_masked"), sem("l_ready"), sem("l_masked"), sem("x0_done")
        tr_ready, tr_copied = sem("tr_ready"), sem("tr_copied")
        ltm_ready, t1_ready, t1_copied, xx_ready, x_updated = sem("ltm_ready"), sem("t1_ready"), sem("t1_copied"), sem("xx_ready"), sem("x_updated")
        p1_ready, rhs_done, sa_ready, sa_done = sem("p1_ready"), sem("rhs_done"), sem("sa_ready"), sem("sa_done")
        delta_ready, y_ready, state_done, y_copied = sem("delta_ready"), sem("y_ready"), sem("state_done"), sem("y_copied")
        red_in, red_ready, red_done, tile_done, stored, out_free = sem("red_in"), sem("red_ready"), sem("red_done"), sem("tile_done"), sem("stored"), sem("out_free")
        edge_sq, edge_exp = sem("edge_sq"), sem("edge_exp")

        def lat(ap):
            return ap[:, 0:LAT].rearrange("p (c n) -> p c n", n=CH)

        def con(ap):
            return ap[:, LAT + 1:SHIFTED].rearrange("p (c n) -> p c n", n=CH)

        def a_of(h, d, c):
            return ar_lat[h][:, d, c, 0] if c < 4 else ar_con[h][:, d, c - 4]

        def ba_of(c):
            return mg_lat[:, c, :, 0:CH] if c < 4 else mg_con[:, c - 4, :, 0]

        def ka_of(c, j):
            return mg_lat[:, c, j, 256:384] if c < 4 else mg_con[:, c - 4, j, 1]

        ORDER = ([4, 5, 0, 1, 2, 3], [5, 4, 3, 2, 1, 0])
        LEVELS = 6
        shifted_halves = ((0, LAT), (LAT, SHIFTED))

        with nc.Block() as block:
            @block.sync
            def _(sp):
                for dst, src in ((ident, "ident"), (mask_g, "mask_g"), (mask_l, "mask_l"), (level_t, "level_t"),
                                 (blockones, "blockones"), (keep, "keep"), (edge, None)):
                    sp.dma_start(dst[:], consts[src] if src else edges).then_inc(const_in, 16)

                def streams(dst, row):
                    for a, b, t0 in ((1, LAT + 1, 0), (LAT + 2, PADDED - 1, LAT)):
                        yield dst[:, a:b], pt[row, :, t0:t0 + b - a] if not isinstance(row, bass.DynSlice) else pt[row, :, t0:t0 + b - a].rearrange("a p t -> (a p) t")

                sp.sem_inc(out_free, 1)
                sp.wait_ge(cols_ready, 1)
                for n, row in enumerate((XW_T, XA_T, XG_T)):
                    for dst, src in list(streams(raw[:, n, :], row))[:2 - n // 2]:
                        sp.dma_start(dst, src).then_inc(edge_in, 16)
                with sp.Fori(0, 8) as i:
                    sp.wait_ge(raw_used, i + 1)
                    for n, row in enumerate((R_T, K_T, V_T)):
                        for dst, src in list(streams(raw[:, n, :], bass.ds(i + row, 1)))[:1 + (n > 0)]:
                            sp.dma_start(dst, src).then_inc(tile_in, 16)
                    sp.wait_ge(tile_done, i + 1)
                    for n, w in enumerate((w2, a2, g2)):
                        sp.dma_start(lora_w[:, n, :], w[:, bass.ds(i * P, P)]).then_inc(tile_in, 16)
                    sp.dma_start(par[:], params[bass.ds(i, 1)].rearrange("a p n -> (a p) n")).then_inc(tile_in, 16)

            @block.vector
            def _(dve):
                def shift(out, u, c, m0, m1):
                    dve.tensor_scalar(out, u[:, 1:PADDED - 1], c, None, ALU.mult)
                    dve.drain()
                    dve.scalar_tensor_tensor(out, u[:, 0:PADDED - 2], m0, out, ALU.mult, ALU.add)
                    dve.drain()
                    dve.scalar_tensor_tensor(out, u[:, 2:PADDED], m1, out, ALU.mult, ALU.add)
                    dve.drain()

                dve.sem_inc(tile_done, 1)
                dve.memset(raw[:], 0.0)
                dve.memset(sig[:], 0.0)
                dve.memset(rkv[:], 0.0)
                for h in range(2):
                    dve.memset(ar_lat[h][:], 0.0)
                    dve.memset(ar_con[h][:], 0.0)
                dve.memset(tiny[:, 0:1], -1e-12)
                dve.memset(tiny[:, 2:3], 1e-12)
                dve.memset(tiny[:, 1:2], 64e-5)
                dve.drain().then_inc(cols_ready, 1)
                dve.wait_ge(const_in, 16 * 7)
                dve.wait_ge(edge_in, 16 * 5)
                e = edge
                for n in range(3):
                    dve.tensor_tensor(col[:, n:n + 1], e[:, 2 * n:2 * n + 1], e[:, 2 * n + 1:2 * n + 2], ALU.add)
                dve.drain()
                dve.tensor_scalar(col[:, 0:3], col[:, 0:3], -1.0, 1.0, ALU.mult, ALU.add)
                dve.drain()
                for n in range(3):
                    shift(small[:, n, :], raw[:, n, :], col[:, n:n + 1], e[:, 2 * n:2 * n + 1], e[:, 2 * n + 1:2 * n + 2])
                dve.drain().then_inc(edge_sq, 1)
                dve.wait_ge(edge_exp, 1)
                dve.drain().then_inc(raw_used, 1)

                with dve.Fori(0, 8) as i:
                    dve.wait_ge(tile_in, i * 144 + 144)
                    mu = par[:, 0:6].rearrange("p (n m) -> p n m", m=2)
                    dve.tensor_tensor(col[:, 0:3], mu[:, :, 0], mu[:, :, 1], ALU.add)
                    dve.tensor_scalar(col[:, 7:8], par[:, 11:12], -1.0, 1.0, ALU.mult, ALU.add)
                    dve.drain()
                    dve.tensor_scalar(col[:, 0:3], col[:, 0:3], -1.0, 1.0, ALU.mult, ALU.add)
                    dve.drain().then_inc(cols_ready, 1)
                    for n in range(3):
                        shift(rkv[:, n, :], raw[:, n, :], col[:, n:n + 1], par[:, 2 * n:2 * n + 1], par[:, 2 * n + 1:2 * n + 2])
                    dve.drain().then_inc(raw_used, 1)
                    dve.tensor_scalar(kk[:], rkv[:, 1, :], par[:, 10:11], None, ALU.mult)
                    dve.drain()
                    dve.tensor_tensor(sq[:], kk[:], kk[:], ALU.mult)
                    dve.drain().then_inc(sq_ready, 1)
                    dve.wait_ge(exps_done, i + 1)
                    dve.wait_ge(out_free, i + 1)
                    for d in range(2):
                        dve.tensor_tensor_scan(run[:, d].rearrange("p c n -> p (c n)"), keep[:].rearrange("p c n -> p (c n)"),
                                               sig[:, d].rearrange("p c n -> p (c n)"), 0.0, ALU.mult, ALU.add)
                        dve.tensor_scalar(keff[:, d, :], aa[:, d, :], par[:, 11:12], col[:, 7:8], ALU.mult, ALU.add)
                    dve.drain()
                    for d in range(2):
                        dve.tensor_tensor(sig[:, d], run[:, d], run[:, d, :, 64:65].to_broadcast([P, 6, CH + 1]), ALU.subtract)
                        dve.tensor_tensor(keff[:, d, :], keff[:, d, :], rkv[:, 1, :], ALU.mult)
                    dve.drain().then_inc(run_ready, 1)
                    dve.wait_ge(rstd_done, i + 1)
                    dve.tensor_tensor(kk[:], kk[:], rstd[:], ALU.mult)
                    dve.drain()
                    dve.wait_ge(decays_done, i + 1)
                    dve.memset(sig[:], 0.0)
                    for d in range(2):
                        r_e = (up[:, 0, :, 1:], down[:, 1, :, 0:CH])[d]
                        a_e = (up[:, 0, :, 0:CH], down[:, 1, :, 1:])[d]
                        k_e = (down[:, 0, :, 1:], up[:, 1, :, 0:CH])[d]
                        for part, c0, c1 in ((lat, 0, 4), (con, 4, 6)):
                            for h in range(2):
                                rows = slice(64 * h, 64 * h + 64)
                                dve.tensor_tensor(ar_lat[h][rows, d, :, 0, :] if part is lat else ar_con[h][rows, d], part(kk[rows, :]), a_e[rows, c0:c1], ALU.mult)
                                if part is lat:
                                    dve.tensor_tensor(ar_lat[h][rows, d, :, 1, :], part(rkv[rows, 0, :]), r_e[rows, c0:c1], ALU.mult)
                            dve.tensor_tensor(km[:, d, c0:c1, :], part(keff[:, d, :]), k_e[:, c0:c1], ALU.mult)
                            dve.tensor_tensor(bm[:, d, c0:c1, :], part(kk[:]), part(aa[:, d, :]), ALU.mult)
                    dve.drain()
                    for d in range(2):
                        k_e = (down[:, 0, :, 1:], up[:, 1, :, 0:CH])[d]
                        dve.tensor_tensor(bm[:, d], bm[:, d], k_e, ALU.mult)
                        for n in range(5):
                            c, c2 = ORDER[d][n], ORDER[d][n + 1]
                            if d == 0:
                                dve.tensor_tensor(fac[:, d, n:n + 1], up[:, 0, c, CH:], down[:, 0, c2, 0:1], ALU.mult)
                            else:
                                dve.tensor_tensor(fac[:, d, n:n + 1], down[:, 1, c, 0:1], up[:, 1, c2, CH:], ALU.mult)
                    dve.tensor_tensor(keff[:, 0, :], keff[:, 0, :], keff[:, 1, :], ALU.add)
                    dve.memset(st[:, 0], 0.0)
                    dve.drain().then_inc(ops_ready, 1)
                    for c in range(6):
                        for j in range(4):
                            n = c * 4 + j
                            dve.wait_ge(g_ready, i * 24 + (n + 1))
                            if c < 4:
                                dve.tensor_tensor(mg_lat[:, c, j, :], big[:, g_bank[n % 2], :], mask_g[:, j // 2, :], ALU.mult).then_inc(g_masked, 1)
                            else:
                                v = lambda ap: ap.rearrange("p (a b n) -> p a b n", a=2, b=2)[:, :, 0, :]
                                dve.tensor_tensor(mg_con[:, c - 4, j], v(big[:, g_bank[n % 2], :]), v(mask_g[:, j // 2, :]), ALU.mult).then_inc(g_masked, 1)
                        dve.wait_ge(l_ready, i * 6 + (c + 1))
                        if c >= 2:
                            dve.wait_ge(x0_done, i * 6 + (c - 1))
                        heads_first = lambda ap: ap.rearrange("p (d h) n -> p h d n", d=2)
                        dve.tensor_tensor(heads_first(lo[:, c % 2]), big[:, t_bank[0]:t_bank[1] + 1, 0:256].rearrange("p h (d n) -> p h d n", d=2),
                                          heads_first(mask_l[:]), ALU.mult).then_inc(l_masked, 1)
                    for pair in range(3):
                        for lv in range(1, LEVELS + 1):
                            for q in range(2):
                                c = 2 * pair + q
                                n = (pair * LEVELS + lv - 1) * 2 + q
                                dve.wait_ge(xx_ready, i * 36 + (n + 1))
                                if lv < LEVELS:
                                    dve.tensor_tensor(xs[:, c], xs[:, c], big[:, x_bank[q], :].rearrange("p (j n) -> p j n", j=4), ALU.subtract)
                                dve.tensor_tensor(xt[:, c], xt[:, c], big[:, xt_bank[q], :].rearrange("p (j n) -> p j n", j=4), ALU.subtract)
                                dve.drain().then_inc(x_updated, 1)
                    for n in range(6):
                        if n < 5:
                            for d in range(2):
                                dve.tensor_scalar(sf[:, d, :], st[:, n % 2, d, :], fac[:, d, n:n + 1], None, ALU.mult)
                            dve.drain()
                            dve.wait_ge(delta_ready, i * 5 + (n + 1))
                            for d in range(2):
                                dve.scalar_tensor_tensor(st[:, (n + 1) % 2, d, :], big[:, xt_bank[0], d * 64:d * 64 + 64], fac[:, d, n:n + 1],
                                                         sf[:, d, :], ALU.mult, ALU.add)
                            dve.drain().then_inc(state_done, 1)
                        if n >= 2:
                            dve.wait_ge(y_ready, i * 4 + (n - 1))
                            for d in range(2):
                                c = ORDER[d][n]
                                for h in range(2):
                                    rows = slice(64 * h, 64 * h + 64)
                                    dve.tensor_copy(ys[rows, d, c * CH:(c + 1) * CH], big[rows, (g_bank, t_bank)[h][d], 0:CH])
                            dve.drain().then_inc(y_copied, 1)
                    dve.tensor_tensor(ys[:, 0, :], ys[:, 0, :], ys[:, 1, :], ALU.add)
                    dve.tensor_tensor(sq[:, 0:LAT], rkv[:, 0, 0:LAT], keff[:, 0, 0:LAT], ALU.mult)
                    dve.drain()
                    dve.tensor_scalar(sq[:, 0:LAT], sq[:, 0:LAT], par[:, 12:13], None, ALU.mult)
                    dve.drain().then_inc(red_in, 1)
                    dve.wait_ge(red_ready, i * 3 + 1)
                    dve.scalar_tensor_tensor(ys[:, 0, :], big[:, 0, :], -1.0 / 64, ys[:, 0, :], ALU.mult, ALU.add)
                    dve.drain()
                    dve.tensor_tensor(ys[:, 1, :], ys[:, 0, :], ys[:, 0, :], ALU.mult)
                    dve.drain().then_inc(red_in, 1)
                    dve.wait_ge(red_ready, i * 3 + 2)
                    dve.tensor_tensor(sq[:, 0:LAT], big[:, 1, :], rkv[:, 2, 0:LAT], ALU.mult)
                    dve.wait_ge(red_done, i + 1)
                    dve.tensor_tensor(ys[:, 0, :], ys[:, 0, :], rstd[:, 0:LAT], ALU.mult)
                    dve.drain()
                    dve.tensor_scalar(ys[:, 0, :], ys[:, 0, :], par[:, 13:14], par[:, 14:15], ALU.mult, ALU.add)
                    dve.drain()
                    dve.tensor_tensor(ys[:, 0, :], ys[:, 0, :], sq[:, 0:LAT], ALU.add)
                    dve.drain()
                    dve.tensor_tensor(outp, ys[:, 0, :], gs[:], ALU.mult)
                    dve.drain().then_inc(tile_done, 1)

            @block.scalar
            def _(act):
                act.wait_ge(edge_sq, 1)
                act.activation(small[:, 0, :], small[:, 0, :], ACT.Tanh)
                act.activation(small[:, 2, :], small[:, 2, :], ACT.Sigmoid)
                act.drain().then_inc(edge_exp, 1)
                with act.Fori(0, 8) as i:
                    act.wait_ge(cols_ready, i + 2)
                    act.wait_ge(lora_ready, i + 1)
                    for d in range(2):
                        w_psum = flat[:, 2048 * d:2048 * d + SHIFTED]
                        act.activation(sig[:, d, 0:4, 1:], lat(w_psum), ACT.Sigmoid, bias=par[:, 6 + d:7 + d])
                        act.activation(sig[:, d, 4:6, 1:], con(w_psum), ACT.Sigmoid, bias=par[:, 6 + d:7 + d])
                        act.activation(aa[:, d, :], flat[:, 2048 * d + 1024:2048 * d + 1024 + SHIFTED], ACT.Sigmoid, bias=par[:, 8 + d:9 + d])
                    act.drain().then_inc(exps_done, 1)
                    act.wait_ge(norm_ready, i + 1)
                    act.copy(gs[:], big[:, 2, :])
                    act.activation(rstd[:], flat[:, 0:SHIFTED], ACT.Relu, bias=tiny[:, 0:1])
                    act.drain()
                    act.activation(rstd[:], rstd[:], ACT.Ln, bias=tiny[:, 2:3])
                    act.drain()
                    act.activation(rstd[:], rstd[:], ACT.Exp, scale=-0.5)
                    act.drain().then_inc(rstd_done, 1)
                    act.wait_ge(run_ready, i + 1)
                    act.activation(up[:], sig[:], ACT.Exp, scale=-C_DECAY)
                    act.activation(down[:], sig[:], ACT.Exp, scale=C_DECAY)
                    act.drain().then_inc(decays_done, 1)
                    for n in range(8):
                        act.wait_ge(tr_ready, i * 8 + (n + 1))
                        if n < 6:
                            act.copy(bkt[:, n].rearrange("p j n -> p (j n)"), big[:, x_bank[n % 2], :]).then_inc(tr_copied, 1)
                        elif n == 6:
                            act.copy(vt[:, 0:4].rearrange("p j n -> p (j n)"), big[:, x_bank[0], :]).then_inc(tr_copied, 1)
                        else:
                            act.copy(vt[:, 4:6].rearrange("p j n -> p (j n)"), big[:, x_bank[1], 0:256]).then_inc(tr_copied, 1)
                    for pair in range(3):
                        for lv in range(1, LEVELS + 1):
                            for q in range(2):
                                n = (pair * LEVELS + lv - 1) * 2 + q
                                act.wait_ge(t1_ready, i * 36 + (n + 1))
                                act.copy(t1[:, q].rearrange("p j n -> p (j n)"), big[:, t_bank[q], :]).then_inc(t1_copied, 1)
                    for n in range(6):
                        act.wait_ge(p1_ready, i * 6 + (n + 1))
                        act.mul(rhs[:].rearrange("p h d n -> p h (d n)"), big[:, x_bank[0]:x_bank[1] + 1, 0:128], -1.0).then_inc(rhs_done, 1)
                        act.wait_ge(sa_ready, i * 6 + (n + 1))
                        act.copy(sas[:].rearrange("p j n -> p (j n)"), big[:, xt_bank[1], 0:256]).then_inc(sa_done, 1)
                    act.wait_ge(red_ready, i * 3 + 3)
                    act.activation(rstd[:, 0:LAT], big[:, 2, :], ACT.Ln, scale=1.0 / 64, bias=tiny[:, 1:2])
                    act.drain()
                    act.activation(rstd[:, 0:LAT], rstd[:, 0:LAT], ACT.Exp, scale=-0.5)
                    act.drain().then_inc(red_done, 1)

            def pairs_of(ap):
                return ap.rearrange("p (d h) n -> p d h n", d=2)

            def level(lv):
                return level_t[:, lv].unsqueeze(2).to_broadcast([P, 2, 2, CH])

            @block.gpsimd
            def _(pool):
                with pool.Fori(0, 8) as i:
                    for c in range(6):
                        pool.wait_ge(l_masked, i * 6 + (c + 1))
                        pool.wait_ge(g_masked, i * 24 + (4 * c + 4))
                        for d in range(2):
                            pool.tensor_tensor(xs[:, c, 2 * d:2 * d + 2], lo[:, c % 2, 2 * d:2 * d + 2],
                                               level_t[:, 0, 1 - d].unsqueeze(1).to_broadcast([P, 2, CH]), ALU.mult)
                        pool.tensor_tensor(pairs_of(xt[:, c]), pairs_of(ba_of(c)), level(0), ALU.mult)
                        pool.drain()
                        pool.tensor_tensor(xs[:, c], ident[:].unsqueeze(1).to_broadcast([P, 4, CH]), xs[:, c], ALU.subtract)
                        pool.tensor_tensor(xt[:, c], ident[:].unsqueeze(1).to_broadcast([P, 4, CH]), xt[:, c], ALU.subtract)
                        pool.drain().then_inc(x0_done, 1)
                    for pair in range(3):
                        for lv in range(1, LEVELS + 1):
                            for q in range(2):
                                n = (pair * LEVELS + lv - 1) * 2 + q
                                if n >= 2:
                                    pool.wait_ge(t1_ready, i * 36 + (n - 1))
                                pool.tensor_tensor(pairs_of(ltm[:, q]), pairs_of(ba_of(2 * pair + q)), level(lv), ALU.mult).then_inc(ltm_ready, 1)
                    pool.wait_ge(tile_done, i + 2)
                    pool.dma_start(ya[bass.ds(i, 1)].rearrange("a p t -> (a p) t"), outp).then_inc(stored, 16)
                    pool.wait_ge(stored, i * 16 + 16)
                    pool.sem_inc(out_free, 1)

            @block.tensor
            def _(pe):
                pe.wait_ge(const_in, 16 * 7)
                with pe.Fori(0, 8) as i:
                    pe.wait_ge(raw_used, i + 1)
                    pe.wait_ge(tile_in, i * 144 + 144)
                    pe.wait_ge(tile_done, i + 1)
                    for d in range(2):
                        for m in range(2):
                            for a, b in shifted_halves:
                                last = pe.matmul(flat[:, 1024 * (2 * d + m) + a:1024 * (2 * d + m) + b], lora_w[64 * d:64 * d + 64, m, :],
                                                 small[64 * d:64 * d + 64, m, a:b], start=True, stop=True)
                    last.then_inc(lora_ready, 1)
                    pe.wait_ge(sq_ready, i + 1)
                    pe.wait_ge(exps_done, i + 1)
                    for a, b in shifted_halves:
                        pe.matmul(flat[:, a:b], blockones[:], sq[:, a:b], start=True, stop=True)
                    pe.matmul(big[:, 2, :], lora_w[:, 2, :], small[:, 2, 0:LAT], start=True, stop=True).then_inc(norm_ready, 1)
                    pe.wait_ge(ops_ready, i + 1)
                    for c in range(6):
                        for j in range(4):
                            n, d = c * 4 + j, j // 2
                            if n >= 2:
                                pe.wait_ge(g_masked, i * 24 + (n - 1))
                            bank = big[:, g_bank[n % 2], :]
                            w = 256 if c < 4 else 128
                            rows = ar_lat[j % 2][:, d, c].rearrange("p a n -> p (a n)") if c < 4 else a_of(j % 2, d, c)
                            pe.matmul(bank[:, 0:w], bm[:, d, c], rows, start=True, stop=True)
                            pe.matmul(bank[:, 256:256 + w], km[:, d, c], rows, start=True, stop=True).then_inc(g_ready, 1)
                        if c:
                            pe.wait_ge(l_masked, i * 6 + c)
                        for j in range(4):
                            d = j // 2
                            last = pe.matmul(big[:, t_bank[j % 2], d * CH:(d + 1) * CH], a_of(j % 2, d, c), bm[:, d, c], start=True, stop=True)
                        last.then_inc(l_ready, 1)
                    for n in range(8):
                        if n >= 2:
                            pe.wait_ge(tr_copied, i * 8 + (n - 1))
                        bank = big[:, x_bank[n % 2], :]
                        if n < 6:
                            srcs = [bm[:, 0, n], bm[:, 1, n], km[:, 0, n], km[:, 1, n]]
                        else:
                            part = lat(rkv[:, 2, :]) if n == 6 else con(rkv[:, 2, :])
                            srcs = [part[:, q] for q in range(4 if n == 6 else 2)]
                        for m, s in enumerate(srcs):
                            last = pe.transpose(bank[:, m * CH:(m + 1) * CH], s, ident[:])
                        last.then_inc(tr_ready, 1)
                    pe.wait_ge(tr_copied, i * 8 + 8)
                    pe.wait_ge(l_masked, i * 6 + 6)
                    for pair in range(3):
                        for lv in range(1, LEVELS + 1):
                            for q in range(2):
                                c = 2 * pair + q
                                n = (pair * LEVELS + lv - 1) * 2 + q
                                pe.wait_ge(ltm_ready, i * 36 + (n + 1))
                                pe.wait_ge(x0_done, i * 6 + (c + 1))
                                if n >= 2:
                                    pe.wait_ge(x_updated, i * 36 + (n - 1))
                                for j in range(4):
                                    last = pe.matmul(big[:, t_bank[q], j * CH:(j + 1) * CH], ltm[:, q, j], xs[:, c, j], start=True, stop=True)
                                last.then_inc(t1_ready, 1)
                            for q in range(2):
                                c = 2 * pair + q
                                n = (pair * LEVELS + lv - 1) * 2 + q
                                pe.wait_ge(t1_copied, i * 36 + (n + 1))
                                for j in range(4):
                                    if lv < LEVELS:
                                        pe.matmul(big[:, x_bank[q], j * CH:(j + 1) * CH], xt[:, c, j], t1[:, q, j], start=True, stop=True)
                                    last = pe.matmul(big[:, xt_bank[q], j * CH:(j + 1) * CH], t1[:, q, j], xt[:, c, j], start=True, stop=True)
                                last.then_inc(xx_ready, 1)
                    heads = [(j, j // 2, 64 * (j % 2)) for j in range(4)]
                    p1_out = lambda j: big[:, x_bank[j % 2], j // 2 * 64:j // 2 * 64 + 64]
                    delta_out = lambda j: big[64 * (j % 2):64 * (j % 2) + 64, xt_bank[0], j // 2 * 64:j // 2 * 64 + 64]
                    y_out = lambda j: big[64 * (j % 2):64 * (j % 2) + 64, (g_bank, t_bank)[j % 2][j // 2], 0:CH]

                    def p1_values(n, j, d, h):
                        c = ORDER[d][n]
                        pe.matmul(p1_out(j), ka_of(c, j), vt[:, c, h:h + 64], start=True, stop=False)

                    def delta_values(n, j, d, h):
                        c = ORDER[d][n]
                        pe.matmul(delta_out(j), bkt[:, c, 2 + d, h:h + 64], vt[:, c, h:h + 64], start=True, stop=False)

                    pe.wait_ge(x_updated, i * 36 + 36)
                    for head in heads[:2]:
                        p1_values(0, *head)
                    for n in range(6):
                        if n:
                            pe.wait_ge(state_done, i * 5 + n)
                        for j, d, h in heads:
                            if d:
                                p1_values(n, j, d, h)
                            last = pe.matmul(p1_out(j), a_of(j % 2, d, ORDER[d][n]), st[:, n % 2, d], start=False, stop=True)
                        last.then_inc(p1_ready, 1)
                        if n < 5:
                            for head in heads[:2]:
                                delta_values(n, *head)
                        if n >= 2:
                            if n > 2:
                                pe.wait_ge(y_copied, i * 4 + (n - 2))
                            for j, d, h in heads:
                                c = ORDER[d][n]
                                pe.matmul(y_out(j), vt[:, c, h:h + 64], mg_lat[:, c, j, 384:512], start=True, stop=False)
                                pe.matmul(y_out(j), st[h:h + 64, n % 2, d], ar_lat[j % 2][h:h + 64, d, c, 1], start=False, stop=False)
                        pe.wait_ge(rhs_done, i * 6 + (n + 1))
                        for j, d, h in heads:
                            last = pe.matmul(big[:, xt_bank[1], j * 64:j * 64 + 64], xt[:, ORDER[d][n], j], rhs[:, j % 2, d], start=True, stop=True)
                        last.then_inc(sa_ready, 1)
                        if n < 5:
                            for head in heads[:2]:
                                p1_values(n + 1, *head)
                        pe.wait_ge(sa_done, i * 6 + (n + 1))
                        if n < 5:
                            for j, d, h in heads:
                                if d:
                                    delta_values(n, j, d, h)
                                last = pe.matmul(delta_out(j), bkt[:, ORDER[d][n], d, h:h + 64], sas[:, j], start=False, stop=True)
                            last.then_inc(delta_ready, 1)
                        if n >= 2:
                            for j, d, h in heads:
                                last = pe.matmul(y_out(j), sas[:, j], mg_lat[:, ORDER[d][n], j, 128:256], start=False, stop=True)
                            last.then_inc(y_ready, 1)
                    pe.wait_ge(red_in, i * 2 + 1)
                    pe.matmul(big[:, 0, :], blockones[:], ys[:, 0, :], start=True, stop=True).then_inc(red_ready, 1)
                    pe.matmul(big[:, 1, :], blockones[:], sq[:, 0:LAT], start=True, stop=True).then_inc(red_ready, 1)
                    pe.wait_ge(red_in, i * 2 + 2)
                    pe.matmul(big[:, 2, :], blockones[:], ys[:, 1, :], start=True, stop=True).then_inc(red_ready, 1)



ROWS, GRID = 8, 64
CONV = 5
CV_W = LAT + 2 + CTX + 4
CV_OUT = CV_W - 4
GH = 8


def ssm(nc, pt, dt_bias, a_log, d_skip, params, consts, u_out):
    with Stage(nc) as ctx:
        def sb(n, shape):
            return ctx.enter_context(nc.sbuf_tensor(f"ss_{n}", shape, F32))

        def sem(n):
            return ctx.sem(f"ss_{n}")

        ident = sb("ident", [P, CH])
        tri = sb("tri", [P, 2, CH])
        ones = sb("ones", [P, CH])
        one = sb("one", [P, 1])
        bias = sb("bias", [64, 1])
        alog = sb("alog", [P, 64])
        skip = sb("skip", [P, 32])
        dtf = sb("dtf", [64, 3, TOK])
        kinds = sb("kinds", [P, 6, 6, 2, 32])
        mine = sb("mine", [P, 6, 6, 2, GH])
        nat = sb("nat", [P, 6, LAT])
        raw = sb("raw", [P, 6, CV_W])
        par = sb("par", [P, 6, 8])
        xbc = sb("xbc", [P, 6, CV_OUT])
        ex = sb("ex", [P, 6, CV_OUT])
        z = sb("z", [P, 4, LAT])
        ez = sb("ez", [P, 4, LAT])
        xtok = sb("xtok", [P, 6, 512])
        btok = sb("btok", [P, 6, CH])
        cbm = sb("cbm", [P, 2, 4, CH])
        xw = sb("xw", [P, 2, 512])
        xdt = sb("xdt", [P, 2, 512])
        seg = sb("seg", [P, 2, 4, CH])
        h = sb("h", [P, 2, 512])
        hf = sb("hf", [P, 512])
        tmp = sb("tmp", [P, 512])
        ys = sb("ys", [P, 4, 512])
        yf = sb("yf", [P, 4, LAT])
        big = ctx.enter_context(nc.psum_tensor("ss_big", [P, 8, 512], F32))
        row_bank, intra_bank, inter_bank, state_bank, tr_bank = (0, 1), 2, 3, 4, (5, 6)
        DT, DTA, CUM, ECUM, ETOT, WJ = range(6)
        ORDER = ([4, 5, 0, 1, 2, 3], [5, 4, 3, 2, 1, 0])
        steps = [(d, n) for d in range(2) for n in range(6)]

        names = ("const_in dt_in dt_ready dtt_ready dtt_copied dta_ready cum_ready cums_done kinds_done group_in raw_used "
                 "permuted conv_done exp_done xbc_done tr_ready tr_copied cb_ready cb_done row_ready seg_done seg_exp g_done "
                 "xw_done xdt_done inter_ready intra_ready y_done state_ready h_done z_exp group_done stored pads mine_done h_zero "
                 "ty_ready ty_copied out_free").split()
        S = {n: sem(n) for n in names}

        def lat_c(ap):
            return ap[..., 0:LAT].rearrange("p (c n) -> p c n", n=CH)

        def token_tile(ap, c):
            a = c * CH if c < 4 else LAT + 2 + (c - 4) * CH
            return ap[:, a:a + CH]

        with nc.Block() as block:
            @block.sync
            def _(sp):
                for dst, src in ((ident[:], consts["ident"]), (tri[:], consts["tri"]), (ones[:], consts["ones"]), (bias[:], dt_bias),
                                 (alog[:], a_log), (skip[:], d_skip)):
                    sp.dma_start(dst, src).then_inc(S["const_in"], 16)
                sp.dma_start(dtf[:, 0, :], pt[DT_T, 0:64, :]).then_inc(S["dt_in"], 16)
                sp.sem_inc(S["out_free"], 1)
                sp.wait_ge(S["pads"], 1)
                with sp.Fori(0, 4) as g:
                    sp.wait_ge(S["permuted"], g + 1)
                    sp.wait_ge(S["raw_used"], g + 1)
                    xs_rows = [(0, 4, bass.ds(g * 4 + XBC_T, 4)), (4, 1, bass.ds(g + (XBC_T + 16), 1)), (5, 1, bass.ds(g + (XBC_T + 20), 1))]
                    for a, n, rows in xs_rows:
                        sp.dma_start(nat[:, a:a + n, :], pt[rows, :, 0:LAT].rearrange("a p t -> p a t")).then_inc(S["group_in"], 16)
                        sp.dma_start(raw[:, a:a + n, LAT + 4:LAT + 4 + CTX], pt[rows, :, LAT:TOK].rearrange("a p t -> p a t")).then_inc(S["group_in"], 16)
                    sp.wait_ge(S["group_done"], g + 1)
                    sp.dma_start(par[:], params[bass.ds(g, 1)].rearrange("a p t n -> (a p) t n")).then_inc(S["group_in"], 16)
                    sp.dma_start(z[:], pt[bass.ds(g * 4 + Z_T, 4), :, 0:LAT].rearrange("a p t -> p a t")).then_inc(S["group_in"], 16)

            @block.vector
            def _(dve):
                for n in ("raw_used", "group_done", "h_done"):
                    dve.sem_inc(S[n], 1)
                dve.memset(raw[:], 0.0)
                dve.memset(one[:], 1.0)
                dve.drain().then_inc(S["pads"], 1)
                dve.wait_ge(S["const_in"], 96)
                dve.wait_ge(S["dt_in"], 16)
                dve.tensor_scalar(dtf[:, 1, 0:LAT].rearrange("p (c r) -> p c r", r=ROWS), dtf[:, 0, 0:LAT].rearrange("p (r c) -> p c r", c=GRID), bias[:, 0:1], None, ALU.add)
                dve.tensor_scalar(dtf[:, 1, LAT:TOK], dtf[:, 0, LAT:TOK], bias[:, 0:1], None, ALU.add)
                dve.drain().then_inc(S["dt_ready"], 1)
                dve.wait_ge(S["dt_ready"], 2)
                dve.scalar_tensor_tensor(dtf[:, 0, :], dtf[:, 1, :], 0.0, dtf[:, 2, :], ALU.max, ALU.add)
                dve.drain().then_inc(S["dtt_ready"], 1)
                dve.wait_ge(S["dtt_copied"], 1)
                for c in range(6):
                    dve.scalar_tensor_tensor(kinds[:, DTA, c].rearrange("p d h -> p (d h)"), alog[:], -1.0, kinds[:, DT, c].rearrange("p d h -> p (d h)"), ALU.mult, ALU.mult)
                dve.drain().then_inc(S["dta_ready"], 1)
                dve.wait_ge(S["cum_ready"], 1)
                for c in range(6):
                    cum_ps, tot_ps = big[:, 0, c * 64:c * 64 + 64], big[:, 1, c * 64:c * 64 + 64]
                    fl = lambda k: kinds[:, k, c].rearrange("p d h -> p (d h)")
                    dve.tensor_copy(fl(CUM), cum_ps)
                    dve.drain()
                    dve.tensor_tensor(fl(WJ), tot_ps, fl(CUM), ALU.subtract)
                dve.drain().then_inc(S["cums_done"], 1)
                dve.wait_ge(S["kinds_done"], 1)
                for c in range(6):
                    fl = lambda k: kinds[:, k, c].rearrange("p d h -> p (d h)")
                    dve.tensor_tensor(fl(WJ), fl(WJ), fl(DT), ALU.mult)
                dve.drain()
                with dve.Fori(0, 4) as g:
                    dve.wait_ge(S["permuted"], g + 2)
                    dve.tensor_copy(mine[:].rearrange("p k c d h -> p (k c d) h"),
                                    kinds[:].rearrange("p k c d h -> p (k c d) h")[:, :, bass.ds(g * GH, GH)])
                    dve.drain().then_inc(S["mine_done"], 1)
                    for pair in range(3):
                        tiles = (2 * pair, 2 * pair + 1)
                        for t in tiles:
                            dve.tensor_scalar(xbc[:, t, :], raw[:, t, 0:CV_OUT], par[:, t, 0:1], par[:, t, 5:6], ALU.mult, ALU.add)
                        for k in range(1, CONV):
                            dve.drain()
                            for t in tiles:
                                dve.scalar_tensor_tensor(xbc[:, t, :], raw[:, t, k:k + CV_OUT], par[:, t, k:k + 1], xbc[:, t, :], ALU.mult, ALU.add)
                        dve.drain().then_inc(S["conv_done"], 1)
                    dve.drain().then_inc(S["raw_used"], 1)
                    for pair in range(3):
                        dve.wait_ge(S["exp_done"], g * 3 + (pair + 1))
                        dve.tensor_tensor(xbc[:, 2 * pair:2 * pair + 2], xbc[:, 2 * pair:2 * pair + 2], ex[:, 2 * pair:2 * pair + 2], ALU.mult)
                    dve.memset(h[:, 0, :], 0.0)
                    dve.drain().then_inc(S["xbc_done"], 1)
                    dve.wait_ge(S["cb_ready"], g + 1)
                    for d in range(2):
                        dve.tensor_tensor(cbm[:, d], big[:, inter_bank, :].rearrange("p (c n) -> p c n", n=CH),
                                          tri[:, d].unsqueeze(1).to_broadcast([P, 4, CH]), ALU.mult)
                    dve.drain().then_inc(S["cb_done"], 1)
                    dve.wait_ge(S["tr_copied"], g * 8 + 8)
                    for c in range(4):
                        heads = lambda ap: ap.rearrange("p (h n) -> p h n", n=64)
                        dve.tensor_tensor(heads(ys[:, c]), heads(xtok[:, c]),
                                          skip[:, bass.ds(g * GH, GH)].unsqueeze(2).to_broadcast([P, GH, 64]), ALU.mult)
                    dve.drain()
                    m = 0
                    ns = 0
                    for d, n in steps:
                        c = ORDER[d][n]
                        if n < 5:
                            dve.tensor_tensor(heads(hf[:]), heads(h[:, n % 2]), mine[:, ETOT, c, d].unsqueeze(2).to_broadcast([P, GH, 64]), ALU.mult)
                            dve.drain()
                            dve.wait_ge(S["state_ready"], g * 10 + (ns + 1))
                            dve.tensor_tensor(h[:, (n + 1) % 2], hf[:], big[:, state_bank, :], ALU.add)
                            ns += 1
                            dve.drain().then_inc(S["h_done"], 1)
                        if n >= 2:
                            for half in range(2):
                                b = 2 * m + half
                                dve.wait_ge(S["row_ready"], g * 16 + (b + 1))
                                if b >= 2:
                                    dve.wait_ge(S["intra_ready"], g * 16 + (b - 1))
                                for e in range(4):
                                    dve.tensor_scalar(seg[:, b % 2, e], big[:, row_bank[b % 2], e * CH:(e + 1) * CH],
                                                      mine[:, CUM, c, d, 4 * half + e:4 * half + e + 1], 0.0, ALU.subtract, ALU.min)
                                dve.drain().then_inc(S["seg_done"], 1)
                            dve.wait_ge(S["inter_ready"], g * 8 + (m + 1))
                            dve.tensor_tensor(heads(tmp[:]), heads(big[:, inter_bank, :]), mine[:, ECUM, c, d].unsqueeze(2).to_broadcast([P, GH, 64]), ALU.mult)
                            dve.drain()
                            dve.tensor_tensor(ys[:, c], ys[:, c], tmp[:], ALU.add)
                            dve.drain()
                            dve.wait_ge(S["intra_ready"], g * 16 + (2 * m + 2))
                            dve.tensor_tensor(ys[:, c], ys[:, c], big[:, intra_bank, :], ALU.add)
                            dve.drain().then_inc(S["y_done"], 1)
                            m += 1
                        if d == 0 and n == 5:
                            dve.memset(h[:, 0, :], 0.0)
                            dve.drain().then_inc(S["h_done"], 1)
                    dve.wait_ge(S["z_exp"], g + 1)
                    dve.tensor_tensor(z[:], z[:], ez[:], ALU.mult)
                    dve.drain()
                    dve.wait_ge(S["ty_copied"], g * 4 + 4)
                    for t in range(4):
                        dve.tensor_tensor(ez[:, t].rearrange("p (r c) -> p r c", c=GRID), yf[:, t].rearrange("p (c r) -> p r c", r=ROWS),
                                          z[:, t].rearrange("p (r c) -> p r c", c=GRID), ALU.mult)
                    dve.drain().then_inc(S["group_done"], 1)

            @block.scalar
            def _(act):
                act.sem_inc(S["permuted"], 1)
                act.wait_ge(S["dt_ready"], 1)
                act.activation(dtf[:, 2, :], dtf[:, 1, :], ACT.Abs)
                act.drain()
                act.activation(dtf[:, 2, :], dtf[:, 2, :], ACT.Exp, scale=-1.0)
                act.drain()
                act.activation(dtf[:, 2, :], dtf[:, 2, :], ACT.Ln, bias=one[0:64, :])
                act.activation(alog[:], alog[:], ACT.Exp)
                act.drain().then_inc(S["dt_ready"], 1)
                act.wait_ge(S["dtt_ready"], 2)
                act.copy(kinds[:, DT].rearrange("p c d h -> p (c d h)"), big[:, 0, 0:384])
                act.drain().then_inc(S["dtt_copied"], 1)
                act.wait_ge(S["cum_ready"], 1)
                act.wait_ge(S["cums_done"], 1)
                act.activation(kinds[:, ETOT].rearrange("p c d h -> p (c d h)"), big[:, 1, 0:384], ACT.Exp)
                act.activation(kinds[:, ECUM], kinds[:, CUM], ACT.Exp)
                act.activation(kinds[:, WJ], kinds[:, WJ], ACT.Exp)
                act.drain().then_inc(S["kinds_done"], 1)
                with act.Fori(0, 4) as g:
                    act.wait_ge(S["group_in"], g * 128 + 128)
                    act.wait_ge(S["raw_used"], g + 1)
                    for t in range(6):
                        act.copy(raw[:, t, 2:LAT + 2].rearrange("p (c r) -> p c r", r=ROWS), nat[:, t].rearrange("p (r c) -> p c r", c=GRID))
                    act.drain().then_inc(S["permuted"], 1)
                    for pair in range(3):
                        act.wait_ge(S["conv_done"], g * 3 + (pair + 1))
                        act.activation(ex[:, 2 * pair:2 * pair + 2], xbc[:, 2 * pair:2 * pair + 2], ACT.Sigmoid).then_inc(S["exp_done"], 1)
                    act.wait_ge(S["out_free"], g + 1)
                    act.activation(ez[:], z[:], ACT.Sigmoid)
                    act.drain().then_inc(S["z_exp"], 1)
                    for n in range(8):
                        act.wait_ge(S["tr_ready"], g * 8 + (n + 1))
                        bank = big[:, tr_bank[n % 2], :]
                        if n < 6:
                            act.copy(xtok[:, n], bank).then_inc(S["tr_copied"], 1)
                        elif n == 6:
                            act.copy(btok[:, 0:4].rearrange("p c n -> p (c n)"), bank).then_inc(S["tr_copied"], 1)
                        else:
                            act.copy(btok[:, 4:6].rearrange("p c n -> p (c n)"), bank[:, 0:256]).then_inc(S["tr_copied"], 1)
                    for b in range(16):
                        act.wait_ge(S["seg_done"], g * 16 + (b + 1))
                        act.activation(seg[:, b % 2], seg[:, b % 2], ACT.Exp).then_inc(S["seg_exp"], 1)
                    for t in range(4):
                        act.wait_ge(S["ty_ready"], g * 4 + (t + 1))
                        act.copy(yf[:, t], big[:, tr_bank[t % 2], :]).then_inc(S["ty_copied"], 1)

            @block.gpsimd
            def _(pool):
                heads = lambda ap: ap.rearrange("p (h n) -> p h n", n=64)
                with pool.Fori(0, 4) as g:
                    pool.wait_ge(S["tr_copied"], g * 8 + 8)
                    pool.wait_ge(S["mine_done"], g + 1)
                    pool.wait_ge(S["cb_done"], g + 1)
                    m = ns = 0
                    for d, n in steps:
                        c = ORDER[d][n]
                        if n < 5:
                            if ns >= 2:
                                pool.wait_ge(S["state_ready"], g * 10 + (ns - 1))
                            pool.tensor_tensor(heads(xw[:, ns % 2]), heads(xtok[:, c]), mine[:, WJ, c, d].unsqueeze(2).to_broadcast([P, GH, 64]), ALU.mult).then_inc(S["xw_done"], 1)
                            ns += 1
                        if n >= 2:
                            if m >= 2:
                                pool.wait_ge(S["intra_ready"], g * 16 + 2 * (m - 1))
                            pool.tensor_tensor(heads(xdt[:, m % 2]), heads(xtok[:, c]), mine[:, DT, c, d].unsqueeze(2).to_broadcast([P, GH, 64]), ALU.mult).then_inc(S["xdt_done"], 1)
                            for half in range(2):
                                b = 2 * m + half
                                pool.wait_ge(S["seg_exp"], g * 16 + (b + 1))
                                pool.tensor_tensor(seg[:, b % 2], seg[:, b % 2], cbm[:, d, c].unsqueeze(1).to_broadcast([P, 4, CH]), ALU.mult).then_inc(S["g_done"], 1)
                            m += 1
                    pool.wait_ge(S["group_done"], g + 2)
                    pool.dma_start(u_out[bass.ds(g * 4, 4)].rearrange("a p t -> p a t"), ez[:]).then_inc(S["stored"], 16)
                    pool.wait_ge(S["stored"], g * 16 + 16)
                    pool.sem_inc(S["out_free"], 1)

            @block.tensor
            def _(pe):
                pe.wait_ge(S["const_in"], 96)
                pe.wait_ge(S["dtt_ready"], 1)
                for c in range(6):
                    last = pe.transpose(big[:, 0, c * 64:c * 64 + 64], dtf[:, 0, c * CH:(c + 1) * CH], ident[0:64, 0:64])
                last.then_inc(S["dtt_ready"], 1)
                pe.wait_ge(S["dta_ready"], 1)
                for c in range(6):
                    for d in range(2):
                        rhs = kinds[:, DTA, c, d]
                        pe.matmul(big[:, 0, c * 64 + d * 32:c * 64 + d * 32 + 32], tri[:, d], rhs, start=True, stop=True)
                        last = pe.matmul(big[:, 1, c * 64 + d * 32:c * 64 + d * 32 + 32], ones[:], rhs, start=True, stop=True)
                last.then_inc(S["cum_ready"], 1)
                pe.wait_ge(S["kinds_done"], 1)
                with pe.Fori(0, 4) as g:
                    pe.wait_ge(S["xbc_done"], g + 1)
                    pe.wait_ge(S["mine_done"], g + 1)
                    for c in range(4):
                        last = pe.matmul(big[:, inter_bank, c * CH:(c + 1) * CH], token_tile(xbc[:, 4], c), token_tile(xbc[:, 5], c), start=True, stop=True)
                    last.then_inc(S["cb_ready"], 1)
                    for n in range(8):
                        if n >= 2:
                            pe.wait_ge(S["tr_copied"], g * 8 + (n - 1))
                        bank = big[:, tr_bank[n % 2], :]
                        srcs = [token_tile(xbc[:, t], n) for t in range(4)] if n < 6 else [token_tile(xbc[:, 4], c) for c in (range(4) if n == 6 else (4, 5))]
                        for k, s in enumerate(srcs):
                            last = pe.transpose(bank[:, k * CH:(k + 1) * CH], s, ident[:])
                        last.then_inc(S["tr_ready"], 1)
                    pe.wait_ge(S["cb_done"], g + 1)
                    pe.wait_ge(S["tr_copied"], g * 8 + 8)

                    def cum_rows(b):
                        d, c = b // 8, ORDER[b // 8][2 + b // 2 % 4]
                        if b >= 2:
                            pe.wait_ge(S["seg_done"], g * 16 + (b - 1))
                        for e in range(4):
                            k = 4 * (b % 2) + e
                            last = pe.matmul(big[:, row_bank[b % 2], e * CH:(e + 1) * CH], mine[:, DTA, c, d, k:k + 1].to_broadcast([P, CH]), tri[:, d], start=True, stop=True)
                        last.then_inc(S["row_ready"], 1)

                    cum_rows(0)
                    m = ns = 0
                    for d, n in steps:
                        c = ORDER[d][n]
                        if n < 5:
                            pe.wait_ge(S["xw_done"], g * 10 + (ns + 1))
                            pe.wait_ge(S["h_done"], g * 11 + (ns + d + 1))
                            pe.matmul(big[:, state_bank, :], btok[:, c], xw[:, ns % 2], start=True, stop=True).then_inc(S["state_ready"], 1)
                            ns += 1
                        if n >= 2:
                            if m:
                                pe.wait_ge(S["y_done"], g * 8 + m)
                            pe.wait_ge(S["h_done"], g * 11 + (n + 6 * d + 1))
                            pe.matmul(big[:, inter_bank, :], token_tile(xbc[:, 5], c), h[:, n % 2], start=True, stop=True).then_inc(S["inter_ready"], 1)
                            pe.wait_ge(S["xdt_done"], g * 8 + (m + 1))
                            for half in range(2):
                                b = 2 * m + half
                                if b < 15:
                                    cum_rows(b + 1)
                                pe.wait_ge(S["g_done"], g * 16 + (b + 1))
                                for e in range(4):
                                    k = 4 * half + e
                                    last = pe.matmul(big[:, intra_bank, k * 64:k * 64 + 64], seg[:, b % 2, e], xdt[:, m % 2, k * 64:k * 64 + 64], start=True, stop=True)
                                last.then_inc(S["intra_ready"], 1)
                            m += 1
                    pe.wait_ge(S["y_done"], g * 8 + 8)
                    for t in range(4):
                        if t >= 2:
                            pe.wait_ge(S["ty_copied"], g * 4 + (t - 1))
                        for c in range(4):
                            last = pe.transpose(big[:, tr_bank[t % 2], c * CH:(c + 1) * CH], ys[:, c, t * CH:(t + 1) * CH], ident[:])
                        last.then_inc(S["ty_ready"], 1)
                    pe.wait_ge(S["ty_copied"], g * 4 + 4)



KD = D // P


def norm_step(nc, name, x_in, x_out, h_out, consts, tokens, gate_mod=None, h_mod=None, shift=None, scale=None,
              gain=None, delta=None, delta_tokens=0, gate=None, post=None):
    def streams(n):
        return [(0, 0, LAT)] + ([(1, LAT, n)] if n > LAT else [])

    rounds = ([(0, delta_tokens)] if post is not None else []) + ([(1, tokens)] if h_out is not None else [])
    with Stage(nc) as ctx:
        def sb(n, shape):
            return ctx.enter_context(nc.sbuf_tensor(f"{name}_{n}", shape, F32))

        def sem(n):
            return ctx.sem(f"{name}_{n}")

        x = sb("x", [P, KD, tokens])
        dl = sb("delta", [P, KD, delta_tokens]) if delta is not None else None
        h = sb("h", [P, KD, tokens])
        sq = sb("sq", [P, 2, tokens])
        rstd = sb("rstd", [P, tokens])
        mod = sb("mod", [P, 2, 48, 2])
        bias = sb("bias", [P, 2, 48])
        gains = sb("gains", [P, 2, KD])
        fac = sb("fac", [P, 2, 2, KD])
        eps = sb("eps", [P, 1])
        ones = sb("ones", [P, CH])
        acc = ctx.enter_context(nc.psum_tensor(f"{name}_acc", [P, 1024], F32))
        loaded, eps_set, mods_done, squares, square_used, rstd_done = (sem(n) for n in ("loaded", "eps_set", "mods_done", "squares", "square_used", "rstd_done"))
        x_ready, scaled, h_ready, stored = sem("x_ready"), sem("scaled"), sem("h_ready"), sem("stored")
        loads = [(ones[:], consts["ones"])]
        for n, m in enumerate((gate_mod, h_mod)):
            if m is not None:
                loads += [(mod[:, n].rearrange("p k s -> p (k s)"), m[0]), (bias[:, n], m[1])]
        if h_out is not None:
            loads.append((gains[:, 1, :], gain))
        if post is not None:
            loads.append((gains[:, 0, :], post))
        if delta is not None:
            loads.append((dl[:], delta[:, 0:delta_tokens].rearrange("(k p) t -> p k t", p=P)))
        for src, a, b in x_in:
            loads.append((x[:, :, a:b], src.rearrange("(k p) t -> p k t", p=P)))

        with nc.Block() as block:
            @block.sync
            def _(sp):
                for dst, src in loads:
                    sp.dma_start(dst, src).then_inc(loaded, 16)
                n = 0
                if x_out is not None:
                    sp.wait_ge(x_ready, 1)
                    sp.dma_start(x_out[:, 0:tokens].rearrange("(k p) t -> p k t", p=P), x[:]).then_inc(stored, 16)
                    n += 16
                if h_out is not None:
                    sp.wait_ge(h_ready, 1)
                    sp.dma_start(h_out[:, 0:tokens].rearrange("(k p) t -> p k t", p=P), h[:]).then_inc(stored, 16)
                    n += 16
                sp.wait_ge(stored, n)

            @block.vector
            def _(dve):
                dve.memset(eps[:], 1e-6)
                dve.drain().then_inc(eps_set, 1)
                dve.wait_ge(loaded, 16 * len(loads))
                for n, m in enumerate((gate_mod, h_mod)):
                    if m is not None:
                        dve.tensor_tensor(mod[:, n], mod[:, n], bias[:, n].unsqueeze(2).to_broadcast([P, 48, 2]), ALU.add)
                dve.drain()
                for s, a, b in streams(delta_tokens):
                    if post is not None:
                        dve.tensor_tensor(fac[:, 0, s], mod[:, 0, gate:gate + KD, s], gains[:, 0], ALU.mult)
                    elif delta is not None:
                        dve.tensor_copy(fac[:, 0, s], mod[:, 0, gate:gate + KD, s])
                if h_out is not None:
                    for s, a, b in streams(tokens):
                        dve.scalar_tensor_tensor(fac[:, 1, s], mod[:, 1, scale:scale + KD, s], 1.0, gains[:, 1], ALU.add, ALU.mult)
                dve.drain().then_inc(mods_done, 1)
                if post is not None:
                    dve.wait_ge(rstd_done, 1)
                    dve.tensor_tensor(dl[:], dl[:], rstd[:, 0:delta_tokens].unsqueeze(1).to_broadcast([P, KD, delta_tokens]), ALU.mult)
                    dve.drain()
                if delta is not None:
                    for k in range(KD):
                        for s, a, b in streams(delta_tokens):
                            dve.scalar_tensor_tensor(x[:, k, a:b], dl[:, k, a:b], fac[:, 0, s, k:k + 1], x[:, k, a:b], ALU.mult, ALU.add)
                dve.drain().then_inc(x_ready, 1)
                if h_out is not None:
                    dve.wait_ge(rstd_done, len(rounds))
                    dve.tensor_tensor(h[:], x[:], rstd[:].unsqueeze(1).to_broadcast([P, KD, tokens]), ALU.mult)
                    dve.drain().then_inc(scaled, 1)

            @block.scalar
            def _(act):
                act.wait_ge(loaded, 16 * len(loads))
                act.wait_ge(eps_set, 1)
                for r, (what, toks) in enumerate(rounds):
                    src = (dl, x)[what]
                    if what == 1:
                        act.wait_ge(x_ready, 1)
                    for k in range(KD):
                        if r * KD + k >= 2:
                            act.wait_ge(square_used, r * KD + k - 1)
                        act.activation(sq[:, k % 2, 0:toks], src[:, k], ACT.Square).then_inc(squares, 1)
                    act.wait_ge(square_used, (r + 1) * KD)
                    act.activation(rstd[:, 0:toks], acc[:, 0:toks], ACT.Ln, scale=1.0 / D, bias=eps[:])
                    act.drain()
                    act.activation(rstd[:, 0:toks], rstd[:, 0:toks], ACT.Exp, scale=-0.5)
                    act.drain().then_inc(rstd_done, 1)
                if h_out is not None:
                    act.wait_ge(scaled, 1)
                    for k in range(KD):
                        for s, a, b in streams(tokens):
                            act.activation(h[:, k, a:b], h[:, k, a:b], ACT.Identity, scale=fac[:, 1, s, k:k + 1], bias=mod[:, 1, shift + k, s:s + 1])
                    act.drain().then_inc(h_ready, 1)

            @block.tensor
            def _(pe):
                pe.wait_ge(loaded, 16 * len(loads))
                for r, (what, toks) in enumerate(rounds):
                    if r:
                        pe.wait_ge(rstd_done, r)
                    for k in range(KD):
                        pe.wait_ge(squares, r * KD + k + 1)
                        for s, a, b in streams(toks):
                            last = pe.matmul(acc[:, a:b], ones[:], sq[:, k % 2, a:b], start=(k == 0), stop=(k == KD - 1))
                        last.then_inc(square_used, 1)


def silu_columns(nc, name, c_in, c_out):
    with Stage(nc) as ctx:
        n = c_in.shape[1]
        c = ctx.enter_context(nc.sbuf_tensor(f"{name}_c", [P, n], F32))
        s = ctx.enter_context(nc.sbuf_tensor(f"{name}_s", [P, n], F32))
        moved, done = (ctx.sem(f"{name}_{k}") for k in ("moved", "done"))
        with nc.Block() as block:
            @block.sync
            def _(sp):
                sp.dma_start(c[:], c_in).then_inc(moved, 16)
                sp.wait_ge(done, 2)
                sp.dma_start(c_out, c[:]).then_inc(moved, 16)
                sp.wait_ge(moved, 32)

            @block.scalar
            def _(act):
                act.wait_ge(moved, 16)
                act.activation(s[:], c[:], ACT.Sigmoid).then_inc(done, 1)

            @block.vector
            def _(dve):
                dve.wait_ge(done, 1)
                dve.tensor_tensor(c[:], c[:], s[:], ALU.mult).then_inc(done, 1)


def branch_norm(nc, u_in, gain, consts, out):
    with Stage(nc) as ctx:
        def sb(n, shape):
            return ctx.enter_context(nc.sbuf_tensor(f"bn_{n}", shape, F32))

        KT = 16
        u, sq, rstd = sb("u", [P, KT, LAT]), sb("sq", [P, 2, LAT]), sb("rstd", [P, LAT])
        g, eps, ones = sb("g", [P, KT]), sb("eps", [P, 1]), sb("ones", [P, CH])
        acc = ctx.enter_context(nc.psum_tensor("bn_acc", [P, LAT], F32))
        loaded, squares, square_used, rstd_done, eps_set, done, stored = (ctx.sem(f"bn_{n}") for n in (
            "loaded", "squares", "square_used", "rstd_done", "eps_set", "done", "stored"))
        with nc.Block() as block:
            @block.sync
            def _(sp):
                sp.dma_start(g[:], gain).then_inc(loaded, 16)
                sp.dma_start(ones[:], consts["ones"]).then_inc(loaded, 16)
                sp.dma_start(u[:], u_in.rearrange("k p t -> p k t")).then_inc(loaded, 16)
                sp.wait_ge(done, 1)
                sp.dma_start(out.rearrange("k p t -> p k t"), u[:]).then_inc(stored, 16)
                sp.wait_ge(stored, 16)

            @block.scalar
            def _(act):
                act.wait_ge(loaded, 48)
                for k in range(KT):
                    if k >= 2:
                        act.wait_ge(square_used, k - 1)
                    act.activation(sq[:, k % 2], u[:, k], ACT.Square).then_inc(squares, 1)
                act.wait_ge(square_used, KT)
                act.wait_ge(eps_set, 1)
                act.activation(rstd[:], acc[:], ACT.Ln, scale=1.0 / (KT * P), bias=eps[:])
                act.drain()
                act.activation(rstd[:], rstd[:], ACT.Exp, scale=-0.5)
                act.drain().then_inc(rstd_done, 1)

            @block.tensor
            def _(pe):
                pe.wait_ge(loaded, 48)
                for k in range(KT):
                    pe.wait_ge(squares, k + 1)
                    pe.matmul(acc[:], ones[:], sq[:, k % 2], start=(k == 0), stop=(k == KT - 1)).then_inc(square_used, 1)

            @block.vector
            def _(dve):
                dve.memset(eps[:], 1e-6)
                dve.drain().then_inc(eps_set, 1)
                dve.wait_ge(rstd_done, 1)
                for k in range(KT):
                    dve.scalar_tensor_tensor(u[:, k], u[:, k], g[:, k:k + 1], rstd[:], ALU.mult, ALU.mult)
                dve.drain().then_inc(done, 1)


def gated_sum(nc, gates, a_in, b_in, out):
    with Stage(nc) as ctx:
        g = ctx.enter_context(nc.sbuf_tensor("gs_g", [P, 2, 2, LAT], F32))
        v = ctx.enter_context(nc.sbuf_tensor("gs_v", [P, 2, 2, LAT], F32))
        loaded = [ctx.sem(f"gs_loaded{s}") for s in range(2)]
        stored = [ctx.sem(f"gs_stored{s}") for s in range(2)]
        gated, done = (ctx.sem(f"gs_{n}") for n in ("gated", "done"))
        with nc.Block() as block:
            @block.sync
            def _(sp):
                for k in range(KD):
                    s = k % 2
                    sp.wait_ge(stored[s], 16 * (k // 2))
                    sp.dma_start(g[:, s, 0], gates[k, :, 0:LAT]).then_inc(loaded[s], 16)
                    sp.dma_start(g[:, s, 1], gates[KD + k, :, 0:LAT]).then_inc(loaded[s], 16)
                    sp.dma_start(v[:, s, 0], a_in[k * P:(k + 1) * P, :]).then_inc(loaded[s], 16)
                    sp.dma_start(v[:, s, 1], b_in[k * P:(k + 1) * P, :]).then_inc(loaded[s], 16)

            @block.scalar
            def _(act):
                for k in range(KD):
                    act.wait_ge(loaded[k % 2], 64 * (k // 2 + 1))
                    act.activation(g[:, k % 2], g[:, k % 2], ACT.Sigmoid).then_inc(gated, 1)

            @block.vector
            def _(dve):
                for k in range(KD):
                    s = k % 2
                    dve.wait_ge(gated, k + 1)
                    dve.tensor_tensor(v[:, s], v[:, s], g[:, s], ALU.mult)
                    dve.drain()
                    dve.tensor_tensor(v[:, s, 0], v[:, s, 0], v[:, s, 1], ALU.add)
                    dve.drain().then_inc(done, 1)

            @block.gpsimd
            def _(pool):
                for k in range(KD):
                    pool.wait_ge(done, k + 1)
                    pool.dma_start(out[k * P:(k + 1) * P, :], v[:, k % 2, 0]).then_inc(stored[k % 2], 16)
                for s in range(2):
                    pool.wait_ge(stored[s], 16 * KD // 2)


N_EXP, CAP = 16, 64


def route(nc, h_in, router, consts, xe_out, sel_out):
    with Stage(nc) as ctx:
        def sb(n, shape):
            return ctx.enter_context(nc.sbuf_tensor(f"ro_{n}", shape, F32))

        ht, htok = sb("ht", [P, KD, LAT]), sb("htok", [P, 4, D])
        wr, ident = sb("wr", [P, KD, N_EXP]), sb("ident", [P, CH])
        slots = sb("slots", [P, CAP])
        aff, mx, work = sb("aff", [P, 4, N_EXP]), sb("mx", [P, 4]), sb("work", [N_EXP, 3, LAT])
        top = sb("top", [N_EXP, 8, 8])
        ones = sb("ones", [N_EXP, LAT])
        slot_t, val = sb("slot_t", [P, 4, N_EXP]), sb("val", [P, 4, N_EXP])
        onehot = sb("onehot", [P, 4, N_EXP * CAP])
        weighted = sb("weighted", [P, 4, N_EXP * CAP])
        xe, sel = sb("xe", [P, KD, N_EXP * CAP]), sb("sel", [P, KD, LAT])
        big = ctx.enter_context(nc.psum_tensor("ro_big", [P, 8, 512], F32))
        S = {n: ctx.sem(f"ro_{n}") for n in (
            "loaded logits maxed exped aff_done rows_ready slots_done cols_ready hot_done weighted_done ht_ready ht_copied xe_ready xe_copied sel_ready sel_copied stored").split()}
        with nc.Block() as block:
            @block.sync
            def _(sp):
                sp.dma_start(wr[:], router.rearrange("(k p) e -> p k e", p=P)).then_inc(S["loaded"], 16)
                sp.dma_start(ident[:], consts["ident"]).then_inc(S["loaded"], 16)
                sp.dma_start(slots[:], consts["slots"]).then_inc(S["loaded"], 16)
                sp.dma_start(ht[:], h_in[:, 0:LAT].rearrange("(k p) t -> p k t", p=P)).then_inc(S["loaded"], 16)
                sp.wait_ge(S["xe_copied"], 16)
                sp.dma_start(xe_out.rearrange("k p n -> p k n"), xe[:]).then_inc(S["stored"], 16)
                sp.wait_ge(S["sel_copied"], 8)
                sp.dma_start(sel_out.rearrange("k p n -> p k n"), sel[:]).then_inc(S["stored"], 16)
                sp.wait_ge(S["stored"], 32)

            @block.tensor
            def _(pe):
                pe.wait_ge(S["loaded"], 64)
                for t in range(4):
                    for k in range(KD):
                        last = pe.matmul(big[:, 0, t * 16:t * 16 + 16], ht[:, k, t * P:(t + 1) * P], wr[:, k], start=(k == 0), stop=(k == KD - 1))
                last.then_inc(S["logits"], 1)
                for n in range(8):
                    t, half = n // 2, n % 2
                    if n >= 2:
                        pe.wait_ge(S["ht_copied"], n - 1)
                    for q in range(4):
                        last = pe.transpose(big[:, 2 + n % 2, q * P:(q + 1) * P], ht[:, 4 * half + q, t * P:(t + 1) * P], ident[:])
                    last.then_inc(S["ht_ready"], 1)
                pe.wait_ge(S["aff_done"], 1)
                for t in range(4):
                    last = pe.transpose(big[0:N_EXP, 1, t * P:(t + 1) * P], aff[:, t], ident[:])
                last.then_inc(S["rows_ready"], 1)
                pe.wait_ge(S["slots_done"], 1)
                for t in range(4):
                    last = pe.transpose(big[:, 0, t * 16:t * 16 + 16], work[:, 2, t * P:(t + 1) * P], ident[0:N_EXP, 0:N_EXP])
                last.then_inc(S["cols_ready"], 1)
                pe.wait_ge(S["ht_copied"], 8)
                pe.wait_ge(S["hot_done"], 1)
                for n in range(16):
                    k, half = n // 2, n % 2
                    if n >= 2:
                        pe.wait_ge(S["xe_copied"], n - 1)
                    for t in range(4):
                        last = pe.matmul(big[:, 4 + n % 2, :], htok[:, t, k * P:(k + 1) * P], onehot[:, t, half * 512:half * 512 + 512], start=(t == 0), stop=(t == 3))
                    last.then_inc(S["xe_ready"], 1)
                pe.wait_ge(S["weighted_done"], 1)
                for n in range(8):
                    if n >= 2:
                        pe.wait_ge(S["sel_copied"], n - 1)
                    for t in range(4):
                        last = pe.transpose(big[:, 6 + n % 2, t * P:(t + 1) * P], weighted[:, t, n * P:(n + 1) * P], ident[:])
                    last.then_inc(S["sel_ready"], 1)

            @block.vector
            def _(dve):
                dve.memset(ones[:], 1.0)
                dve.wait_ge(S["logits"], 1)
                logits = big[:, 0, 0:64].rearrange("p (t e) -> p t e", e=N_EXP)
                dve.tensor_reduce(mx[:], logits, AX, ALU.max)
                dve.drain()
                dve.tensor_tensor(aff[:], logits, mx[:].unsqueeze(2).to_broadcast([P, 4, N_EXP]), ALU.subtract)
                dve.drain().then_inc(S["maxed"], 1)
                dve.wait_ge(S["exped"], 1)
                dve.tensor_reduce(mx[:], aff[:], AX, ALU.add)
                dve.drain()
                dve.reciprocal(mx[:], mx[:])
                dve.drain()
                dve.tensor_tensor(aff[:], aff[:], mx[:].unsqueeze(2).to_broadcast([P, 4, N_EXP]), ALU.mult)
                dve.drain().then_inc(S["aff_done"], 1)
                dve.wait_ge(S["rows_ready"], 1)
                dve.tensor_copy(work[:, 0], big[0:N_EXP, 1, :])
                for r in range(8):
                    dve.drain()
                    dve.max(out=top[:, r], in_=work[:, 0])
                    dve.drain()
                    dve.match_replace(out=work[:, 0], in_to_replace=top[:, r], in_values=work[:, 0], imm_value=-1.0)
                dve.drain()
                dve.tensor_scalar(work[:, 1], work[:, 0], 0.0, None, ALU.is_lt)
                dve.drain()
                dve.tensor_tensor_scan(work[:, 2], ones[:], work[:, 1], 0.0, ALU.mult, ALU.add)
                dve.drain()
                dve.tensor_tensor(work[:, 2], work[:, 2], work[:, 1], ALU.mult)
                dve.drain().then_inc(S["slots_done"], 1)
                dve.wait_ge(S["cols_ready"], 1)
                dve.tensor_copy(slot_t[:], big[:, 0, 0:64].rearrange("p (t e) -> p t e", e=N_EXP))
                dve.drain()
                for t in range(4):
                    dve.tensor_tensor(onehot[:, t].rearrange("p (e c) -> p e c", c=CAP), slot_t[:, t].unsqueeze(2).to_broadcast([P, N_EXP, CAP]),
                                      slots[:].unsqueeze(1).to_broadcast([P, N_EXP, CAP]), ALU.is_equal)
                dve.drain().then_inc(S["hot_done"], 1)
                for t in range(4):
                    dve.tensor_tensor(weighted[:, t].rearrange("p (e c) -> p e c", c=CAP), onehot[:, t].rearrange("p (e c) -> p e c", c=CAP),
                                      aff[:, t].unsqueeze(2).to_broadcast([P, N_EXP, CAP]), ALU.mult)
                dve.drain().then_inc(S["weighted_done"], 1)
                for n in range(8):
                    dve.wait_ge(S["sel_ready"], n + 1)
                    dve.tensor_copy(sel[:, n], big[:, 6 + n % 2, :]).then_inc(S["sel_copied"], 1)

            @block.scalar
            def _(act):
                act.wait_ge(S["maxed"], 1)
                act.activation(aff[:], aff[:], ACT.Exp).then_inc(S["exped"], 1)
                for n in range(8):
                    act.wait_ge(S["ht_ready"], n + 1)
                    act.copy(htok[:, n // 2, (n % 2) * 512:(n % 2) * 512 + 512], big[:, 2 + n % 2, :]).then_inc(S["ht_copied"], 1)
                for n in range(16):
                    act.wait_ge(S["xe_ready"], n + 1)
                    act.copy(xe[:, n // 2, (n % 2) * 512:(n % 2) * 512 + 512], big[:, 4 + n % 2, :]).then_inc(S["xe_copied"], 1)


def experts(nc, xe_in, sel_in, w1, w3, w2, consts, out):
    KH = KD // 2
    with Stage(nc) as ctx:
        def sb(n, shape):
            return ctx.enter_context(nc.sbuf_tensor(f"ex_{n}", shape, F32))

        def sem(n):
            return ctx.sem(f"ex_{n}")

        xe = sb("xe", [P, KD, N_EXP * CAP])
        xe_now = [sb(f"xe_now{s}", [P, KD, CAP]) for s in range(2)]
        sel = sb("sel", [P, KD, LAT])
        ident = sb("ident", [P, P])
        w13 = [sb(f"w13_{s}", [P, 2, 2, KH, 512]) for s in range(2)]
        w2s = [sb(f"w2_{s}", [P, 2, KH, 512]) for s in range(2)]
        sg, hid = sb("sg", [P, 512]), sb("hid", [P, 512])
        hid_t = sb("hid_t", [P, KH, 2, CAP])
        ye = sb("ye", [P, KD, D])
        res = sb("res", [P, 2, LAT])
        big = ctx.enter_context(nc.psum_tensor("ex_big", [P, 8, 512], F32))
        in_, sel_in_, xe_ready = sem("in_"), sem("sel_in"), sem("xe_ready")
        w13_in = [sem(f"w13_in{s}") for s in range(2)]
        w2_in = [sem(f"w2_in{s}") for s in range(2)]
        up_ready, act_done, hid_done, turned_ready, turned_done, down_ready, ye_done = (sem(n) for n in (
            "up_ready", "act_done", "hid_done", "turned_ready", "turned_done", "down_ready", "ye_done"))
        out_ready, out_done, stored = sem("out_ready"), sem("out_done"), [sem("stored0"), sem("stored1")]
        with nc.Block() as block:
            @block.sync
            def _(sp):
                def load(slot, w, e, kh, done):
                    for half in range(2):
                        sp.dma_start(slot[:, half], w[bass.ds(e, 1), half, :, kh * KH:(kh + 1) * KH].rearrange("a p k n -> (a p) k n")).then_inc(done, 16)

                def load13(e, kh):
                    for m, w in enumerate((w1, w3)):
                        load(w13[kh][:, m], w, e, kh, w13_in[kh])

                sp.dma_start(xe[:], xe_in.rearrange("k p n -> p k n")).then_inc(in_, 16)
                sp.dma_start(ident[:], consts["ident"]).then_inc(in_, 16)
                for kh in range(2):
                    load13(0, kh)
                for kh in range(2):
                    load(w2s[kh], w2, 0, kh, w2_in[kh])
                with sp.Fori(1, N_EXP) as e:
                    for kh in range(2):
                        sp.wait_ge(up_ready, e * 2 + (kh + 3))
                        load13(e, kh)
                    for kh in range(2):
                        sp.wait_ge(down_ready, e * 2 + (kh - 1))
                        load(w2s[kh], w2, e, kh, w2_in[kh])
                sp.dma_start(sel[:], sel_in.rearrange("k p n -> p k n")).then_inc(sel_in_, 16)

            @block.tensor
            def _(pe):
                pe.sem_inc(up_ready, 4)
                pe.wait_ge(in_, 32)

                def expert(e2, par):
                    e = e2 * 2 + par
                    pe.wait_ge(xe_ready, e + 1)
                    for kh in range(2):
                        pe.wait_ge(w13_in[kh], e * 64 + 64)
                        for k in range(KH):
                            for m in range(2):
                                for half in range(2):
                                    last = pe.matmul(big[64 * half:64 * half + 64, 2 * par + m, :], xe_now[par][:, kh * KH + k],
                                                     w13[kh][:, m, half, k], start=(kh == 0 and k == 0), stop=(kh == 1 and k == KH - 1))
                        last.then_inc(up_ready, 1)
                    pe.wait_ge(hid_done, e + 1)
                    for j in range(KH):
                        last = pe.transpose(big[:, 4 + par, j * P:(j + 1) * P], hid[:, j * P:(j + 1) * P], ident[:])
                    last.then_inc(turned_ready, 1)
                    pe.wait_ge(turned_done, e + 1)
                    pe.wait_ge(ye_done, e * 2 + 2)
                    for kh in range(2):
                        pe.wait_ge(w2_in[kh], e * 32 + 32)
                        for k in range(KH):
                            for half in range(2):
                                last = pe.matmul(big[64 * half:64 * half + 64, 6 + par, :], hid_t[:, k, kh], w2s[kh][:, half, k],
                                                 start=(kh == 0 and k == 0), stop=(kh == 1 and k == KH - 1))
                        last.then_inc(down_ready, 1)
                with pe.Fori(0, N_EXP // 2) as e2:
                    expert(e2, 0)
                    expert(e2, 1)
                pe.wait_ge(ye_done, 2 * N_EXP + 4)
                pe.wait_ge(sel_in_, 16)
                for d in range(KD):
                    if d >= 2:
                        pe.wait_ge(out_done, d - 1)
                    for k in range(KD):
                        last = pe.matmul(big[:, 6 + d % 2, :], ye[:, k, d * P:(d + 1) * P], sel[:, k], start=(k == 0), stop=(k == KD - 1))
                    last.then_inc(out_ready, 1)

            @block.scalar
            def _(act):
                act.sem_inc(ye_done, 4)
                with act.Fori(0, N_EXP // 2) as e2:
                    for par in range(2):
                        act.wait_ge(up_ready, e2 * 4 + (2 * par + 6))
                        act.activation(sg[:], big[:, 2 * par, :], ACT.Sigmoid).then_inc(act_done, 1)
                        act.wait_ge(down_ready, e2 * 4 + (2 * par + 2))
                        rows = slice(64 * par, 64 * par + 64)
                        for half in range(2):
                            act.copy(ye[rows, bass.ds(e2, 1), half * 512:half * 512 + 512].rearrange("p a n -> p (a n)"),
                                     big[64 * half:64 * half + 64, 6 + par, :]).then_inc(ye_done, 1)

            @block.vector
            def _(dve):
                with dve.Fori(0, N_EXP // 2) as e2:
                    for par in range(2):
                        dve.wait_ge(act_done, e2 * 2 + (par + 1))
                        dve.tensor_tensor(sg[:], sg[:], big[:, 2 * par, :], ALU.mult)
                        dve.drain()
                        dve.tensor_tensor(hid[:], sg[:], big[:, 2 * par + 1, :], ALU.mult)
                        dve.drain().then_inc(hid_done, 1)
                        dve.wait_ge(turned_ready, e2 * 2 + (par + 1))
                        dve.tensor_copy(hid_t[:].rearrange("p k h c -> p (k h c)"), big[:, 4 + par, :]).then_inc(turned_done, 1)
                for d in range(KD):
                    if d >= 2:
                        dve.wait_ge(stored[d % 2], 16 * (d // 2))
                    dve.wait_ge(out_ready, d + 1)
                    dve.tensor_copy(res[:, d % 2], big[:, 6 + d % 2, :]).then_inc(out_done, 1)

            @block.gpsimd
            def _(pool):
                pool.wait_ge(in_, 32)
                with pool.Fori(0, N_EXP // 2) as e2:
                    for par in range(2):
                        pool.wait_ge(up_ready, e2 * 4 + (2 * par + 2))
                        pool.tensor_copy(xe_now[par][:], xe[:, :, bass.ds(e2 * (2 * CAP) + par * CAP, CAP)]).then_inc(xe_ready, 1)
                for d in range(KD):
                    pool.wait_ge(out_done, d + 1)
                    pool.dma_start(out[d * P:(d + 1) * P, :], res[:, d % 2]).then_inc(stored[d % 2], 16)
                for s in range(2):
                    pool.wait_ge(stored[s], 16 * KD // 2)



HQ, HD = 16, 64
ATT_SCALE = HD ** -0.5


def attention(nc, qkv, sinks, gains, consts, o_out):
    with Stage(nc) as ctx:
        def sb(n, shape):
            return ctx.enter_context(nc.sbuf_tensor(f"at_{n}", shape, F32))

        ident, blockones, turn = sb("ident", [P, CH]), sb("blockones", [P, CH]), sb("turn", [P, CH])
        cos, sin, mask = sb("cos", [P, LAT]), sb("sin", [P, LAT]), sb("mask", [P, 3 * CH])
        sink, sink4, gain, eps = sb("sink", [P, HQ]), sb("sink4", [P, 4]), sb("gain", [P, 2]), sb("eps", [P, 1])
        x = sb("x", [P, 3, TOK])
        v = sb("v", [HD, TOK])
        sq, rstd = sb("sq", [P, 3, TOK]), sb("rstd", [P, 3, TOK])
        vt = sb("vt", [P, 6, HD])
        s = sb("s", [P, 2, 384])
        p = sb("p", [P, 2, 640])
        pt_s = sb("pt", [P, 2, 640])
        st = sb("st", [P, 2, 8])
        o = sb("o", [P, 2, TOK])
        big = ctx.enter_context(nc.psum_tensor("at_big", [P, 8, 512], F32))
        flat = big[:].rearrange("p b n -> p (b n)")
        S = {n: ctx.sem(f"at_{n}") for n in (
            "const_in head_in squares sums_ready rstd_done normed turned roped vt_ready vt_copied sinks_done scores maxed exped den_done scaled "
            "pt_ready pt_copied pv_ready o_copied stored out_free").split()}
        units = [(h, b) for h in range(4) for b in range(6)]
        NU = len(units)

        def window(b):
            lo, hi = max(0, b - 1), min(3, b + 1)
            return (lo, hi) if b < 4 else (0, -1)

        def width(b):
            lo, hi = window(b)
            return (hi - lo + 1) * CH

        with nc.Block() as block:
            @block.sync
            def _(sp):
                for dst, src in ((ident, "ident"), (blockones, "blockones"), (turn, "turn"), (cos, "cos"), (sin, "sin"), (mask, "window")):
                    sp.dma_start(dst[:], consts[src]).then_inc(S["const_in"], 16)
                sp.dma_start(sink[:], sinks).then_inc(S["const_in"], 16)
                sp.dma_start(gain[:], gains).then_inc(S["const_in"], 16)
                sp.sem_inc(S["out_free"], 1)
                with sp.Fori(0, 4) as g:
                    sp.wait_ge(S["pv_ready"], g * NU + 1)
                    sp.dma_start(x[:, 0:2], qkv[bass.ds(g * 256, 256), :].rearrange("(a p) t -> p a t", p=P)).then_inc(S["head_in"], 16)
                    for half in range(2):
                        sp.dma_start(x[64 * half:64 * half + 64, 2], qkv[bass.ds(g * 64 + 1024, 64), :]).then_inc(S["head_in"], 16)
                    sp.dma_start(v[:], qkv[bass.ds(g * 64 + 1280, 64), :]).then_inc(S["head_in"], 16)

            @block.vector
            def _(dve):
                dve.memset(eps[:], 1e-6)
                dve.wait_ge(S["const_in"], 128)
                with dve.Fori(0, 4) as g:
                    dve.wait_ge(S["head_in"], g * 64 + 64)
                    dve.tensor_copy(sink4[:], sink[:, bass.ds(g * 4, 4)])
                    dve.tensor_tensor(sq[:], x[:], x[:], ALU.mult)
                    dve.drain().then_inc(S["squares"], 1)
                    dve.wait_ge(S["rstd_done"], g + 1)
                    for k in range(3):
                        dve.scalar_tensor_tensor(x[:, k], x[:, k], gain[:, k // 2:k // 2 + 1], rstd[:, k], ALU.mult, ALU.mult)
                    dve.drain().then_inc(S["normed"], 1)
                    dve.wait_ge(S["turned"], g + 1)
                    turned = big[:].rearrange("p (k b) n -> p k b n", b=2)[:, 0:3, 0, :]
                    tab = lambda a: a[:].unsqueeze(1).to_broadcast([P, 3, LAT])
                    dve.tensor_tensor(sq[:, :, 0:LAT], turned, tab(sin), ALU.mult)
                    dve.tensor_tensor(x[:, :, 0:LAT], x[:, :, 0:LAT], tab(cos), ALU.mult)
                    dve.drain()
                    dve.tensor_tensor(x[:, :, 0:LAT], x[:, :, 0:LAT], sq[:, :, 0:LAT], ALU.add)
                    dve.drain().then_inc(S["roped"], 1)

                    def maxima(u):
                        h, b = units[u]
                        w, lo = width(b), window(b)[0]
                        st_u = st[:, u % 2]
                        dve.wait_ge(S["scores"], g * NU + (u + 1))
                        if u >= 2:
                            dve.wait_ge(S["den_done"], g * NU + (u - 1))
                        bank = 2 * (u % 2)
                        if w:
                            off = (lo - (b - 1)) * CH
                            dve.tensor_tensor(s[:, u % 2, 0:w], big[:, bank, 0:w], mask[:, off:off + w], ALU.add)
                            dve.drain()
                            dve.tensor_reduce(st_u[:, 0:1], s[:, u % 2, 0:w], AX, ALU.max)
                        dve.tensor_reduce(st_u[:, 1:2], big[:, bank + 1, 0:256], AX, ALU.max)
                        dve.drain()
                        if w:
                            dve.tensor_tensor(st_u[:, 1:2], st_u[:, 0:1], st_u[:, 1:2], ALU.max)
                            dve.drain()
                        dve.scalar_tensor_tensor(st_u[:, 1:2], st_u[:, 1:2], ATT_SCALE, sink4[:, h:h + 1], ALU.mult, ALU.max)
                        dve.drain()
                        dve.tensor_scalar(st_u[:, 2:3], st_u[:, 1:2], -1.0, None, ALU.mult)
                        dve.drain().then_inc(S["maxed"], 1)

                    def denominators(u):
                        st_u = st[:, u % 2]
                        dve.wait_ge(S["exped"], g * NU + (u + 1))
                        lo_col = 3 if width(units[u][1]) else 4
                        dve.tensor_reduce(st_u[:, 6:7], st_u[:, lo_col:6], AX, ALU.add)
                        dve.drain()
                        dve.reciprocal(st_u[:, 7:8], st_u[:, 6:7])
                        dve.drain().then_inc(S["den_done"], 1)

                    def transposed(u):
                        w = width(units[u][1]) + 256
                        dve.wait_ge(S["pt_ready"], g * NU + (u + 1))
                        dve.tensor_copy(pt_s[:, u % 2, 0:w], flat[:, 2048:2048 + w]).then_inc(S["pt_copied"], 1)

                    maxima(0)
                    for u in range(NU):
                        if u + 1 < NU:
                            maxima(u + 1)
                        denominators(u)
                        if u:
                            transposed(u - 1)
                    transposed(NU - 1)

            @block.scalar
            def _(act):
                act.sem_inc(S["o_copied"], 1)
                act.wait_ge(S["const_in"], 128)
                with act.Fori(0, 4) as g:
                    act.wait_ge(S["sums_ready"], g + 1)
                    act.activation(rstd[:], flat[:, 0:3072].rearrange("p (k n) -> p k n", k=3)[:, :, 0:TOK], ACT.Ln, scale=1.0 / HD, bias=eps[:])
                    act.drain()
                    act.activation(rstd[:], rstd[:], ACT.Exp, scale=-0.5)
                    act.drain().then_inc(S["rstd_done"], 1)
                    act.wait_ge(S["vt_ready"], g + 1)
                    act.copy(vt[:].rearrange("p c n -> p (c n)"), big[:, 6, 0:384]).then_inc(S["vt_copied"], 1)

                    def outputs(u):
                        h, b = units[u]
                        rows = slice(64 * (h % 2), 64 * (h % 2) + 64)
                        act.wait_ge(S["pv_ready"], g * NU + (u + 2))
                        if u == 0:
                            act.wait_ge(S["out_free"], g + 1)
                        act.copy(o[rows, h // 2, b * CH:(b + 1) * CH], big[rows, 6 + u % 2, 0:CH]).then_inc(S["o_copied"], 1)

                    for u in range(NU):
                        h, b = units[u]
                        w = width(b)
                        st_u, bank = st[:, u % 2], 2 * (u % 2)
                        act.wait_ge(S["maxed"], g * NU + (u + 1))
                        if u >= 2:
                            act.wait_ge(S["pt_ready"], g * NU + (u - 1))
                        if w:
                            act.activation(p[:, u % 2, 0:w], s[:, u % 2, 0:w], ACT.Exp, scale=ATT_SCALE, bias=st_u[:, 2:3], accum_out=st_u[:, 3:4])
                        act.activation(p[:, u % 2, w:w + 256], big[:, bank + 1, 0:256], ACT.Exp, scale=ATT_SCALE, bias=st_u[:, 2:3], accum_out=st_u[:, 4:5])
                        act.activation(st_u[:, 5:6], sink4[:, h:h + 1], ACT.Exp, bias=st_u[:, 2:3])
                        act.drain().then_inc(S["exped"], 1)
                        if u >= 2:
                            outputs(u - 2)
                    outputs(NU - 2)
                    outputs(NU - 1)

            @block.gpsimd
            def _(pool):
                with pool.Fori(0, 4) as g:
                    for u in range(NU):
                        w = width(units[u][1]) + 256
                        pool.wait_ge(S["den_done"], g * NU + (u + 1))
                        pool.tensor_tensor(p[:, u % 2, 0:w], p[:, u % 2, 0:w], st[:, u % 2, 7:8].to_broadcast([P, w]), ALU.mult).then_inc(S["scaled"], 1)
                    pool.wait_ge(S["o_copied"], g * NU + (NU + 1))
                    pool.dma_start(o_out[bass.ds(g * 256, 256), :].rearrange("(a p) t -> p a t", p=P), o[:]).then_inc(S["stored"], 16)
                    pool.wait_ge(S["stored"], g * 16 + 16)
                    pool.sem_inc(S["out_free"], 1)

            @block.tensor
            def _(pe):
                pe.sem_inc(S["pv_ready"], 1)
                pe.wait_ge(S["const_in"], 128)
                with pe.Fori(0, 4) as g:
                    pe.wait_ge(S["squares"], g + 1)
                    pe.wait_ge(S["o_copied"], g * NU + 1)
                    for k in range(3):
                        for a, b in ((0, LAT), (LAT, TOK)):
                            last = pe.matmul(flat[:, 1024 * k + a:1024 * k + b], blockones[:], sq[:, k, a:b], start=True, stop=True)
                    last.then_inc(S["sums_ready"], 1)
                    for c in range(6):
                        last = pe.transpose(big[:, 6, c * HD:(c + 1) * HD], v[:, c * CH:(c + 1) * CH], ident[0:HD, 0:HD])
                    last.then_inc(S["vt_ready"], 1)
                    pe.wait_ge(S["normed"], g + 1)
                    for k in range(3):
                        last = pe.matmul(big[:, 2 * k, :], turn[:], x[:, k, 0:LAT], start=True, stop=True)
                    last.then_inc(S["turned"], 1)
                    pe.wait_ge(S["roped"], g + 1)
                    pe.wait_ge(S["vt_copied"], g + 1)

                    def scores(u):
                        h, b = units[u]
                        half = slice(64 * (h % 2), 64 * (h % 2) + 64)
                        bank = 2 * (u % 2)
                        if u >= 2:
                            pe.wait_ge(S["exped"], g * NU + (u - 1))
                        q = x[half, h // 2, b * CH:(b + 1) * CH]
                        w, lo = width(b), window(b)[0]
                        if w:
                            pe.matmul(big[:, bank, 0:w], q, x[half, 2, lo * CH:lo * CH + w], start=True, stop=True)
                        pe.matmul(big[:, bank + 1, 0:256], q, x[half, 2, LAT:TOK], start=True, stop=True).then_inc(S["scores"], 1)

                    def transposes(u):
                        pe.wait_ge(S["scaled"], g * NU + (u + 1))
                        if u:
                            pe.wait_ge(S["pt_copied"], g * NU + u)
                        for k in range(width(units[u][1]) // CH + 2):
                            last = pe.transpose(flat[:, 2048 + k * CH:2048 + (k + 1) * CH], p[:, u % 2, k * CH:(k + 1) * CH], ident[:])
                        last.then_inc(S["pt_ready"], 1)

                    def values(u):
                        h, b = units[u]
                        lo, hi = window(b)
                        tiles = list(range(lo, hi + 1)) + [4, 5]
                        pe.wait_ge(S["pt_copied"], g * NU + (u + 1))
                        if u >= 2:
                            pe.wait_ge(S["o_copied"], g * NU + u)
                        out = big[64 * (h % 2):64 * (h % 2) + 64, 6 + u % 2, 0:CH]
                        for k, t in enumerate(tiles):
                            last = pe.matmul(out, vt[:, t], pt_s[:, u % 2, k * CH:(k + 1) * CH], start=(k == 0), stop=(k == len(tiles) - 1))
                        last.then_inc(S["pv_ready"], 1)

                    scores(0)
                    scores(1)
                    for u in range(NU):
                        if u + 2 < NU:
                            scores(u + 2)
                        transposes(u)
                        if u:
                            values(u - 1)
                    values(NU - 1)


def dense_glu(nc, name, w, conv, x_t, out_t, tokens, groups):
    k_tiles = KD
    span = 512 if tokens % 512 == 0 else tokens // 2
    spans = tokens // span
    padded = tokens + 2 + (tokens > LAT)
    out_w = padded - 2
    with Stage(nc) as ctx:
        def sb(n, shape):
            return ctx.enter_context(nc.sbuf_tensor(f"{name}_{n}", shape, F32))

        def sem(n):
            return ctx.sem(f"{name}_{n}")

        ops = SplitOperands(ctx, name, w, x_t[:, 0:tokens].rearrange("(k p) t -> p k t", p=P), k_tiles, tokens, groups, 512)
        cpar, cp = sb("cpar", [P, groups * 2, 4]), sb("cp", [P, 2, 4])
        gate, conved, sg = sb("gate", [P, 2, padded]), sb("conved", [P, 2, out_w]), sb("sg", [P, 2, out_w])
        stage = [sb(f"stage{s}", [P, 2, tokens]) for s in range(2)]
        acc = [ctx.enter_context(nc.psum_tensor(f"{name}_acc{b}", [P, spans, BANK], F32)) for b in range(2)]
        acc_v = [ctx.enter_context(nc.psum_tensor(f"{name}_accv{b}", [P, spans, BANK], F32)) for b in range(2)]
        conv_loaded, pads = sem("conv_loaded"), sem("pads")
        gate_ready, value_ready, gate_done, conv_done, sig_done, value_done = (sem(n) for n in (
            "gate_ready", "value_ready", "gate_done", "conv_done", "sig_done", "value_done"))
        stored = [sem(f"stored{s}") for s in range(2)]
        stage_free = [sem(f"stage_free{s}") for s in range(2)]
        out_v = out_t.rearrange("(g c p) t -> g p c t", p=P, c=2)
        pieces = [(0, LAT, 0)] + ([(LAT, TOK, 1)] if tokens > LAT else [])

        with nc.Block() as block:
            @block.sync
            def _(sp):
                ops.load(sp)
                sp.dma_start(cpar[:], conv).then_inc(conv_loaded, 16)
                ops.reload(sp)

            @block.tensor
            def _(pe):
                pe.sem_inc(value_ready, 2)
                pe.wait_ge(ops.x_ready, ops.CHUNKS)

                def products(g, s, i, more):
                    pe.wait_ge(ops.w_ready, g + 1)
                    for c in range(2):
                        for bank, col, freed, ready in ((acc[c], 2 * c, gate_done, gate_ready), (acc_v[c], 2 * c + 1, value_done, value_ready)):
                            pe.wait_ge(freed, g * 2 + (c + 1))
                            ops.products(pe, bank, s, col, span, spans).then_inc(ready, 1)
                each_group(pe, groups, products)

            def copy_spans(act, c):
                for h in range(spans):
                    for a, b, o in pieces:
                        lo, hi = max(a, h * span), min(b, (h + 1) * span)
                        if lo < hi:
                            act.copy(gate[:, c, 1 + o + lo:1 + o + hi], acc[c][:, h, lo - h * span:hi - h * span])

            @block.scalar
            def _(act):
                act.wait_ge(pads, 1)
                act.sem_inc(gate_done, 2)
                ops.w_hi_part(act, 0, 0)
                ops.x_hi_parts(act)

                def gates(g, s, i, more):
                    if more:
                        act.wait_ge(value_ready, g * 2 + 2)
                        ops.w_hi_part(act, 1 - s, i + s)
                    for c in range(2):
                        act.wait_ge(gate_ready, g * 2 + (c + 1))
                        act.wait_ge(conv_done, g * 2 + (c + 1))
                        copy_spans(act, c)
                        act.drain().then_inc(gate_done, 1)
                        act.wait_ge(conv_done, g * 2 + (c + 3))
                        act.activation(sg[:, c], conved[:, c], ACT.Sigmoid).then_inc(sig_done, 1)
                each_group(act, groups, gates)

            @block.vector
            def _(dve):
                dve.memset(gate[:], 0.0)
                dve.drain().then_inc(pads, 1)
                dve.sem_inc(conv_done, 2)
                dve.sem_inc(value_done, 2)
                ops.w_lo_part(dve, 0, 0)
                ops.x_lo_parts(dve)
                dve.wait_ge(conv_loaded, 16)

                def values(g, s, i, more):
                    if more:
                        ops.w_lo_part(dve, g + 1, 1 - s)
                    dve.tensor_copy(cp[:], cpar[:, bass.ds(g * 2, 2), :])
                    dve.drain()
                    for c in range(2):
                        dve.wait_ge(gate_done, g * 2 + (c + 3))
                        dve.tensor_scalar(conved[:, c], gate[:, c, 0:out_w], cp[:, c, 0:1], cp[:, c, 3:4], ALU.mult, ALU.add)
                        dve.drain()
                        dve.scalar_tensor_tensor(conved[:, c], gate[:, c, 1:1 + out_w], cp[:, c, 1:2], conved[:, c], ALU.mult, ALU.add)
                        dve.drain()
                        dve.scalar_tensor_tensor(conved[:, c], gate[:, c, 2:2 + out_w], cp[:, c, 2:3], conved[:, c], ALU.mult, ALU.add)
                        dve.drain().then_inc(conv_done, 1)
                        dve.wait_ge(sig_done, g * 2 + (c + 1))
                        dve.tensor_tensor(conved[:, c], conved[:, c], sg[:, c], ALU.mult)
                        dve.drain()
                        dve.wait_ge(value_ready, g * 2 + (c + 3))
                        if c == 0:
                            dve.wait_ge(stage_free[s], i + 1)
                        for h in range(spans):
                            for a, b, o in pieces:
                                lo, hi = max(a, h * span), min(b, (h + 1) * span)
                                if lo < hi:
                                    dve.tensor_tensor(stage[s][:, c, lo:hi], conved[:, c, lo + o:hi + o], acc_v[c][:, h, lo - h * span:hi - h * span], ALU.mult)
                        dve.drain().then_inc(value_done, 1)
                each_group(dve, groups, values)

            @block.gpsimd
            def _(pool):
                def store(g, s, i, more):
                    pool.wait_ge(value_done, g * 2 + 4)
                    pool.dma_start(out_v[bass.ds(g, 1), :, :, 0:tokens].rearrange("a p c t -> (a p) c t"), stage[s][:]).then_inc(stored[s], 16)
                    pool.wait_ge(stored[s], i * 16 + 16)
                    pool.sem_inc(stage_free[s], 1)
                for s in range(2):
                    pool.sem_inc(stage_free[s], 1)
                each_group(pool, groups, store)



HG = 8
F_T, I_T, Q_T, G_T = 0, 16, 24, 32
HALVES = (64, 32, 16, 8, 4, 2, 1)


def hgrn(nc, hp, lb_logits, gain, consts, out):
    with Stage(nc) as ctx:
        def sb(n, shape):
            return ctx.enter_context(nc.sbuf_tensor(f"hg_{n}", shape, F32))

        ident, ones, keep = sb("ident", [P, CH]), sb("ones", [P, CH]), sb("keep", [P, 6, CH + 1])
        masks = sb("masks", [P, 2, 8, CH])
        logits, lb, gains, eps, colh = sb("logits", [P, 2, HG]), sb("lb", [P, 2, HG]), sb("gains", [P, 1]), sb("eps", [P, 1]), sb("colh", [P, 2])
        q, f, v, gate = sb("q", [P, LAT]), sb("f", [P, 2, TOK]), sb("v", [P, TOK]), sb("gate", [P, LAT])
        f_raw, q_raw, gate_raw = sb("f_raw", [P, 2, TOK]), sb("q_raw", [P, LAT]), sb("gate_raw", [P, LAT])
        sq, sgate = sb("sq", [P, LAT]), sb("sgate", [P, LAT])
        k = sb("k", [P, 2, TOK])
        g = sb("g", [P, 2, 6, CH + 1])
        run = sb("run", [P, 2, 6, CH + 1])
        rest = sb("rest", [P, 2, 6, CH + 1])
        ea, eb = sb("ea", [P, 2, 6, CH + 1]), sb("eb", [P, 2, 6, CH + 1])
        kd, qd = sb("kd", [P, 2, 6, CH]), sb("qd", [P, 2, 4, CH])
        lev = sb("lev", [P, 2, 7, LAT])
        vt, kt = sb("vt", [P, 6, CH]), sb("kt", [P, 2, 6, CH])
        state = sb("state", [P, 2, 6, CH])
        prod = sb("prod", [P, 16, CH])
        a = sb("a", [P, 4, CH])
        o, rstd = sb("o", [P, LAT]), sb("rstd", [P, LAT])
        big = ctx.enter_context(nc.psum_tensor("hg_big", [P, 8, 512], F32))
        S = {n: ctx.sem(f"hg_{n}") for n in (
            "const_in pads lb_done head_in sig_done f_done logs_done run_ready decays_done lev_right lev_left lev_exp lev_q lev_k kd_done "
            "tr_ready tr_copied pair_ready pair_done a_done st_ready st_done o_ready o_copied sum_ready rstd_done head_done stored v_in out_free").split()}
        ORDER = ([4, 5, 0, 1, 2, 3], [5, 4, 3, 2, 1, 0])

        def halves(ap, h, side):
            return ap.rearrange("p (b s n) -> p b s n", s=2, n=h)[:, :, side, :]

        with nc.Block() as block:
            @block.sync
            def _(sp):
                for dst, src in ((ident, consts["ident"]), (ones, consts["ones"]), (keep, consts["keep"]), (masks, consts["pairs"]), (logits, lb_logits), (gains, gain)):
                    sp.dma_start(dst[:], src).then_inc(S["const_in"], 16)
                tile = lambda row, n: hp[bass.ds(row, 1), :, 0:n].rearrange("a p t -> (a p) t")
                sp.sem_inc(S["out_free"], 1)
                with sp.Fori(0, HG) as i:
                    sp.wait_ge(S["f_done"], i + 1)
                    for d in range(2):
                        sp.dma_start(f_raw[:, d], tile(i + (F_T + 8 * d), TOK)).then_inc(S["head_in"], 16)
                    sp.dma_start(q_raw[:], tile(i + Q_T, LAT)).then_inc(S["head_in"], 16)
                    sp.dma_start(gate_raw[:], tile(i + G_T, LAT)).then_inc(S["head_in"], 16)
                    sp.wait_ge(S["head_done"], i + 1)
                    sp.dma_start(v[:], tile(i + I_T, TOK)).then_inc(S["v_in"], 16)

            @block.scalar
            def _(act):
                act.wait_ge(S["pads"], 1)
                act.activation(lb[:, 0], lb[:, 1], ACT.Sigmoid)
                act.drain().then_inc(S["lb_done"], 1)
                with act.Fori(0, HG) as i:
                    act.wait_ge(S["head_in"], i * 64 + 64)
                    act.activation(f[:], f_raw[:], ACT.Sigmoid)
                    act.activation(sq[:], q_raw[:], ACT.Sigmoid)
                    act.activation(sgate[:], gate_raw[:], ACT.Sigmoid)
                    act.drain().then_inc(S["sig_done"], 1)
                    act.wait_ge(S["f_done"], i + 2)
                    for d in range(2):
                        act.activation(g[:, d, 0:4, 1:], f[:, d, 0:LAT].rearrange("p (c n) -> p c n", n=CH), ACT.Ln)
                        act.activation(g[:, d, 4:6, 1:], f[:, d, LAT:TOK].rearrange("p (c n) -> p c n", n=CH), ACT.Ln)
                    act.drain().then_inc(S["logs_done"], 1)
                    act.wait_ge(S["run_ready"], i + 1)
                    act.activation(ea[:], run[:], ACT.Exp)
                    act.activation(eb[:], rest[:], ACT.Exp)
                    act.drain().then_inc(S["decays_done"], 1)
                    for n in range(14):
                        act.wait_ge(S["lev_right"], i * 14 + (n + 1))
                        act.wait_ge(S["lev_left"], i * 14 + (n + 1))
                        act.activation(lev[:, n // 7, n % 7], lev[:, n // 7, n % 7], ACT.Exp)
                        act.drain().then_inc(S["lev_exp"], 1)
                    for n in range(5):
                        act.wait_ge(S["tr_ready"], i * 5 + (n + 1))
                        bank = big[:, n % 2, :]
                        if n < 4:
                            dst = kt[:, n // 2, 3 * (n % 2):3 * (n % 2) + 3]
                            act.copy(dst.rearrange("p c n -> p (c n)"), bank[:, 0:384]).then_inc(S["tr_copied"], 1)
                        else:
                            act.copy(vt[:].rearrange("p (b c) n -> p b (c n)", b=2), big[:, 4:6, 0:384]).then_inc(S["tr_copied"], 1)
                    act.wait_ge(S["o_ready"], i + 1)
                    act.wait_ge(S["out_free"], i + 1)
                    act.copy(o[:], big[:, 6, :])
                    act.drain()
                    act.activation(rstd[:], o[:], ACT.Square)
                    act.drain().then_inc(S["o_copied"], 1)
                    act.wait_ge(S["sum_ready"], i + 1)
                    act.activation(rstd[:], big[:, 7, :], ACT.Ln, scale=1.0 / P, bias=eps[:])
                    act.drain()
                    act.activation(rstd[:], rstd[:], ACT.Exp, scale=-0.5)
                    act.drain().then_inc(S["rstd_done"], 1)

            @block.vector
            def _(dve):
                dve.sem_inc(S["head_done"], 1)
                dve.sem_inc(S["f_done"], 1)
                dve.memset(g[:], 0.0)
                dve.memset(eps[:], 1e-6)
                dve.memset(state[:], 0.0)
                dve.wait_ge(S["const_in"], 96)
                dve.tensor_tensor(lb[:, 1], logits[:, 1], logits[:, 0], ALU.subtract)
                dve.drain().then_inc(S["pads"], 1)
                dve.wait_ge(S["lb_done"], 1)
                dve.tensor_scalar(lb[:, 1], lb[:, 0], -1.0, 1.0, ALU.mult, ALU.add)
                dve.drain()
                with dve.Fori(0, HG) as i:
                    dve.tensor_copy(colh[:].unsqueeze(2), lb[:, :, bass.ds(i, 1)])
                    dve.drain()
                    dve.wait_ge(S["sig_done"], i + 1)
                    dve.tensor_scalar(f[:], f[:], colh[:, 1:2], colh[:, 0:1], ALU.mult, ALU.add)
                    dve.tensor_tensor(q[:], q_raw[:], sq[:], ALU.mult)
                    dve.tensor_tensor(gate[:], gate_raw[:], sgate[:], ALU.mult)
                    dve.drain().then_inc(S["f_done"], 1)
                    dve.tensor_scalar(k[:], f[:], -1.0, 1.0, ALU.mult, ALU.add)
                    dve.wait_ge(S["logs_done"], i + 1)
                    for d in range(2):
                        dve.tensor_tensor_scan(run[:, d].rearrange("p c n -> p (c n)"), keep[:].rearrange("p c n -> p (c n)"),
                                               g[:, d].rearrange("p c n -> p (c n)"), 0.0, ALU.mult, ALU.add)
                    dve.drain()
                    for d in range(2):
                        dve.tensor_tensor(rest[:, d], run[:, d, :, CH:].to_broadcast([P, 6, CH + 1]), run[:, d], ALU.subtract)
                    dve.drain().then_inc(S["run_ready"], 1)
                    for n in range(14):
                        d, h = n // 7, HALVES[n % 7]
                        for c in range(4):
                            mid = run[:, d, c, h:h + CH - h:2 * h].unsqueeze(2).to_broadcast([P, CH // (2 * h), h])
                            b = run[:, d, c, 1 - d:1 - d + CH]
                            right = halves(lev[:, d, n % 7, c * CH:(c + 1) * CH], h, 1)
                            dve.tensor_tensor(right, halves(b, h, 1), mid, ALU.subtract)
                        dve.drain().then_inc(S["lev_right"], 1)
                    dve.wait_ge(S["decays_done"], i + 1)
                    for d in range(2):
                        k_e = (eb[:, 0, :, 1:], ea[:, 1, :, 0:CH])[d]
                        q_e = (ea[:, 0, 0:4, 1:], eb[:, 1, 0:4, 0:CH])[d]
                        dve.tensor_tensor(kd[:, d], k[:, d].rearrange("p (c n) -> p c n", n=CH), k_e, ALU.mult)
                        dve.tensor_tensor(qd[:, d], q[:].rearrange("p (c n) -> p c n", n=CH), q_e, ALU.mult)
                    dve.drain().then_inc(S["kd_done"], 1)
                    for n in range(14):
                        d, h = n // 7, HALVES[n % 7]
                        src = q[:] if d == 0 else k[:, 1, 0:LAT]
                        right = halves(lev[:, d, n % 7], h, 1)
                        dve.wait_ge(S["lev_exp"], i * 14 + (n + 1))
                        dve.tensor_tensor(right, right, halves(src, h, 1), ALU.mult)
                        dve.drain().then_inc(S["lev_q"], 1)
                    for n in range(5):
                        dve.wait_ge(S["st_ready"], i * 5 + (n + 1))
                        for d in range(2):
                            c = ORDER[d][n]
                            dve.scalar_tensor_tensor(state[:, d, n + 1], state[:, d, n], ea[:, d, c, CH:], big[:, 2 + n % 2, d * CH:(d + 1) * CH], ALU.mult, ALU.add)
                        dve.drain().then_inc(S["st_done"], 1)
                    for c in range(4):
                        dve.wait_ge(S["pair_ready"], i * 4 + (c + 1))
                        dve.tensor_tensor(prod[:], big[:, 0:4, :].rearrange("p b (l n) -> p (b l) n", n=CH), masks[:].rearrange("p d l n -> p (d l) n"), ALU.mult)
                        dve.drain().then_inc(S["pair_done"], 1)
                        dve.tensor_reduce(a[:, c], prod[:].rearrange("p l n -> p n l"), AX, ALU.add)
                        dve.drain().then_inc(S["a_done"], 1)
                    dve.wait_ge(S["rstd_done"], i + 1)
                    dve.scalar_tensor_tensor(o[:], o[:], gains[:, 0:1], rstd[:], ALU.mult, ALU.mult)
                    dve.drain()
                    dve.tensor_tensor(o[:], o[:], gate[:], ALU.mult)
                    dve.drain().then_inc(S["head_done"], 1)

            @block.gpsimd
            def _(pool):
                with pool.Fori(0, HG) as i:
                    pool.wait_ge(S["run_ready"], i + 1)
                    for n in range(14):
                        d, h = n // 7, HALVES[n % 7]
                        for c in range(4):
                            mid = run[:, d, c, h:h + CH - h:2 * h].unsqueeze(2).to_broadcast([P, CH // (2 * h), h])
                            b = run[:, d, c, 1 - d:1 - d + CH]
                            left = halves(lev[:, d, n % 7, c * CH:(c + 1) * CH], h, 0)
                            pool.tensor_tensor(left, mid, halves(b, h, 0), ALU.subtract)
                        pool.drain().then_inc(S["lev_left"], 1)
                    for n in range(14):
                        d, h = n // 7, HALVES[n % 7]
                        src = k[:, 0, 0:LAT] if d == 0 else q[:]
                        left = halves(lev[:, d, n % 7], h, 0)
                        pool.wait_ge(S["lev_exp"], i * 14 + (n + 1))
                        pool.tensor_tensor(left, left, halves(src, h, 0), ALU.mult)
                        pool.drain().then_inc(S["lev_k"], 1)
                    pool.wait_ge(S["head_done"], i + 2)
                    pool.dma_start(out[bass.ds(i, 1)].rearrange("a p t -> (a p) t"), o[:]).then_inc(S["stored"], 16)
                    pool.wait_ge(S["stored"], i * 16 + 16)
                    pool.sem_inc(S["out_free"], 1)

            @block.tensor
            def _(pe):
                pe.wait_ge(S["const_in"], 96)
                with pe.Fori(0, HG) as i:
                    pe.wait_ge(S["head_done"], i + 1)
                    pe.wait_ge(S["v_in"], i * 16 + 16)
                    pe.wait_ge(S["kd_done"], i + 1)
                    for n in range(5):
                        if n >= 2:
                            pe.wait_ge(S["tr_copied"], i * 5 + (n - 1))
                        for c in range(3):
                            if n < 4:
                                last = pe.transpose(big[:, n % 2, c * CH:(c + 1) * CH], kd[:, n // 2, 3 * (n % 2) + c], ident[:])
                            else:
                                for b in range(2):
                                    last = pe.transpose(big[:, 4 + b, c * CH:(c + 1) * CH], v[:, (3 * b + c) * CH:(3 * b + c + 1) * CH], ident[:])
                        last.then_inc(S["tr_ready"], 1)
                    pe.wait_ge(S["tr_copied"], i * 5 + 5)
                    for n in range(5):
                        if n >= 2:
                            pe.wait_ge(S["st_done"], i * 5 + (n - 1))
                        for d in range(2):
                            c = ORDER[d][n]
                            last = pe.matmul(big[:, 2 + n % 2, d * CH:(d + 1) * CH], kt[:, d, c], vt[:, c], start=True, stop=True)
                        last.then_inc(S["st_ready"], 1)
                    pe.wait_ge(S["st_done"], i * 5 + 5)
                    pe.wait_ge(S["lev_q"], i * 14 + 14)
                    pe.wait_ge(S["lev_k"], i * 14 + 14)

                    def outputs(c):
                        pe.wait_ge(S["a_done"], i * 4 + (c + 1))
                        dst = big[:, 6, c * CH:(c + 1) * CH]
                        for d in range(2):
                            pe.matmul(dst, state[:, d, ORDER[d].index(c)], qd[:, d, c], start=(d == 0), stop=False)
                        last = pe.matmul(dst, vt[:, c], a[:, c], start=False, stop=True)
                        if c == 3:
                            last.then_inc(S["o_ready"], 1)

                    for c in range(4):
                        if c:
                            pe.wait_ge(S["pair_done"], i * 4 + c)
                        for d in range(2):
                            for l in range(8):
                                bank = big[:, 2 * d + l // 4, (l % 4) * CH:(l % 4 + 1) * CH]
                                if l < 7:
                                    x = lev[:, d, l, c * CH:(c + 1) * CH]
                                    last = pe.matmul(bank, x, x, start=True, stop=True)
                                else:
                                    last = pe.matmul(bank, k[:, d, c * CH:(c + 1) * CH], q[:, c * CH:(c + 1) * CH], start=True, stop=True)
                        last.then_inc(S["pair_ready"], 1)
                        if c:
                            outputs(c - 1)
                    outputs(3)
                    pe.wait_ge(S["o_copied"], i + 1)
                    pe.matmul(big[:, 7, :], ones[:], rstd[:], start=True, stop=True).then_inc(S["sum_ready"], 1)



def modulation(nc, name, w, cond, consts, out, groups):
    QUARTERS, COLS = 4, 4
    SLOTS = 2
    with Stage(nc) as ctx:
        sb = lambda n, shape: ctx.enter_context(nc.sbuf_tensor(f"{name}_{n}", shape, F32))
        sem = lambda n: ctx.sem(f"{name}_{n}")
        w_slot = [sb(f"w{s}", [P, KD, BANK]) for s in range(SLOTS)]
        x, ident, fold = sb("x", [P, KD, 2]), sb("ident", [P, P]), sb("fold", [P, 2])
        x_wide = sb("x_wide", [P, KD, 32])
        sums = [sb(f"sums{s}", [P, BANK]) for s in range(2)]
        res = sb("res", [P, groups, COLS * 2])
        acc = [ctx.enter_context(nc.psum_tensor(f"{name}_acc{s}", [P, BANK], F32)) for s in range(2)]
        turned = [ctx.enter_context(nc.psum_tensor(f"{name}_turned{s}", [P, BANK], F32)) for s in range(2)]
        w_loaded = [sem(f"w_loaded{s}") for s in range(SLOTS)]
        x_loaded, x_ready, acc_ready, sums_ready, turned_ready, res_done, stored = (sem(n) for n in (
            "x_loaded", "x_ready", "acc_ready", "sums_ready", "turned_ready", "res_done", "stored"))

        def each(eng, step, first=0):
            with eng.Fori(first, groups // 2) as i:
                step(i * 2, 0, i)
                step(i * 2 + 1, 1, i)

        with nc.Block() as block:
            @block.sync
            def _(sp):
                def load(g, s):
                    sp.dma_start(w_slot[s][:], w[bass.ds(g, 1)].rearrange("a p k n -> (a p) k n")).then_inc(w_loaded[s], 16)

                def reload(g, s, i):
                    sp.wait_ge(acc_ready, g - 1)
                    load(g, s)

                sp.dma_start(x[:], cond.rearrange("p (k s) -> p k s", s=2)).then_inc(x_loaded, 16)
                sp.dma_start(ident[:], consts["ident"]).then_inc(x_loaded, 16)
                load(0, 0)
                load(1, 1)
                each(sp, reload, 1)
                sp.wait_ge(res_done, groups + 2)
                sp.dma_start(out, res[:].rearrange("p g n -> p (g n)")).then_inc(stored, 16)
                sp.wait_ge(stored, 16)

            @block.tensor
            def _(pe):
                pe.wait_ge(x_ready, 1)

                def products(g, s, i):
                    pe.wait_ge(w_loaded[s], i * 16 + 16)
                    pe.wait_ge(sums_ready, g + 1)
                    for n in range(KD // QUARTERS):
                        for q in range(QUARTERS):
                            last = pe.matmul(acc[s][32 * q:32 * q + 32, :], x_wide[:, 2 * q + n], w_slot[s][:, 2 * q + n],
                                             start=(n == 0), stop=(n == KD // QUARTERS - 1))
                    last.then_inc(acc_ready, 1)
                    pe.wait_ge(sums_ready, g + 3)
                    pe.wait_ge(res_done, g + 1)
                    for c in range(COLS):
                        last = pe.matmul(turned[s][:, 2 * c:2 * c + 2], sums[s][:, c * P:(c + 1) * P], fold[:], start=True, stop=True)
                    last.then_inc(turned_ready, 1)
                each(pe, products)

            @block.scalar
            def _(act):
                act.sem_inc(sums_ready, 2)
                act.sem_inc(turned_ready, 2)

                def copy_sums(g, s, i):
                    act.wait_ge(acc_ready, g + 1)
                    act.wait_ge(turned_ready, g + 1)
                    act.copy(sums[s][:], acc[s][:]).then_inc(sums_ready, 1)
                each(act, copy_sums)

            @block.vector
            def _(dve):
                dve.sem_inc(res_done, 2)
                dve.memset(x_wide[:], 0.0)
                dve.drain()
                dve.wait_ge(x_loaded, 32)
                dve.tensor_copy(x_wide[:, :, 0:2], x[:])
                dve.tensor_tensor(fold[:], ident[:, 0:2], ident[:, 32:34], ALU.add)
                for q in range(2, QUARTERS):
                    dve.drain()
                    dve.tensor_tensor(fold[:], fold[:], ident[:, 32 * q:32 * q + 2], ALU.add)
                dve.drain().then_inc(x_ready, 1)

                def results(g, s, i):
                    dve.wait_ge(turned_ready, g + 3)
                    dve.tensor_copy(res[:, bass.ds(g, 1), :].rearrange("p a n -> p (a n)"), turned[s][:, 0:COLS * 2]).then_inc(res_done, 1)
                each(dve, results)



def shape_constants():
    f=np.float32
    eye=np.eye(P,dtype=f)
    a,b=np.indices((P,P))
    strict=(a<b).astype(f); incl=(a<=b).astype(f)
    fwd=np.concatenate([strict,incl,strict,incl],1)
    bwd=np.concatenate([strict.T,incl.T,strict.T,incl.T],1)
    def level(k):
        blk,half=2<<k,1<<k
        return ((a//blk==b//blk)&(a%blk<half)&(b%blk>=half)).astype(f)
    lt=np.stack([np.stack([level(k),level(k).T],1) for k in range(7)],1)
    keep=np.ones((P,6,CH+1),f); keep[:,:,0]=0
    c={}
    c["ident"]=eye
    c["mask_g"]=np.stack([fwd,bwd],1)
    c["mask_l"]=np.stack([strict.T]*2+[strict]*2,1)
    c["level_t"]=lt
    c["blockones"]=(a//64==b//64).astype(f)
    c["keep"]=keep
    c["tri"]=np.stack([incl,incl.T],1)
    c["ones"]=np.ones((P,P),f)
    turn=np.zeros((P,P),f)
    for i in range(P):
        if i%32<16: turn[i+16,i]=-1
        else: turn[i-16,i]=1
    c["turn"]=turn
    dy=[level(k) for k in range(6,-1,-1)]
    c["pairs"]=np.stack([np.stack(dy+[eye],1),np.stack([m.T for m in dy]+[eye],1)],1)
    inv=(np.float32(10000.0)**(-np.arange(16,dtype=f)/np.float32(16))).astype(f)
    t=np.arange(512)
    pos=np.where((np.arange(P)[:,None]%64)<32,(t//64)[None],(t%64)[None]).astype(f)
    ang=pos*inv[np.arange(P)%16][:,None]
    c["cos"],c["sin"]=np.cos(ang),np.sin(ang)
    q,k=np.indices((P,3*CH)); k=k-CH
    c["window"]=np.where(np.abs(q-k)<=CH,0.0,-1e30)
    c["slots"]=np.broadcast_to(np.arange(1,65,dtype=f),(P,64))
    return {k:np.ascontiguousarray(v,f) for k,v in c.items()}



SHIFT1, SCALE1, GATE1, SHIFT2, SCALE2, GATE2 = (KD * n for n in range(6))
FF = 2816


def program(nc, a, out):
    def scratch(name, shape):
        return nc.dram_tensor(name, shape, F32).ap()

    def rows(t, tokens):
        return t[:, 0:tokens].rearrange("(k p) t -> p k t", p=P)

    def tiles(t, tokens, cols=4):
        return t[:, 0:tokens].rearrange("(g c p) t -> g p c t", p=P, c=cols)

    cond = scratch("cond", [P, 32])
    mod1, mod2 = scratch("mod1", [P, 96]), scratch("mod2", [P, 192])
    h = scratch("h", [D, TOK])
    pt = scratch("pt", [84, P, TOK])
    ya, yb_raw, yb = scratch("ya", [KD, P, LAT]), scratch("yb_raw", [16, P, LAT]), scratch("yb", [16, P, LAT])
    pa, pb, merged, ml = (scratch(n, [D, LAT]) for n in ("pa", "pb", "merged", "ml"))
    x1, moe = scratch("x1", [D, LAT]), scratch("moe", [D, LAT])
    xe, sel = scratch("xe", [KD, P, N_EXP * CAP]), scratch("sel", [KD, P, LAT])
    x2, x3, x4, x5 = (scratch(n, [D, TOK]) for n in ("x2", "x3", "x4", "x5"))
    qkv, att, y = scratch("qkv", [1536, TOK]), scratch("att", [D, TOK]), scratch("y", [D, TOK])
    hp, hg = scratch("hp", [40, P, TOK]), scratch("hg", [KD, P, LAT])
    ff = scratch("ff", [FF, TOK])

    silu_columns(nc, "sc", a["cond"], cond)
    modulation(nc, "ada1", a["ada_w"], cond[:, 0:16], a, mod1, 12)
    modulation(nc, "ada2", a["ada_w_2"], cond[:, 16:32], a, mod2, 24)
    m1 = (mod1, a["ada_b"])
    m2 = [(mod2[:, 96 * n:96 * n + 96], a["ada_b_2"][:, 48 * n:48 * n + 48]) for n in range(2)]

    norm_step(nc, "n1", [(a["x"], 0, LAT), (a["ctx"], LAT, TOK)], None, h, a, TOK, h_mod=m1, shift=SHIFT1, scale=SCALE1, gain=a["norm1_pre"])
    pt_v = pt.rearrange("(g c) p t -> g p c t", c=4)
    dense_split(nc, "in_both", a["w_in_both"], rows(h, TOK), pt_v[0:11], KD, TOK, 11, 512)
    dense_split(nc, "in_lat", a["w_in_lat"], rows(h, LAT), pt_v[11:21, :, :, 0:LAT], KD, LAT, 10, 512)
    rwkv(nc, pt, (a["rw_w2"], a["rw_a2"], a["rw_g2"]), a["rw_params"], a["rw_edges"], a, ya)
    ssm(nc, pt, a["dt_bias"], a["a_log"], a["d_skip"], a["ssm_params"], a, yb_raw)
    branch_norm(nc, yb_raw, a["ssm_norm"], a, yb)
    dense_split(nc, "proj_a", a["proj_a"], ya.rearrange("k p t -> p k t"), tiles(pa, LAT), KD, LAT, 2, 512)
    dense(nc, "proj_b", a["proj_b"], yb.rearrange("k p t -> p k t"), tiles(pb, LAT), 16, LAT, 2, 512)
    gated_sum(nc, pt[GATE_T:GATE_T + 16], pa, pb, merged)
    dense_split(nc, "w_out", a["w_out"], rows(merged, LAT), tiles(ml, LAT), KD, LAT, 2, 512)
    norm_step(nc, "n2", [(a["x"], 0, LAT)], x1, h, a, LAT, gate_mod=m1, h_mod=m1, shift=SHIFT2, scale=SCALE2, gain=a["norm2_pre"],
              delta=ml, delta_tokens=LAT, gate=GATE1, post=a["norm1_post"])
    route(nc, h, a["router"], a, xe, sel)
    experts(nc, xe, sel, a["exp_w1"], a["exp_w3"], a["exp_w2"], a, moe)
    norm_step(nc, "n3", [(x1, 0, LAT), (a["ctx_2"], LAT, TOK)], x2, h, a, TOK, gate_mod=m1, h_mod=m2[0], shift=SHIFT1, scale=SCALE1,
              gain=a["norm1_g_2"][:, 0:KD], delta=moe, delta_tokens=LAT, gate=GATE2, post=a["norm2_post"])

    dense_split(nc, "att_in", a["attn_w_in"], rows(h, TOK), tiles(qkv, TOK), KD, TOK, 3, 512)
    attention(nc, qkv, a["attn_sink"], a["attn_gains"], a, att)
    dense_split(nc, "att_out", a["attn_w_out"], rows(att, TOK), tiles(y, TOK), KD, TOK, 2, 512)
    norm_step(nc, "n4", [(x2, 0, TOK)], x3, h, a, TOK, gate_mod=m2[0], h_mod=m2[0], shift=SHIFT2, scale=SCALE2,
              gain=a["norm2_g_2"][:, 0:KD], delta=y, delta_tokens=TOK, gate=GATE1)
    dense_glu(nc, "up0", a["ffn_w_up_0"], a["ffn_conv_0"], h, ff, TOK, 11)
    dense(nc, "down0", a["ffn_w_down_0"], rows(ff, TOK), tiles(y, TOK, 2), 22, TOK, 4, 256)
    norm_step(nc, "n5", [(x3, 0, TOK)], x4, h, a, TOK, gate_mod=m2[0], h_mod=m2[1], shift=SHIFT1, scale=SCALE1,
              gain=a["norm1_g_2"][:, KD:2 * KD], delta=y, delta_tokens=TOK, gate=GATE2)
    hp_v = hp.rearrange("(g c) p t -> g p c t", c=4)
    dense_split(nc, "hg_both", a["hgrn_w_both"], rows(h, TOK), hp_v[0:6], KD, TOK, 6, 512)
    dense_split(nc, "hg_lat", a["hgrn_w_lat"], rows(h, LAT), hp_v[6:10, :, :, 0:LAT], KD, LAT, 4, 512)
    hgrn(nc, hp, a["lb_logits"], a["hgrn_gain"], a, hg)
    dense_split(nc, "hg_out", a["hgrn_w_out"], hg.rearrange("k p t -> p k t"), tiles(y, LAT), KD, LAT, 2, 512)
    norm_step(nc, "n6", [(x4[:, 0:LAT], 0, LAT)], x5, h, a, LAT, gate_mod=m2[1], h_mod=m2[1], shift=SHIFT2, scale=SCALE2,
              gain=a["norm2_g_2"][:, KD:2 * KD], delta=y, delta_tokens=LAT, gate=GATE1)
    dense_glu(nc, "up1", a["ffn_w_up_1"], a["ffn_conv_1"], h, ff, LAT, 11)
    dense(nc, "down1", a["ffn_w_down_1"], rows(ff, LAT), tiles(y, LAT, 2), 22, LAT, 4, 256)
    norm_step(nc, "n7", [(x5[:, 0:LAT], 0, LAT)], out, None, a, LAT, gate_mod=m2[1], delta=y, delta_tokens=LAT, gate=GATE2)



def layouts(i):
    def cols(v):
        return v.reshape(-1, P).T

    def tiled(w, width=512):
        k, n = w.shape
        return w.reshape(k // P, P, n // width, width).transpose(2, 1, 0, 3)

    def expert_tiled(w):
        e, k, n = w.shape
        return w.reshape(e, k // P, P, n // 512, 512).transpose(0, 3, 2, 1, 4)

    def both(u, v):
        return np.stack([cols(u.reshape(-1)), cols(v.reshape(-1))], axis=2).reshape(P, 2 * KD)

    def spread(v):
        return np.broadcast_to(v.reshape(1, -1), (P, v.size))

    a = dict(shape_constants())
    a["x"], a["ctx"], a["ctx_2"] = i["x"][0].T, i["ctx"][0].T, i["ctx_2"][0].T
    a["cond"] = np.concatenate([both(i["c"], i["c_ctx"]), both(i["c_2"], i["c_ctx_2"])], axis=1)
    a["ada_w"], a["ada_b"] = tiled(i["ada_w"][0]), cols(i["ada_b"][0])
    a["ada_w_2"] = np.concatenate([tiled(i["ada_w_2"][0]), tiled(i["ada_w_2"][1])], axis=0)
    a["ada_b_2"] = cols(i["ada_b_2"])
    for n in ("norm1_pre", "norm1_post", "norm2_pre", "norm2_post", "ssm_norm"):
        a[n] = cols(i[n][0])
    a["norm1_g_2"], a["norm2_g_2"] = cols(i["norm1_g_2"]), cols(i["norm2_g_2"])

    w = i["w_in"][0]
    rw = 3 * D
    s0 = rw + 3 * P
    part = lambda first, n: w[:, first:first + n]
    pad = np.zeros((D, 64), w.dtype)
    a["w_in_both"] = tiled(np.concatenate([part(D, 2 * D), part(rw, 2 * P), part(s0 + 2 * D, 3 * D), part(s0 + 5 * D, 64), pad, part(0, P)], axis=1))
    a["w_in_lat"] = tiled(np.concatenate([part(P, D - P), part(rw + 2 * P, P), part(s0, 2 * D), part(s0 + 5 * D + 64, 2 * D)], axis=1))

    mu = i["rw_mu"][0]
    per_tile = [mu[0, 0:D], mu[1, 0:D], mu[0, D:2 * D], mu[1, D:2 * D], mu[0, 2 * D:rw], mu[1, 2 * D:rw],
                i["rw_w0"][0, 0], i["rw_w0"][0, 1], i["rw_a0"][0, 0], i["rw_a0"][0, 1],
                i["rw_kk"][0], i["rw_ka"][0], i["rw_rk"][0].reshape(-1), i["rw_ln_w"][0], i["rw_ln_b"][0], i["rw_ln_b"][0]]
    a["rw_params"] = np.stack(per_tile, axis=1).reshape(KD, P, 16)
    edges = mu[:, rw:rw + 3 * P].reshape(2, 3, P).transpose(2, 1, 0).reshape(P, 6)
    a["rw_edges"] = np.concatenate([edges, edges[:, 0:2]], axis=1)
    a["rw_w2"], a["rw_a2"], a["rw_g2"] = i["rw_w2"][0].reshape(P, D), i["rw_a2"][0].reshape(P, D), i["rw_g2"][0]

    a["dt_bias"] = i["ssm_dt_bias"][0].reshape(64, 1)
    a["a_log"], a["d_skip"] = spread(i["ssm_a_log"][0]), spread(i["ssm_d"][0])
    taps = np.concatenate([i["ssm_conv_w"][0], i["ssm_conv_b"][0][:, None], i["ssm_conv_w"][0][:, 0:2]], axis=1).reshape(24, P, 8)
    a["ssm_params"] = np.stack([np.concatenate([taps[4 * g:4 * g + 4], taps[16 + g:17 + g], taps[20 + g:21 + g]], axis=0).transpose(1, 0, 2) for g in range(4)])
    a["proj_a"], a["proj_b"], a["w_out"] = tiled(i["proj_a"][0]), tiled(i["proj_b"][0]), tiled(i["w_out"][0])
    a["router"] = i["router"][0]
    for n in ("exp_w1", "exp_w3", "exp_w2"):
        a[n] = expert_tiled(i[n][0])

    a["attn_w_in"], a["attn_w_out"] = tiled(i["attn_w_in_2"][0]), tiled(i["attn_w_out_2"][0])
    a["attn_sink"] = spread(i["attn_sink_2"][0])
    a["attn_gains"] = np.stack([np.concatenate([i[n][0]] * 2) for n in ("attn_q_gain_2", "attn_k_gain_2")], axis=1)
    w = i["hgrn_w_in_2"][0]
    a["hgrn_w_both"] = tiled(w[:, D:4 * D])
    a["hgrn_w_lat"] = tiled(np.concatenate([w[:, 0:D], w[:, 4 * D:5 * D]], axis=1))
    a["hgrn_w_out"] = tiled(i["hgrn_w_out_2"][0])
    a["hgrn_gain"] = i["hgrn_o_gain_2"][0].reshape(P, 1)
    a["lb_logits"] = i["hgrn_lb_logits_2"].reshape(2, HG, P).transpose(2, 0, 1)
    for n in range(2):
        up = i["ffn_w_up_2"][n].reshape(D, 2, FF // 256, 2, P)
        a[f"ffn_w_up_{n}"] = up.transpose(2, 0, 3, 1, 4).reshape(FF // 256, KD, P, 512).transpose(0, 2, 1, 3)
        a[f"ffn_conv_{n}"] = np.concatenate([i["ffn_conv_w_2"][n], i["ffn_conv_b_2"][n][None]], axis=0).reshape(4, FF // P, P).transpose(2, 1, 0)
        a[f"ffn_w_down_{n}"] = tiled(i["ffn_w_down_2"][n], 256)
    return {k: np.ascontiguousarray(v) for k, v in a.items()}


def kernel(**inputs):
    import concourse.bacc as bacc
    from concourse.bass_utils import run_bass_kernel_spmd

    arrays = layouts({k: np.asarray(v) for k, v in inputs.items()})
    nc = bacc.Bacc("TRN2", target_bir_lowering=False, num_devices=1)
    aps = {n: nc.dram_tensor(f"in_{n}", v.shape, mybir.dt.from_np(v.dtype), kind="ExternalInput").ap() for n, v in arrays.items()}
    out = nc.dram_tensor("out_x", (D, LAT), F32, kind="ExternalOutput").ap()
    program(nc, aps, out)
    r = run_bass_kernel_spmd(nc, [{f"in_{n}": v for n, v in arrays.items()}], core_ids=[0])
    return r.results[0]["out_x"].T.reshape(1, LAT, D)
```
